# Optimizing a Trainium2 kernel written in Bass

```python
import math
import jax
import jax.numpy as jnp
from jax import lax
import numpy as np

D_MODEL = 1024
BATCH = 1
SEQ = 512
DEPTH = 2

N_EVEN = (DEPTH + 1) // 2
N_ODD = DEPTH // 2
HEAD_DIM = 64
A_HEADS = 4
A_MAPS = 2 * A_HEADS
A_V_DIM = 2 * HEAD_DIM
B_Q_HEADS = 8
B_KV_HEADS = 2
B_GROUP = B_Q_HEADS // B_KV_HEADS
A_Q_W = A_MAPS * HEAD_DIM
A_V_W = A_HEADS * A_V_DIM
B_Q_W = B_Q_HEADS * HEAD_DIM
B_KV_W = B_KV_HEADS * HEAD_DIM
IN_SPLITS = (A_Q_W, 2 * A_Q_W, 2 * A_Q_W + A_V_W, 2 * A_Q_W + A_V_W + B_Q_W, 2 * A_Q_W + A_V_W + B_Q_W + B_KV_W)
IN_W = 2 * A_Q_W + A_V_W + B_Q_W + 2 * B_KV_W
MIX_W = A_V_W + B_Q_W
Q_BLOCK = 128
GRID_W = 64
ROPE_AXIS_DIM = HEAD_DIM // 2
ROPE_THETA = 10000.0
REL_BUCKETS = 32
REL_MAX_DIST = 128
RWKV_HEAD = 64
RWKV_HEADS = D_MODEL // RWKV_HEAD
DECAY_LORA = 64
ICLR_LORA = 64
GATE_LORA = 128
GN_EPS = 64e-5
PEER_HEADS = 8
N_KEYS = 128
N_EXPERTS = N_KEYS * N_KEYS
PEER_TOPK = 16
D_KEY = 256
D_KEY_HALF = D_KEY // 2
TOKEN_BLOCK = 128
NORM_EPS = 1e-6

kernel_name = 'hybrid_diffattn_gqa_rwkv7_peer_encoder'

def rms_norm(x, g):
    xf = x.astype(jnp.float32)
    y = xf * lax.rsqrt(jnp.mean(xf * xf, axis=-1, keepdims=True) + NORM_EPS)
    return (y * g.astype(jnp.float32)).astype(x.dtype)

def t5_bucket(rel):
    nb = REL_BUCKETS // 2
    max_exact = nb // 2
    ret = jnp.where(rel > 0, nb, 0)
    n = jnp.abs(rel)
    nf = jnp.maximum(n, 1).astype(jnp.float32)
    large = max_exact + (jnp.log(nf / max_exact) / math.log(REL_MAX_DIST / max_exact) * (nb - max_exact)).astype(jnp.int32)
    large = jnp.minimum(large, nb - 1)
    return ret + jnp.where(n < max_exact, n, large)

def axial_angles(seq_len):
    rows = seq_len // GRID_W
    row = jnp.repeat(jnp.arange(rows), GRID_W).astype(jnp.float32)
    col = jnp.tile(jnp.arange(GRID_W), rows).astype(jnp.float32)
    inv = ROPE_THETA ** (-jnp.arange(0, ROPE_AXIS_DIM, 2, dtype=jnp.float32) / ROPE_AXIS_DIM)
    return row[:, None] * inv, col[:, None] * inv

def rot_half(x, ang):
    x1, x2 = jnp.split(x, 2, axis=-1)
    cos = jnp.cos(ang)[:, None, :]
    sin = jnp.sin(ang)[:, None, :]
    return jnp.concatenate([x1 * cos - x2 * sin, x2 * cos + x1 * sin], axis=-1)

def axial_rope(x, ang_row, ang_col):
    xf = x.astype(jnp.float32)
    out = jnp.concatenate([rot_half(xf[..., :ROPE_AXIS_DIM], ang_row), rot_half(xf[..., ROPE_AXIS_DIM:], ang_col)], axis=-1)
    return out.astype(x.dtype)

def hybrid_attention(h, w_in, qk_g, lam_vec, subln_g, w_out, rel_bias, lambda_init):
    B_, S_, _ = h.shape
    nb = S_ // Q_BLOCK
    scale = HEAD_DIM ** -0.5
    qa, ka, va, qb, kb, vb = jnp.split(h @ w_in, IN_SPLITS, axis=-1)
    qa = rms_norm(qa.reshape(B_, S_, A_MAPS, HEAD_DIM), qk_g[0])
    ka = rms_norm(ka.reshape(B_, S_, A_MAPS, HEAD_DIM), qk_g[1])
    va = va.reshape(B_, S_, A_HEADS, A_V_DIM)
    qb = rms_norm(qb.reshape(B_, S_, B_Q_HEADS, HEAD_DIM), qk_g[2])
    kb = rms_norm(kb.reshape(B_, S_, B_KV_HEADS, HEAD_DIM), qk_g[3])
    vb = vb.reshape(B_, S_, B_KV_HEADS, HEAD_DIM)
    ang_r, ang_c = axial_angles(S_)
    qb = axial_rope(qb, ang_r, ang_c)
    kb = axial_rope(kb, ang_r, ang_c)
    ka_t = ka.transpose(0, 2, 1, 3)
    va_t = va.transpose(0, 2, 1, 3)
    kb_t = kb.transpose(0, 2, 1, 3)
    vb_t = vb.transpose(0, 2, 1, 3)
    qa_blk = qa.reshape(B_, nb, Q_BLOCK, A_MAPS, HEAD_DIM).transpose(1, 0, 3, 2, 4)
    qb_blk = qb.reshape(B_, nb, Q_BLOCK, B_KV_HEADS, B_GROUP, HEAD_DIM).transpose(1, 0, 3, 4, 2, 5)
    lv = lam_vec.astype(jnp.float32)
    lam = jnp.exp(jnp.sum(lv[0] * lv[1])) - jnp.exp(jnp.sum(lv[2] * lv[3])) + lambda_init
    key_pos = jnp.arange(S_)

    def block(args):
        qa_i, qb_i, start = args
        qpos = start + jnp.arange(Q_BLOCK)
        bias = rel_bias[t5_bucket(key_pos[None, :] - qpos[:, None])]
        bias = bias.transpose(2, 0, 1).astype(jnp.float32)
        sa = jnp.einsum('bmqd,bmkd->bmqk', qa_i, ka_t).astype(jnp.float32) * scale + bias
        pa = jax.nn.softmax(sa, axis=-1).reshape(B_, A_HEADS, 2, Q_BLOCK, S_)
        diff = (pa[:, :, 0] - lam * pa[:, :, 1]).astype(va_t.dtype)
        oa = jnp.einsum('bhqk,bhkd->bhqd', diff, va_t)
        sb = jnp.einsum('bgrqd,bgkd->bgrqk', qb_i, kb_t).astype(jnp.float32) * scale
        pb = jax.nn.softmax(sb, axis=-1).astype(vb_t.dtype)
        ob = jnp.einsum('bgrqk,bgkd->bgrqd', pb, vb_t)
        return oa, ob

    oa, ob = lax.map(block, (qa_blk, qb_blk, jnp.arange(nb) * Q_BLOCK))
    oa = oa.transpose(1, 0, 3, 2, 4).reshape(B_, S_, A_HEADS, A_V_DIM)
    oa = (rms_norm(oa, subln_g) * (1.0 - lambda_init)).reshape(B_, S_, A_V_W)
    ob = ob.transpose(1, 0, 4, 2, 3, 5).reshape(B_, S_, B_Q_W)
    return jnp.concatenate([oa, ob], axis=-1) @ w_out

def token_shift_centred(x):
    prev = jnp.pad(x, ((0, 0), (1, 0), (0, 0)))[:, :-1]
    nxt = jnp.pad(x, ((0, 0), (0, 1), (0, 0)))[:, 1:]
    return 0.5 * (prev + nxt) - x

def wkv_scan(r, w, k, v, a_vec, b_vec, reverse):
    B_, S_, H_, N_ = r.shape
    xs = tuple(jnp.moveaxis(t, 1, 0) for t in (r, w, k, v, a_vec, b_vec))

    def step(state, inp):
        r_t, w_t, k_t, v_t, a_t, b_t = inp
        sa = jnp.einsum('bhvk,bhk->bhv', state, a_t)
        state = state * w_t[:, :, None, :] + sa[..., None] * b_t[:, :, None, :] + v_t[..., None] * k_t[:, :, None, :]
        return state, jnp.einsum('bhvk,bhk->bhv', state, r_t)

    s0 = jnp.zeros((B_, H_, N_, N_), jnp.float32)
    _, y = lax.scan(step, s0, xs, reverse=reverse)
    return jnp.moveaxis(y, 0, 1)

def rwkv7_bidir(h, mix, w_rkv, w0, w1, w2, a0, a1, a2, g1, g2, k_k, k_a, r_k, ln_g, ln_b, w_o):
    B_, S_, D_ = h.shape
    f32 = jnp.float32
    xx = token_shift_centred(h)
    xr, xw, xk, xv, xa, xg = (h + xx * mix[i] for i in range(6))
    r = xr @ w_rkv[0]
    k = xk @ w_rkv[1]
    v = xv @ w_rkv[2]
    g = jax.nn.sigmoid(xg @ g1) @ g2
    heads = lambda t: t.astype(f32).reshape(B_, S_, RWKV_HEADS, RWKV_HEAD)
    kk = heads(k * k_k)
    kk = kk / jnp.maximum(jnp.sqrt(jnp.sum(kk * kk, axis=-1, keepdims=True)), 1e-12)
    rf = heads(r)
    vf = heads(v)
    rk = r_k.astype(f32)
    ys = []
    bonuses = []
    for z in range(2):
        wlog = -jax.nn.softplus(-(w0[z] + jnp.tanh(xw @ w1[z]) @ w2[z]).astype(f32)) - 0.5
        decay = heads(jnp.exp(-jnp.exp(wlog)))
        a = jax.nn.sigmoid((a0[z] + (xa @ a1[z]) @ a2[z]).astype(f32))
        kz = heads(k.astype(f32) * (1.0 + (a - 1.0) * k_a.astype(f32)))
        az = heads(a)
        ys.append(wkv_scan(rf, decay, kz, vf, -kk, kk * az, reverse=(z == 1)))
        bonuses.append(jnp.sum(rf * kz * rk, axis=-1, keepdims=True) * vf)
    y = ys[0] + ys[1]
    mu = jnp.mean(y, axis=-1, keepdims=True)
    var = jnp.mean(jnp.square(y - mu), axis=-1, keepdims=True)
    yn = ((y - mu) * lax.rsqrt(var + GN_EPS)).reshape(B_, S_, D_) * ln_g.astype(f32) + ln_b.astype(f32)
    out = (yn + (bonuses[0] + bonuses[1]).reshape(B_, S_, D_)) * g.astype(f32)
    return out.astype(h.dtype) @ w_o

def peer(h, w_q, subkeys, u_tab, v_tab):
    B_, S_, D_ = h.shape
    T = B_ * S_
    ht = h.reshape(T, D_)
    q = (ht @ w_q).reshape(T, PEER_HEADS, 2, D_KEY_HALF)
    s = jnp.einsum('thpc,hpnc->thpn', q, subkeys).astype(jnp.float32)
    s_top, i_top = lax.top_k(s, PEER_TOPK)
    cand = s_top[:, :, 0, :, None] + s_top[:, :, 1, None, :]
    cidx = i_top[:, :, 0, :, None] * N_KEYS + i_top[:, :, 1, None, :]
    best, pos = lax.top_k(cand.reshape(T, PEER_HEADS, PEER_TOPK * PEER_TOPK), PEER_TOPK)
    eidx = jnp.take_along_axis(cidx.reshape(T, PEER_HEADS, PEER_TOPK * PEER_TOPK), pos, axis=-1)
    gate = jax.nn.softmax(best, axis=-1).astype(h.dtype)
    nblk = T // TOKEN_BLOCK

    def expert_block(args):
        xb, eb, gb = args
        u = jnp.take(u_tab, eb, axis=0)
        act = jax.nn.gelu(jnp.einsum('thkd,td->thk', u, xb))
        vv = jnp.take(v_tab, eb, axis=0)
        return jnp.einsum('thk,thkd->td', gb * act, vv)

    y = lax.map(expert_block, (ht.reshape(nblk, TOKEN_BLOCK, D_),
                               eidx.reshape(nblk, TOKEN_BLOCK, PEER_HEADS, PEER_TOPK),
                               gate.reshape(nblk, TOKEN_BLOCK, PEER_HEADS, PEER_TOPK)))
    return y.reshape(B_, S_, D_)

def setup_inputs(seed: int = 0) -> dict:
    key = jax.random.key(seed)
    ks = jax.random.split(key, 32)
    D = D_MODEL
    nrm = lambda k, shape, s: jax.random.normal(k, shape, jnp.float32) * s
    return {
        'x': nrm(ks[0], (BATCH, SEQ, D), 1.0),
        'c': nrm(ks[1], (BATCH, D), 1.0),
        'ada_w': nrm(ks[2], (DEPTH, D, 6 * D), 0.5 * D ** -0.5),
        'ada_b': nrm(ks[3], (DEPTH, 6 * D), 0.01),
        'norm_g': 1.0 + nrm(ks[4], (DEPTH, 2, D), 0.02),
        'attn_w_in': nrm(ks[5], (N_EVEN, D, IN_W), D ** -0.5),
        'attn_qk_g': 1.0 + nrm(ks[6], (N_EVEN, 4, HEAD_DIM), 0.02),
        'diff_lambda': nrm(ks[7], (N_EVEN, 4, HEAD_DIM), 0.1),
        'diff_subln_g': 1.0 + nrm(ks[8], (N_EVEN, A_V_DIM), 0.02),
        'attn_w_out': nrm(ks[9], (N_EVEN, MIX_W, D), MIX_W ** -0.5),
        'rel_bias': nrm(ks[10], (REL_BUCKETS, A_MAPS), 0.2),
        'rwkv_mix': jax.random.uniform(ks[11], (N_ODD, 6, D), jnp.float32),
        'rwkv_w_rkv': nrm(ks[12], (N_ODD, 3, D, D), D ** -0.5),
        'rwkv_w0': jax.random.uniform(ks[13], (N_ODD, 2, D), jnp.float32, -4.0, 0.0),
        'rwkv_w1': nrm(ks[14], (N_ODD, 2, D, DECAY_LORA), D ** -0.5),
        'rwkv_w2': nrm(ks[15], (N_ODD, 2, DECAY_LORA, D), 0.5 * DECAY_LORA ** -0.5),
        'rwkv_a0': nrm(ks[16], (N_ODD, 2, D), 0.1),
        'rwkv_a1': nrm(ks[17], (N_ODD, 2, D, ICLR_LORA), D ** -0.5),
        'rwkv_a2': nrm(ks[18], (N_ODD, 2, ICLR_LORA, D), 0.5 * ICLR_LORA ** -0.5),
        'rwkv_g1': nrm(ks[19], (N_ODD, D, GATE_LORA), D ** -0.5),
        'rwkv_g2': nrm(ks[20], (N_ODD, GATE_LORA, D), GATE_LORA ** -0.5),
        'rwkv_k_k': 0.85 + nrm(ks[21], (N_ODD, D), 0.02),
        'rwkv_k_a': 1.0 + nrm(ks[22], (N_ODD, D), 0.02),
        'rwkv_r_k': nrm(ks[23], (N_ODD, RWKV_HEADS, RWKV_HEAD), 0.1),
        'rwkv_ln_g': 1.0 + nrm(ks[24], (N_ODD, D), 0.02),
        'rwkv_ln_b': nrm(ks[25], (N_ODD, D), 0.01),
        'rwkv_w_o': nrm(ks[26], (N_ODD, D, D), D ** -0.5),
        'peer_w_q': nrm(ks[27], (DEPTH, D, PEER_HEADS * D_KEY), D ** -0.5),
        'peer_subkeys': nrm(ks[28], (DEPTH, PEER_HEADS, 2, N_KEYS, D_KEY_HALF), D_KEY_HALF ** -0.5),
        'peer_u': nrm(ks[29], (DEPTH, N_EXPERTS, D), D ** -0.5),
        'peer_v': nrm(ks[30], (DEPTH, N_EXPERTS, D), 0.5),
    }

def reference(x, c, ada_w, ada_b, norm_g, attn_w_in, attn_qk_g, diff_lambda, diff_subln_g, attn_w_out, rel_bias,
              rwkv_mix, rwkv_w_rkv, rwkv_w0, rwkv_w1, rwkv_w2, rwkv_a0, rwkv_a1, rwkv_a2, rwkv_g1, rwkv_g2,
              rwkv_k_k, rwkv_k_a, rwkv_r_k, rwkv_ln_g, rwkv_ln_b, rwkv_w_o,
              peer_w_q, peer_subkeys, peer_u, peer_v):
    cs = jax.nn.silu(c)
    for layer in range(DEPTH):
        mod = cs @ ada_w[layer] + ada_b[layer]
        sh1, sc1, gt1, sh2, sc2, gt2 = jnp.split(mod[:, None, :], 6, axis=-1)
        h = rms_norm(x, norm_g[layer, 0]) * (1.0 + sc1) + sh1
        j = layer // 2
        if layer % 2 == 0:
            lambda_init = 0.8 - 0.6 * math.exp(-0.3 * layer)
            y = hybrid_attention(h, attn_w_in[j], attn_qk_g[j], diff_lambda[j], diff_subln_g[j], attn_w_out[j], rel_bias, lambda_init)
        else:
            y = rwkv7_bidir(h, rwkv_mix[j], rwkv_w_rkv[j], rwkv_w0[j], rwkv_w1[j], rwkv_w2[j], rwkv_a0[j], rwkv_a1[j], rwkv_a2[j],
                            rwkv_g1[j], rwkv_g2[j], rwkv_k_k[j], rwkv_k_a[j], rwkv_r_k[j], rwkv_ln_g[j], rwkv_ln_b[j], rwkv_w_o[j])
        x = x + (gt1 * y).astype(x.dtype)
        h = rms_norm(x, norm_g[layer, 1]) * (1.0 + sc2) + sh2
        x = x + (gt2 * peer(h, peer_w_q[layer], peer_subkeys[layer], peer_u[layer], peer_v[layer])).astype(x.dtype)
    return x


_drawn_inputs = setup_inputs


def setup_inputs(seed=0):
    import zlib

    import numpy as np

    out = dict(_drawn_inputs(seed))
    spreads = {}
    factors = {'ada_b': 2.706,
     'norm_g': 2.971,
     'attn_qk_g': 8.0,
     'diff_lambda': 3.543,
     'diff_subln_g': 6.341,
     'rel_bias': 4.851,
     'rwkv_w1': 3.792,
     'rwkv_w2': 3.879,
     'rwkv_a0': 5.815,
     'rwkv_k_k': 6.619,
     'rwkv_k_a': 6.115,
     'rwkv_ln_g': 8.0,
     'rwkv_ln_b': 8.0}
    for name, (base, spread) in spreads.items():
        noise = np.random.default_rng([zlib.crc32(name.encode()), seed]).standard_normal(out[name].shape)
        drawn = base * np.exp(spread * noise) if base else spread * noise
        out[name] = jnp.asarray(drawn.astype(out[name].dtype))
    for name, factor in factors.items():
        out[name] = (out[name] * factor).astype(out[name].dtype)
    return out
```

```python
from contextlib import ExitStack

import concourse.bass as bass
import numpy as np
from concourse import mybir

F32 = mybir.dt.float32
BF16 = mybir.dt.bfloat16
U32 = mybir.dt.uint32
ALU = mybir.AluOpType
ACT = mybir.ActivationFunctionType
AX = mybir.AxisListType

P = 128
D = 1024
T = 512
DC = D // P
TC = T // P
DEPTH = 2
EPS = 1e-6

HD = 64
QKV_CHUNKS = 18
QK_CHUNKS = 13
ROPE_FIRST = 8
REL_BUCKETS = 32
MAPS = 8
REL_W = 1024
TOEP_W = T + (TC - 1) * P
LAMBDA_INIT = 0.2

PH = 8
HP = 2 * PH
NK = 128
TOPK = 16
NEG = -3.0e38
GROUP = 4
GROUPS = NK // GROUP

COLS = {}
_n = 0
for _name, _w in (("c", 8), ("ada_b", 96), ("norm_g", 32), ("qk_g", QK_CHUNKS), ("subln_g", 1),
                  ("mix", 48), ("w0", 16), ("a0", 16), ("k_k", 8), ("k_a", 8), ("r_k", 8),
                  ("ln_g", 8), ("ln_b", 8)):
    COLS[_name] = (_n, _n + _w)
    _n += _w
NCOLS = _n

CONSTS = {}
_n = 0
for _name, _w in (("ident", P), ("ones_d", P), ("ones_head", P), ("ones_v", P), ("ones_sum", P), ("anti", P),
                  ("rot", P), ("cos", T), ("sin", T), ("iota", P), ("lower", P), ("upper", P),
                  ("lower_incl", P), ("upper_incl", P), ("blockdiag", P)):
    CONSTS[_name] = (_n, _n + _w)
    _n += _w
NCONST = _n

LEVELS = 7


def host_constants():
    c = np.zeros((P, NCONST), np.float32)

    def put(name, a):
        c[:, CONSTS[name][0]:CONSTS[name][1]] = a

    i = np.arange(P)
    put("ident", np.eye(P))
    put("ones_d", np.full((P, P), 1.0 / D))
    put("ones_head", (i[:, None] // HD == i[None] // HD) / HD)
    put("ones_v", np.full((P, P), 1.0 / P))
    put("ones_sum", i[:, None] // HD == i[None] // HD)
    put("anti", np.eye(P)[::-1])
    rot = np.zeros((P, P))
    for m in range(P):
        if m % 32 < 16:
            rot[m + 16, m] = -1.0
        else:
            rot[m - 16, m] = 1.0
    put("rot", rot)
    inv = 10000.0 ** (-np.arange(0, 32, 2, dtype=np.float32) / 32)
    t = np.arange(T)
    pos = np.where((i % HD < 32)[:, None], (t // 64)[None], (t % 64)[None]).astype(np.float32)
    ang = pos * inv[i % 16][:, None].astype(np.float32)
    put("cos", np.cos(ang))
    put("sin", np.sin(ang))
    put("iota", np.tile(i, (P, 1)))
    put("lower", i[:, None] > i[None])
    put("upper", i[:, None] < i[None])
    put("lower_incl", i[:, None] >= i[None])
    put("upper_incl", i[:, None] <= i[None])
    put("blockdiag", i[:, None] // HD == i[None] // HD)
    return c


def host_level_masks():
    i = np.arange(P)
    out = np.zeros((P, 2, LEVELS, P), np.uint32)
    for lv in range(LEVELS):
        b = i >> lv
        m = (b[:, None] % 2 == 1) & (b[:, None] - 1 == b[None])
        out[:, 0, lv] = m
        out[:, 1, lv] = m.T
    return out


def host_bucket_onehot():
    rel = np.arange(-(T - 1), T)
    nb, me = REL_BUCKETS // 2, REL_BUCKETS // 4
    n = np.abs(rel)
    nf = np.maximum(n, 1).astype(np.float32)
    large = me + (np.log(nf / np.float32(me)) / np.float32(np.log(128 / me)) * np.float32(nb - me)).astype(np.int32)
    bucket = np.where(rel > 0, nb, 0) + np.where(n < me, n, np.minimum(large, nb - 1))
    out = np.zeros((REL_BUCKETS, REL_W), np.float32)
    out[bucket, np.arange(2 * T - 1)] = 1.0
    return out


class Kernel:

    def __init__(self, nc, io, ctx):
        self.nc, self.io, self.ctx = nc, io, ctx
        self.stage_sems = []
        self.x = self.sb(ctx, "x", [P, DC, T])
        self.h = self.sb(ctx, "h", [P, DC, T + 2])
        self.cols = self.sb(ctx, "cols", [P, NCOLS])
        self.consts = self.sb(ctx, "consts", [P, NCONST])
        self.mod = self.sb(ctx, "mod", [P, DEPTH, 48])
        self.scale = self.sb(ctx, "scale", [P, DEPTH, 2, DC])
        self.eps = self.sb(ctx, "eps", [P, 4])
        self.ps = [ctx.enter_context(nc.psum_tensor(f"bank{i}", [P, T], F32)) for i in range(8)]

    def sb(self, ctx, name, shape, dt=F32):
        return ctx.enter_context(self.nc.sbuf_tensor(name, shape, dt))

    def sem(self, name):
        handle = self.nc.alloc_semaphore(name)
        self.stage_sems.append(handle)
        return handle

    def end_stage(self):
        self.nc.clear_and_free_semaphores(self.stage_sems)
        self.nc.all_engine_barrier()
        self.stage_sems = []

    def col(self, name, i):
        a = COLS[name][0] + i
        return self.cols[:, a:a + 1]

    def const(self, name):
        return self.consts[:, CONSTS[name][0]:CONSTS[name][1]]

    def hc(self, c):
        return self.h[:, c, 1:T + 1]


def stage_modulation(K):
    nc, io = K.nc, K.io
    RING, W = 3, 3072
    with ExitStack() as ctx:
        ring = K.sb(ctx, "ada_ring", [P, RING, W])
        acc = K.sb(ctx, "ada_acc", [P, 2, W])
        cs = K.sb(ctx, "cs", [P, DC])
        sig = K.sb(ctx, "cs_sigmoid", [P, DC])
        ones = K.sb(ctx, "ones_col", [P, 1])
        loaded = [K.sem(f"ada_loaded{i}") for i in range(RING)]
        in_loaded = K.sem("inputs_loaded")
        sig_done = K.sem("cs_sigmoid_done")
        cs_done = K.sem("cs_done")
        accumulated = K.sem("ada_accumulated")
        summed = K.sem("ada_summed")
        mod_done = K.sem("mod_done")
        tiles = [(l, k, hf) for l in range(DEPTH) for k in range(DC) for hf in range(2)]
        with nc.Block() as block:
            @block.sync
            def _(sp):
                sp.dma_start(K.cols[:, :], io["cols"]).then_inc(in_loaded, 16)
                for i, (l, k, hf) in enumerate(tiles):
                    if i >= RING:
                        sp.wait_ge(accumulated, i - RING + 1)
                    sp.dma_start(ring[:, i % RING, :],
                                 io["ada_w"][l, k * P:(k + 1) * P, hf * W:(hf + 1) * W]).then_inc(loaded[i % RING], 16)
                    if i == 1:
                        sp.dma_start(K.x[:, :, :], io["xT"]).then_inc(in_loaded, 16)
                        sp.dma_start(K.consts[:, :], io["consts"]).then_inc(in_loaded, 16)

            @block.scalar
            def _(act):
                act.wait_ge(in_loaded, 48)
                nc.scalar.activation(sig[:, :], K.cols[:, COLS["c"][0]:COLS["c"][1]], ACT.Sigmoid).then_inc(sig_done, 1)

            @block.vector
            def _(dve):
                nc.vector.memset(ones[:, :], 1.0).then_inc(cs_done, 1)
                nc.vector.memset(K.eps[:, 0:1], EPS).then_inc(cs_done, 1)
                nc.vector.memset(K.eps[:, 1:2], 64e-5).then_inc(cs_done, 1)
                nc.vector.memset(K.h[:, :, :], 0.0).then_inc(cs_done, 1)
                dve.wait_ge(sig_done, 1)
                nc.vector.tensor_tensor(cs[:, :], sig[:, :], K.cols[:, COLS["c"][0]:COLS["c"][1]],
                                        ALU.mult).then_inc(cs_done, 1)
                dve.wait_ge(cs_done, 5)
                for i, (l, k, hf) in enumerate(tiles):
                    dve.wait_ge(loaded[i % RING], 16 * (i // RING + 1))
                    if k == 0:
                        if l:
                            dve.wait_ge(summed, l)
                        nc.vector.tensor_scalar(acc[:, hf, :], ring[:, i % RING, :], cs[:, k:k + 1], None,
                                                ALU.mult).then_inc(accumulated, 1)
                    else:
                        dve.wait_ge(accumulated, i - 1)
                        nc.vector.scalar_tensor_tensor(out=acc[:, hf, :], in0=ring[:, i % RING, :],
                                                       scalar=cs[:, k:k + 1], in1=acc[:, hf, :], op0=ALU.mult,
                                                       op1=ALU.add).then_inc(accumulated, 1)
                    if k == DC - 1 and hf == 1:
                        b = COLS["ada_b"][0] + 48 * l
                        dve.wait_ge(summed, l + 1)
                        nc.vector.tensor_tensor(K.mod[:, l, :], K.ps[l][:, 0:48], K.cols[:, b:b + 48],
                                                ALU.add).then_inc(mod_done, 1)
                        for s in range(2):
                            g = COLS["norm_g"][0] + (2 * l + s) * DC
                            dve.wait_ge(mod_done, 3 * l + 1)
                            nc.vector.scalar_tensor_tensor(
                                out=K.scale[:, l, s, :], in0=K.mod[:, l, 8 + 24 * s:16 + 24 * s], scalar=1.0,
                                in1=K.cols[:, g:g + DC], op0=ALU.add, op1=ALU.mult).then_inc(mod_done, 1)

            @block.tensor
            def _(pe):
                pe.wait_ge(cs_done, 5)
                for l in range(DEPTH):
                    pe.wait_ge(accumulated, 2 * DC * (l + 1))
                    for j in range(48):
                        last = nc.tensor.matmul(K.ps[l][:, j:j + 1], acc[:, j // 24, (j % 24) * P:(j % 24 + 1) * P],
                                                ones[:, :], start=True, stop=True)
                    last.then_inc(summed, 1)


def stage_norm(K, layer, sub):
    nc = K.nc
    tag = f"n{layer}{sub}_"
    with ExitStack() as ctx:
        sq = K.sb(ctx, tag + "sq", [P, DC, T])
        std = K.sb(ctx, tag + "std", [P, T])
        rstd = K.sb(ctx, tag + "rstd", [P, T])
        squared = K.sem(tag + "squared")
        mean_done = K.sem(tag + "mean_done")
        std_done = K.sem(tag + "std_done")
        rstd_done = K.sem(tag + "rstd_done")
        scaled = K.sem(tag + "scaled")
        shifted = K.sem(tag + "shifted")
        with nc.Block() as block:
            @block.scalar
            def _(act):
                for c in range(DC):
                    nc.scalar.activation(sq[:, c, :], K.x[:, c, :], ACT.Square).then_inc(squared, 1)
                act.wait_ge(mean_done, 1)
                nc.scalar.activation(std[:, :], K.ps[0][:, :], ACT.Sqrt, bias=K.eps[:, 0:1]).then_inc(std_done, 1)
                for c in range(DC):
                    act.wait_ge(scaled, c + 1)
                    nc.scalar.activation(K.hc(c), K.hc(c), ACT.Identity,
                                         bias=K.mod[:, layer, 24 * sub + c:24 * sub + c + 1]).then_inc(shifted, 1)

            @block.tensor
            def _(pe):
                for c in range(DC):
                    pe.wait_ge(squared, c + 1)
                    last = nc.tensor.matmul(K.ps[0][:, :], K.const("ones_d"), sq[:, c, :], start=(c == 0),
                                            stop=(c == DC - 1))
                last.then_inc(mean_done, 1)

            @block.vector
            def _(dve):
                dve.wait_ge(std_done, 1)
                nc.vector.reciprocal(rstd[:, :], std[:, :]).then_inc(rstd_done, 1)
                dve.wait_ge(rstd_done, 1)
                for c in range(DC):
                    nc.vector.scalar_tensor_tensor(out=K.hc(c), in0=K.x[:, c, :],
                                                   scalar=K.scale[:, layer, sub, c:c + 1], in1=rstd[:, :],
                                                   op0=ALU.mult, op1=ALU.mult).then_inc(scaled, 1)


def stage_output(K):
    with ExitStack() as ctx:
        out_written = K.sem("out_written")
        with K.nc.Block() as block:
            @block.sync
            def _(sp):
                sp.dma_start(K.io["outT"], K.x[:, :, :]).then_inc(out_written, 16)
                sp.wait_ge(out_written, 16)


def stage_attention(K):
    nc, io = K.nc, K.io
    WR = 4
    UNITS = [(kind, a, qb) for kind in "AB" for a in range(4) for qb in range(TC)]
    with ExitStack() as ctx:
        wt = K.sb(ctx, "at_wt", [P, WR, DC, P])
        qkv = K.sb(ctx, "at_qkv", [P, QKV_CHUNKS, T])
        vtok = K.sb(ctx, "at_vtok", [P, TC, 4, P])
        vpad = K.sb(ctx, "at_vpad", [P, TC, 2, P])
        heads = K.sb(ctx, "at_heads", [P, DC, T])
        toep = K.sb(ctx, "at_toep", [P, MAPS, TOEP_W])
        sq = K.sb(ctx, "at_sq", [P, 2, T])
        std = K.sb(ctx, "at_std", [P, 2, T])
        rstd = K.sb(ctx, "at_rstd", [P, 2, T])
        rtmp = K.sb(ctx, "at_rtmp", [P, 2, T])
        bucket = K.sb(ctx, "at_bucket", [REL_BUCKETS, REL_W])
        relb = K.sb(ctx, "at_relb", [REL_BUCKETS, MAPS])
        relrow = K.sb(ctx, "at_relrow", [MAPS, REL_W])
        lam_in = K.sb(ctx, "at_lam_in", [P, 4, HD])
        lam_p = K.sb(ctx, "at_lam_p", [P, 2, HD])
        lam_s = K.sb(ctx, "at_lam_s", [P, 8])
        gq = K.sb(ctx, "at_gq", [P, QK_CHUNKS])
        subg = K.sb(ctx, "at_subg", [P, 1])
        prob = K.sb(ctx, "at_prob", [P, 2, 2, T])
        probT = K.sb(ctx, "at_probT", [P, 2, 2, TC, P])
        nmax = K.sb(ctx, "at_nmax", [P, 2, 2])
        esum = K.sb(ctx, "at_esum", [P, 2, 2])
        rinv = K.sb(ctx, "at_rinv", [P, 2, 2])
        rlam = K.sb(ctx, "at_rlam", [P, 2])

        w_loaded = [K.sem(f"at_w_loaded{i}") for i in range(WR)]
        small_loaded = K.sem("at_small_loaded")
        rel_done = K.sem("at_rel_done")
        relrow_done = K.sem("at_relrow_done")
        relrow_stored = K.sem("at_relrow_stored")
        toep_loaded = K.sem("at_toep_loaded")
        prepared = K.sem("at_prepared")
        lam_exp = K.sem("at_lam_exp")
        projected = K.sem("at_projected")
        raw_copied = K.sem("at_raw_copied")
        squared = K.sem("at_squared")
        meaned = K.sem("at_meaned")
        std_done = K.sem("at_std_done")
        rstd_done = K.sem("at_rstd_done")
        normed = K.sem("at_normed")
        rotated = K.sem("at_rotated")
        roped = K.sem("at_roped")
        rope_step = K.sem("at_rope_step")
        v_transposed = K.sem("at_v_transposed")
        v_copied = K.sem("at_v_copied")
        with nc.Block() as block:
            @block.sync
            def _(sp):
                sp.dma_start(bucket[:, :], io["bucket"]).then_inc(small_loaded, 16)
                sp.dma_start(relb[:, :], io["rel_bias"]).then_inc(small_loaded, 16)
                sp.dma_start(lam_in[:, :, :].rearrange("p a b -> p (a b)"),
                             io["lam"].to_broadcast([P, 4 * HD])).then_inc(small_loaded, 16)
                for m in range(QKV_CHUNKS):
                    if m >= WR:
                        sp.wait_ge(projected, m - WR + 1)
                    sp.dma_start(wt[:, m % WR], io["w_in"][m]).then_inc(w_loaded[m % WR], 16)
                    if m == 2:
                        sp.wait_ge(relrow_done, 2)
                        sp.dma_start(io["rel_scratch"], relrow[:, :]).then_inc(relrow_stored, 16)
                    if m == 6:
                        sp.wait_ge(relrow_stored, 16)
                        sp.dma_start(toep[:, :, :], io["rel_toeplitz"]).then_inc(toep_loaded, 16)

            @block.tensor
            def _(pe):
                pe.wait_ge(small_loaded, 48)
                for half in range(2):
                    nc.tensor.matmul(K.ps[6 + half][0:MAPS, :], relb[:, :], bucket[:, half * T:(half + 1) * T],
                                     start=True, stop=True).then_inc(rel_done, 1)

                def mean_of(m):
                    pe.wait_ge(squared, m + 1)
                    if m >= 2:
                        pe.wait_ge(std_done, m - 1)
                    nc.tensor.matmul(K.ps[3 + m % 2][:, :], K.const("ones_head"), sq[:, m % 2, :], start=True,
                                     stop=True).then_inc(meaned, 1)

                def rotate(m):
                    j = m - ROPE_FIRST
                    pe.wait_ge(normed, m + 1)
                    if j >= 1:
                        pe.wait_ge(rope_step, 3 * j)
                    nc.tensor.matmul(K.ps[5][:, :], K.const("rot"), qkv[:, m, :], start=True,
                                     stop=True).then_inc(rotated, 1)

                for m in range(QKV_CHUNKS):
                    pe.wait_ge(w_loaded[m % WR], 16 * (m // WR + 1))
                    if m >= 3:
                        pe.wait_ge(raw_copied, m - 2)
                        if m - 3 < QK_CHUNKS:
                            pe.wait_ge(squared, m - 2)
                    for k in range(DC):
                        last = nc.tensor.matmul(K.ps[m % 3][:, :], wt[:, m % WR, k, :], K.hc(k), start=(k == 0),
                                                stop=(k == DC - 1))
                    last.then_inc(projected, 1)
                    if 1 <= m <= QK_CHUNKS:
                        mean_of(m - 1)
                    if ROPE_FIRST + 3 <= m < QK_CHUNKS + 3:
                        rotate(m - 3)
                for j in range(5):
                    pe.wait_ge(raw_copied, QK_CHUNKS + j + 1)
                    if j < 2:
                        pe.wait_ge(relrow_done, 2)
                    else:
                        pe.wait_ge(v_copied, j - 1)
                    for t in range(TC):
                        last = nc.tensor.transpose(K.ps[6 + j % 2][:, t * P:(t + 1) * P],
                                                   qkv[:, QK_CHUNKS + j, t * P:(t + 1) * P], K.const("ident"))
                    last.then_inc(v_transposed, 1)

            @block.scalar
            def _(act):
                def std_of(m):
                    act.wait_ge(meaned, m + 1)
                    if m >= 2:
                        act.wait_ge(rstd_done, m - 1)
                    nc.scalar.activation(std[:, m % 2, :], K.ps[3 + m % 2][:, :], ACT.Sqrt,
                                         bias=K.eps[:, 0:1]).then_inc(std_done, 1)

                for m in range(QKV_CHUNKS):
                    act.wait_ge(projected, m + 1)
                    if m < QK_CHUNKS:
                        if m >= 2:
                            act.wait_ge(meaned, m - 1)
                        nc.scalar.activation(sq[:, m % 2, :], K.ps[m % 3][:, :], ACT.Square).then_inc(squared, 1)
                    nc.scalar.activation(qkv[:, m, :], K.ps[m % 3][:, :], ACT.Copy).then_inc(raw_copied, 1)
                    if 1 <= m <= QK_CHUNKS:
                        std_of(m - 1)
                act.wait_ge(prepared, 5)
                nc.scalar.activation(lam_s[:, 2:4], lam_s[:, 0:2], ACT.Exp).then_inc(lam_exp, 1)

            @block.vector
            def _(dve):
                for half in range(2):
                    dve.wait_ge(rel_done, half + 1)
                    nc.vector.tensor_copy(relrow[:, half * T:(half + 1) * T],
                                          K.ps[6 + half][0:MAPS, :]).then_inc(relrow_done, 1)
                q0 = COLS["qk_g"][0]
                nc.vector.tensor_copy(gq[:, :], K.cols[:, q0:q0 + QK_CHUNKS]).then_inc(prepared, 1)
                dve.wait_ge(prepared, 1)
                nc.vector.tensor_scalar(gq[:, 0:4], gq[:, 0:4], HD ** -0.5, None, ALU.mult).then_inc(prepared, 1)
                nc.vector.tensor_scalar(gq[:, 8:12], gq[:, 8:12], HD ** -0.5, None, ALU.mult).then_inc(prepared, 1)
                nc.vector.tensor_tensor(lam_p[:, :, :], lam_in[:, 0:4:2, :], lam_in[:, 1:4:2, :],
                                        ALU.mult).then_inc(prepared, 1)
                dve.wait_ge(prepared, 4)
                nc.vector.tensor_reduce(lam_s[:, 0:2], lam_p[:, :, :], AX.X, ALU.add).then_inc(prepared, 1)
                nc.vector.tensor_scalar(subg[:, :], K.col("subln_g", 0), 1.0 - LAMBDA_INIT, None,
                                        ALU.mult).then_inc(prepared, 1)
                nc.vector.memset(vpad[:, :, :, :], 0.0).then_inc(prepared, 1)

                def rope(m):
                    j = m - ROPE_FIRST
                    dve.wait_ge(rotated, j + 1)
                    nc.vector.tensor_tensor(rtmp[:, 0, :], K.ps[5][:, :], K.const("sin"), ALU.mult).then_inc(rope_step, 1)
                    nc.vector.tensor_tensor(rtmp[:, 1, :], qkv[:, m, :], K.const("cos"), ALU.mult).then_inc(rope_step, 1)
                    dve.wait_ge(rope_step, 3 * j + 2)
                    nc.vector.tensor_tensor(qkv[:, m, :], rtmp[:, 0, :], rtmp[:, 1, :], ALU.add).then_inc(rope_step, 1)

                for m in range(QK_CHUNKS):
                    dve.wait_ge(std_done, m + 1)
                    nc.vector.reciprocal(rstd[:, m % 2, :], std[:, m % 2, :]).then_inc(rstd_done, 1)
                    dve.wait_ge(rstd_done, m + 1)
                    dve.wait_ge(raw_copied, m + 1)
                    nc.vector.scalar_tensor_tensor(out=qkv[:, m, :], in0=qkv[:, m, :], scalar=gq[:, m:m + 1],
                                                   in1=rstd[:, m % 2, :], op0=ALU.mult,
                                                   op1=ALU.mult).then_inc(normed, 1)
                    if m - 2 >= ROPE_FIRST:
                        rope(m - 2)
                rope(QK_CHUNKS - 2)
                rope(QK_CHUNKS - 1)
                for j in range(5):
                    dve.wait_ge(v_transposed, j + 1)
                    if j < 4:
                        nc.vector.tensor_copy(vtok[:, :, j, :],
                                              K.ps[6 + j % 2][:, :].rearrange("p (t f) -> p t f", t=TC)).then_inc(v_copied, 1)
                    else:
                        vb = K.ps[6][:, :].rearrange("p (t g f) -> p t g f", t=TC, g=2)
                        nc.vector.tensor_copy(vpad[:, :, 0, 0:HD], vb[:, :, 0, :]).then_inc(v_copied, 1)
                        nc.vector.tensor_copy(vpad[:, :, 1, HD:P], vb[:, :, 1, :]).then_inc(v_copied, 1)
                dve.wait_ge(lam_exp, 1)
                nc.vector.tensor_tensor(lam_s[:, 4:5], lam_s[:, 3:4], lam_s[:, 2:3], ALU.subtract).then_inc(prepared, 1)
                dve.wait_ge(prepared, 8)
                nc.vector.tensor_scalar(lam_s[:, 5:6], lam_s[:, 4:5], -LAMBDA_INIT, None, ALU.add).then_inc(prepared, 1)

        scored = K.sem("at_scored")
        maxed = K.sem("at_maxed")
        exped = K.sem("at_exped")
        inverted = K.sem("at_inverted")
        weighted = K.sem("at_weighted")
        p_transposed = K.sem("at_p_transposed")
        p_copied = K.sem("at_p_copied")
        attended = K.sem("at_attended")
        head_copied = K.sem("at_head_copied")

        def tiles_before(u):
            return sum(1 if kind == "A" else 2 for kind, _, _ in UNITS[:u])

        def weights_before(u):
            return 3 * u if u < 16 else 48 + 2 * (u - 16)

        with nc.Block() as block:
            @block.tensor
            def _(pe):
                def scores(u):
                    kind, a, qb = UNITS[u]
                    qs = slice(qb * P, (qb + 1) * P)
                    if u >= 2:
                        pe.wait_ge(exped, 2 * (u - 1))
                    for e in range(2):
                        out = K.ps[2 * (u % 2) + e][:, :]
                        rows = slice(HD * e, HD * (e + 1))
                        if kind == "A":
                            off = (TC - 1 - qb) * P
                            nc.tensor.matmul(out, K.const("anti"), toep[:, 2 * a + e, off:off + T], start=True,
                                             stop=False)
                            last = nc.tensor.matmul(out, qkv[rows, a, qs], qkv[rows, 4 + a, :], start=False, stop=True)
                        else:
                            last = nc.tensor.matmul(out, qkv[rows, 8 + a, qs], qkv[rows, 12, :], start=True, stop=True)
                        last.then_inc(scored, 1)

                def attend(u):
                    kind, a, qb = UNITS[u]
                    n = 1 if kind == "A" else 2
                    pe.wait_ge(weighted, weights_before(u + 1))
                    for e in range(n):
                        tile = tiles_before(u) + e
                        if tile >= 2:
                            pe.wait_ge(p_copied, tile - 1)
                        for kc in range(TC):
                            last = nc.tensor.transpose(K.ps[4 + tile % 2][:, kc * P:(kc + 1) * P],
                                                       prob[:, u % 2, e, kc * P:(kc + 1) * P], K.const("ident"))
                        last.then_inc(p_transposed, 1)
                    if u >= 2:
                        pe.wait_ge(head_copied, u - 1)
                    out = K.ps[6 + u % 2][:, 0:P]
                    for e in range(n):
                        pe.wait_ge(p_copied, tiles_before(u) + e + 1)
                        for kc in range(TC):
                            v = vtok[:, kc, a, :] if kind == "A" else vpad[:, kc, e, :]
                            last = nc.tensor.matmul(out, v, probT[:, u % 2, e, kc, :], start=(e == 0 and kc == 0),
                                                    stop=(e == n - 1 and kc == TC - 1))
                    last.then_inc(attended, 1)

                pe.wait_ge(toep_loaded, 16)
                for u in range(len(UNITS)):
                    scores(u)
                    if u:
                        attend(u - 1)
                attend(len(UNITS) - 1)

            @block.scalar
            def _(act):
                def copy_out(u):
                    kind, a, qb = UNITS[u]
                    for e in range(1 if kind == "A" else 2):
                        tile = tiles_before(u) + e
                        act.wait_ge(p_transposed, tile + 1)
                        if u >= 2:
                            act.wait_ge(attended, u - 1)
                        nc.scalar.activation(probT[:, u % 2, e, :, :],
                                             K.ps[4 + tile % 2][:, :].rearrange("p (k q) -> p k q", k=TC),
                                             ACT.Copy).then_inc(p_copied, 1)
                for u in range(len(UNITS)):
                    for e in range(2):
                        act.wait_ge(maxed, 2 * u + e + 1)
                        if u >= 2:
                            act.wait_ge(p_transposed, tiles_before(u - 1))
                        nc.scalar.activation(prob[:, u % 2, e, :], K.ps[2 * (u % 2) + e][:, :], ACT.Exp,
                                             bias=nmax[:, u % 2, e:e + 1],
                                             accum_out=esum[:, u % 2, e:e + 1]).then_inc(exped, 1)
                    if u:
                        copy_out(u - 1)
                copy_out(len(UNITS) - 1)

            @block.vector
            def _(dve):
                def copy_head(u):
                    kind, a, qb = UNITS[u]
                    c = a if kind == "A" else 4 + a
                    dve.wait_ge(attended, u + 1)
                    nc.vector.tensor_copy(heads[:, c, qb * P:(qb + 1) * P],
                                          K.ps[6 + u % 2][:, 0:P]).then_inc(head_copied, 1)
                for u, (kind, a, qb) in enumerate(UNITS):
                    for e in range(2):
                        dve.wait_ge(scored, 2 * u + e + 1)
                        if u >= 2:
                            dve.wait_ge(exped, 2 * (u - 1))
                        nc.vector.tensor_reduce(nmax[:, u % 2, e:e + 1], K.ps[2 * (u % 2) + e][:, :], AX.X, ALU.max,
                                                negate=True).then_inc(maxed, 1)
                    if u >= 2:
                        copy_head(u - 2)
                    dve.wait_ge(exped, 2 * u + 2)
                    if u >= 2:
                        dve.wait_ge(weighted, weights_before(u - 1))
                    nc.vector.reciprocal(rinv[:, u % 2, :], esum[:, u % 2, :]).then_inc(inverted, 1)
                    dve.wait_ge(inverted, u + 1)
                    w = weights_before(u)
                    if kind == "A":
                        nc.vector.tensor_tensor(rlam[:, u % 2:u % 2 + 1], rinv[:, u % 2, 1:2], lam_s[:, 5:6],
                                                ALU.mult).then_inc(weighted, 1)
                        nc.vector.tensor_scalar(prob[:, u % 2, 0, :], prob[:, u % 2, 0, :], rinv[:, u % 2, 0:1], None,
                                                ALU.mult).then_inc(weighted, 1)
                        dve.wait_ge(weighted, w + 2)
                        nc.vector.scalar_tensor_tensor(out=prob[:, u % 2, 0, :], in0=prob[:, u % 2, 1, :],
                                                       scalar=rlam[:, u % 2:u % 2 + 1], in1=prob[:, u % 2, 0, :],
                                                       op0=ALU.mult, op1=ALU.add).then_inc(weighted, 1)
                    else:
                        for e in range(2):
                            nc.vector.tensor_scalar(prob[:, u % 2, e, :], prob[:, u % 2, e, :], rinv[:, u % 2, e:e + 1],
                                                    None, ALU.mult).then_inc(weighted, 1)
                copy_head(len(UNITS) - 2)
                copy_head(len(UNITS) - 1)

        sub_squared = K.sem("at_sub_squared")
        sub_meaned = K.sem("at_sub_meaned")
        sub_std = K.sem("at_sub_std")
        sub_rstd = K.sem("at_sub_rstd")
        sub_normed = K.sem("at_sub_normed")
        wo_loaded = [K.sem(f"at_wo_loaded{i}") for i in range(WR)]
        wo_done = K.sem("at_wo_done")
        added = K.sem("at_added")
        with nc.Block() as block:
            @block.sync
            def _(sp):
                for m in range(DC):
                    if m >= WR:
                        sp.wait_ge(wo_done, m - WR + 1)
                    sp.dma_start(wt[:, m % WR], io["w_out"][m]).then_inc(wo_loaded[m % WR], 16)

            @block.scalar
            def _(act):
                for a in range(4):
                    if a >= 2:
                        act.wait_ge(sub_meaned, a - 1)
                    nc.scalar.activation(sq[:, a % 2, :], heads[:, a, :], ACT.Square).then_inc(sub_squared, 1)
                    act.wait_ge(sub_meaned, a + 1)
                    if a >= 2:
                        act.wait_ge(sub_rstd, a - 1)
                    nc.scalar.activation(std[:, a % 2, :], K.ps[a % 2][:, :], ACT.Sqrt,
                                         bias=K.eps[:, 0:1]).then_inc(sub_std, 1)

            @block.vector
            def _(dve):
                for a in range(4):
                    dve.wait_ge(sub_std, a + 1)
                    nc.vector.reciprocal(rstd[:, a % 2, :], std[:, a % 2, :]).then_inc(sub_rstd, 1)
                    dve.wait_ge(sub_rstd, a + 1)
                    nc.vector.scalar_tensor_tensor(out=heads[:, a, :], in0=heads[:, a, :], scalar=subg[:, 0:1],
                                                   in1=rstd[:, a % 2, :], op0=ALU.mult,
                                                   op1=ALU.mult).then_inc(sub_normed, 1)
                for m in range(DC):
                    dve.wait_ge(wo_done, m + 1)
                    nc.vector.scalar_tensor_tensor(out=K.x[:, m, :], in0=K.ps[2 + m % 4][:, :],
                                                   scalar=K.mod[:, 0, 16 + m:17 + m], in1=K.x[:, m, :], op0=ALU.mult,
                                                   op1=ALU.add).then_inc(added, 1)

            @block.tensor
            def _(pe):
                for a in range(4):
                    pe.wait_ge(sub_squared, a + 1)
                    if a >= 2:
                        pe.wait_ge(sub_std, a - 1)
                    nc.tensor.matmul(K.ps[a % 2][:, :], K.const("ones_v"), sq[:, a % 2, :], start=True,
                                     stop=True).then_inc(sub_meaned, 1)
                for m in range(DC):
                    pe.wait_ge(wo_loaded[m % WR], 16 * (m // WR + 1))
                    if m >= 4:
                        pe.wait_ge(added, m - 3)
                    for i, k in enumerate((4, 5, 6, 7, 0, 1, 2, 3)):
                        if m == 0 and k < 4:
                            pe.wait_ge(sub_normed, k + 1)
                        last = nc.tensor.matmul(K.ps[2 + m % 4][:, :], wt[:, m % WR, k, :], heads[:, k, :],
                                                start=(i == 0), stop=(i == DC - 1))
                    last.then_inc(wo_done, 1)


GATE_SCALE = 4096.0
TOKENS_PER_BANK = 4


def stage_peer(K, layer):
    nc, io = K.nc, K.io
    tag = f"pe{layer}_"
    with ExitStack() as ctx:
        pairT = K.sb(ctx, tag + "pairT", [P, 4, T])
        peer_choose(K, layer, tag, pairT)
        peer_gates(K, layer, tag, pairT)
    peer_experts(K, layer, tag)


def peer_choose(K, layer, tag, pairT):
    nc, io = K.nc, K.io
    WR = 4
    HT = PH * TOPK
    with ExitStack() as ctx:
        wt = K.sb(ctx, tag + "wt", [P, WR, DC, P])
        qT = K.sb(ctx, tag + "qT", [P, 2, T])
        keys = K.sb(ctx, tag + "keys", [P, HP, NK])
        s = K.sb(ctx, tag + "s", [P, TC, HP, NK])
        cut = K.sb(ctx, tag + "cut", [P, TC, 2, NK])
        top = K.sb(ctx, tag + "top", [P, TC, HP, TOPK])
        topi = K.sb(ctx, tag + "topi", [P, TC, HP, TOPK], U32)
        topf = K.sb(ctx, tag + "topf", [P, TC, HP, TOPK])
        best = K.sb(ctx, tag + "best", [P, TC, PH, TOPK])
        pos = K.sb(ctx, tag + "pos", [P, TC, PH, TOPK], U32)
        posab = K.sb(ctx, tag + "posab", [P, 2, TC, PH, TOPK], U32)
        posf = K.sb(ctx, tag + "posf", [P, 2, TC, PH, TOPK])
        ij = K.sb(ctx, tag + "ij", [P, 2, TC, PH, TOPK])
        gate = K.sb(ctx, tag + "gate", [P, 2, TC, HT])
        ghalf = K.sb(ctx, tag + "ghalf", [P, TC, HT], mybir.dt.float16)
        zsum = K.sb(ctx, tag + "zsum", [P, 2, TC, PH])
        w_loaded = [K.sem(f"{tag}w_loaded{i}") for i in range(WR)]
        keys_loaded = K.sem(tag + "keys_loaded")
        queried = K.sem(tag + "queried")
        q_copied = K.sem(tag + "q_copied")
        scored = K.sem(tag + "scored")
        s_copied = K.sem(tag + "s_copied")
        step = K.sem(tag + "top_step")
        chosen = K.sem(tag + "chosen")
        exped = K.sem(tag + "exped")
        ready = K.sem(tag + "pairs_ready")
        transposed = K.sem(tag + "pairs_transposed")
        pairs_copied = K.sem(tag + "pairs_copied")
        with nc.Block() as block:
            @block.sync
            def _(sp):
                sp.dma_start(keys[:, :, :].rearrange("p a b -> p (a b)"), io["subkeys"][layer]).then_inc(keys_loaded, 16)
                for m in range(HP):
                    if m >= WR:
                        sp.wait_ge(queried, m - WR + 1)
                    sp.dma_start(wt[:, m % WR], io["w_q"][layer, m]).then_inc(w_loaded[m % WR], 16)

            @block.tensor
            def _(pe):
                def score(m):
                    pe.wait_ge(q_copied, m + 1)
                    if m >= 2:
                        pe.wait_ge(s_copied, m - 1)
                    for t in range(TC):
                        last = nc.tensor.matmul(K.ps[2 + m % 2][:, t * NK:(t + 1) * NK], qT[:, m % 2, t * P:(t + 1) * P],
                                                keys[:, m, :], start=True, stop=True)
                    last.then_inc(scored, 1)

                pe.wait_ge(keys_loaded, 16)
                for m in range(HP):
                    pe.wait_ge(w_loaded[m % WR], 16 * (m // WR + 1))
                    if m >= 2:
                        pe.wait_ge(q_copied, m - 1)
                    for k in range(DC):
                        last = nc.tensor.matmul(K.ps[m % 2][:, :], wt[:, m % WR, k, :], K.hc(k), start=(k == 0),
                                                stop=(k == DC - 1))
                    last.then_inc(queried, 1)
                    if m:
                        score(m - 1)
                score(HP - 1)
                for a in range(4):
                    pe.wait_ge(ready, a + 1)
                    for t in range(TC):
                        src = gate[:, a, t, :] if a < 2 else ij[:, a - 2, t, :, :].rearrange("p h k -> p (h k)")
                        last = nc.tensor.transpose(K.ps[4 + a][:, t * P:(t + 1) * P], src, K.const("ident"))
                    last.then_inc(transposed, 1)

            @block.scalar
            def _(act):
                def copy_scores(m):
                    act.wait_ge(scored, m + 1)
                    nc.scalar.activation(s[:, :, m, :], K.ps[2 + m % 2][:, :].rearrange("p (t n) -> p t n", t=TC),
                                         ACT.Copy).then_inc(s_copied, 1)
                for m in range(HP):
                    act.wait_ge(queried, m + 1)
                    if m >= 2:
                        act.wait_ge(scored, m - 1)
                    nc.scalar.activation(qT[:, m % 2, :], K.ps[m % 2][:, :], ACT.Copy).then_inc(q_copied, 1)
                    if m:
                        copy_scores(m - 1)
                copy_scores(HP - 1)
                act.wait_ge(chosen, 1)
                nc.scalar.activation(gate[:, 0], gate[:, 0], ACT.Exp).then_inc(exped, 1)
                for a in range(4):
                    act.wait_ge(transposed, a + 1)
                    nc.scalar.activation(pairT[:, a, :], K.ps[4 + a][:, :], ACT.Copy).then_inc(pairs_copied, 1)

            @block.vector
            def _(dve):
                n = [0]

                def then(ins):
                    n[0] += 1
                    ins.then_inc(step, 1)

                def top16(values, cuts, tops, indices):
                    k = len(values)
                    dve.wait_ge(step, n[0])
                    for v, o in zip(values, tops):
                        then(nc.vector.max(o[:, 0:8], v))
                    for i, (v, o, x) in enumerate(zip(values, tops, indices)):
                        dve.wait_ge(step, n[0] - (k - 1))
                        then(nc.vector.max_index(x[:, 0:8], o[:, 0:8], v))
                    for v, o, c in zip(values, tops, cuts):
                        then(nc.vector.match_replace(c, o[:, 0:8], v, NEG))
                    for c, o in zip(cuts, tops):
                        dve.wait_ge(step, n[0] - (k - 1))
                        then(nc.vector.max(o[:, 8:16], c))
                    for c, o, x in zip(cuts, tops, indices):
                        dve.wait_ge(step, n[0] - (k - 1))
                        then(nc.vector.max_index(x[:, 8:16], o[:, 8:16], c))

                for m in range(HP):
                    dve.wait_ge(s_copied, m + 1)
                    top16([s[:, t, m, :] for t in range(TC)], [cut[:, t, m % 2, :] for t in range(TC)],
                          [top[:, t, m, :] for t in range(TC)], [topi[:, t, m, :] for t in range(TC)])
                dve.wait_ge(step, n[0])
                then(nc.vector.tensor_copy(topf[:, :, :, :], topi[:, :, :, :]))

                cand = s[:, :, :, :].rearrange("p t (h c) n -> p t h (c n)", h=PH)
                shape = [P, PH, TOPK, TOPK]
                for t in range(TC):
                    first = top[:, t, 0:HP:2, :].unsqueeze(3).to_broadcast(shape)
                    second = top[:, t, 1:HP:2, :].unsqueeze(2).to_broadcast(shape)
                    then(nc.vector.tensor_tensor(cand[:, t].rearrange("p h (a b) -> p h a b", a=TOPK), first, second,
                                                 ALU.add))
                cuts = cut[:, :, :, :].rearrange("p t a n -> p t (a n)")
                for t in range(TC):
                    for h in range(0, PH, 4):
                        top16([cand[:, t, h + e, :] for e in range(4)], [cuts[:, e, :] for e in range(4)],
                              [best[:, t, h + e, :] for e in range(4)], [pos[:, t, h + e, :] for e in range(4)])
                dve.wait_ge(step, n[0])
                bestv = best[:, :, :, :].rearrange("p t h k -> p (t h) k")
                gatev = gate[:, 0].rearrange("p t (h k) -> p (t h) k", h=PH)
                flat = [P, TC * PH, TOPK]
                nc.vector.tensor_tensor(gatev, bestv, bestv[:, :, 0:1].to_broadcast(flat), ALU.subtract).then_inc(chosen, 1)
                then(nc.vector.tensor_scalar(posab[:, 0], pos[:, :, :, :], 4, None, ALU.logical_shift_right))
                then(nc.vector.tensor_scalar(posab[:, 1], pos[:, :, :, :], TOPK - 1, None, ALU.bitwise_and))
                dve.wait_ge(step, n[0])
                then(nc.vector.tensor_copy(posf[:, :, :, :, :], posab[:, :, :, :, :]))
                dve.wait_ge(exped, 1)
                zs = zsum[:, :, :, :].rearrange("p a t h -> p a (t h)")
                then(nc.vector.tensor_reduce(zs[:, 0, :], gatev, AX.X, ALU.add))
                dve.wait_ge(step, n[0])
                then(nc.vector.reciprocal(zs[:, 1, :], zs[:, 0, :]))
                dve.wait_ge(step, n[0])
                then(nc.vector.tensor_scalar(zs[:, 1, :], zs[:, 1, :], GATE_SCALE, None, ALU.mult))
                dve.wait_ge(step, n[0])
                then(nc.vector.tensor_tensor(gatev, gatev, zs[:, 1, :].unsqueeze(2).to_broadcast(flat), ALU.mult))
                dve.wait_ge(step, n[0])
                then(nc.vector.tensor_copy(ghalf[:, :, :], gate[:, 0]))
                dve.wait_ge(step, n[0])
                then(nc.vector.tensor_tensor(gate[:, 1], gate[:, 0], ghalf[:, :, :], ALU.subtract))
                dve.wait_ge(step, n[0])
                nc.vector.tensor_copy(gate[:, 0], ghalf[:, :, :]).then_inc(ready, 1)
                nc.vector.memset(zsum[:, 0, :, :], 0.0).then_inc(ready, 1)
                iota16 = K.const("iota")[:, 0:TOPK].unsqueeze(1).unsqueeze(1).to_broadcast(shape)
                eq = cand[:, 0].rearrange("p h (a b) -> p h a b", a=TOPK)
                picked = cand[:, 1].rearrange("p h (a b) -> p h a b", a=TOPK)
                for half in range(2):
                    for t in range(TC):
                        dve.wait_ge(step, n[0])
                        then(nc.vector.tensor_tensor(eq, posf[:, half, t].unsqueeze(3).to_broadcast(shape), iota16,
                                                     ALU.is_equal))
                        dve.wait_ge(step, n[0])
                        then(nc.vector.tensor_tensor(picked, eq, topf[:, t, half:HP:2, :].unsqueeze(2).to_broadcast(shape),
                                                     ALU.mult))
                        dve.wait_ge(step, n[0])
                        ins = nc.vector.tensor_reduce(ij[:, half, t], picked, AX.X, ALU.add)
                        if t < TC - 1:
                            then(ins)
                        else:
                            ins.then_inc(ready, 1)
                            dve.wait_ge(ready, 3 + half)


def peer_gates(K, layer, tag, pairT):
    nc, io = K.nc, K.io
    F16 = mybir.dt.float16
    G = TOKENS_PER_BANK
    STEPS = P // (2 * G)
    with ExitStack() as ctx:
        iota = K.sb(ctx, tag + "iota", [P, P], F16)
        hot = K.sb(ctx, tag + "hot", [P, 2, G, 3, P], F16)
        stage = K.sb(ctx, tag + "stage", [P, 2, NK, P])
        hot_ready = K.sem(tag + "hot_ready")
        bank_done = K.sem(tag + "bank_done")
        bank_free = K.sem(tag + "bank_free")
        chunk_done = K.sem(tag + "chunk_done")
        chunk_stored = [K.sem(f"{tag}chunk_stored{i}") for i in range(2)]
        with nc.Block() as block:
            @block.vector
            def _(dve):
                nc.vector.tensor_copy(iota[:, :], K.const("iota")).then_inc(hot_ready, 1)
                dve.wait_ge(hot_ready, 1)
                with dve.Fori(0, TC * STEPS) as i:
                    for g in range(2):
                        dve.wait_ge(bank_done, 2 * i + g + 1)
                        for r in range(G):
                            t = i * (2 * G) + (g * G + r)
                            for part, (idx, by) in enumerate(((3, None), (2, 0), (2, 1))):
                                ins = nc.vector.tensor_scalar(
                                    hot[:, g, r, part, :], iota[:, :], pairT[:, idx, bass.ds(t, 1)],
                                    None if by is None else pairT[:, by, bass.ds(t, 1)], ALU.is_equal,
                                    *(() if by is None else (ALU.mult,)))
                        ins.then_inc(hot_ready, 1)

            @block.tensor
            def _(pe):
                pe.nop().then_inc(bank_done, 2)
                with pe.Fori(0, TC * STEPS) as i:
                    for g in range(2):
                        pe.wait_ge(hot_ready, 2 * i + g + 2)
                        pe.wait_ge(bank_free, 2 * i + g + 1)
                        for r in range(G):
                            nc.tensor.matmul(K.ps[g][:, r * NK:(r + 1) * NK], hot[:, g, r, 0, :], hot[:, g, r, 1, :],
                                             start=True, stop=False)
                            last = nc.tensor.matmul(K.ps[g][:, r * NK:(r + 1) * NK], hot[:, g, r, 0, :],
                                                    hot[:, g, r, 2, :], start=False, stop=True)
                        last.then_inc(bank_done, 1)

            @block.scalar
            def _(act):
                act.nop().then_inc(bank_free, 2)
                for c in range(TC):
                    if c >= 2:
                        act.wait_ge(chunk_stored[c % 2], 16 * (c // 2))
                    with act.Fori(0, STEPS) as i:
                        for g in range(2):
                            act.wait_ge(bank_done, 2 * i + (2 * STEPS * c + g + 3))
                            nc.scalar.activation(stage[:, c % 2, :, bass.ds(i * (2 * G) + g * G, G)],
                                                 K.ps[g][:, :].rearrange("p (t n) -> p n t", t=G), ACT.Copy,
                                                 scale=1.0 / GATE_SCALE).then_inc(bank_free, 1)
                    act.wait_ge(bank_free, 2 * STEPS * (c + 1) + 2)
                    act.nop().then_inc(chunk_done, 1)

            @block.sync
            def _(sp):
                for c in range(TC):
                    sp.wait_ge(chunk_done, c + 1)
                    sp.dma_start(io["gates"][:, :, c * P:(c + 1) * P].rearrange("i j t -> j i t"),
                                 stage[:, c % 2, :, :]).then_inc(chunk_stored[c % 2], 16)
                for c in range(2):
                    sp.wait_ge(chunk_stored[c], 16 * (TC // 2))


def peer_experts(K, layer, tag):
    nc, io = K.nc, K.io
    G = GROUP
    with ExitStack() as ctx:
        u = K.sb(ctx, tag + "u", [P, 2, G, DC, P])
        v = K.sb(ctx, tag + "v", [P, 2, G, D])
        w = K.sb(ctx, tag + "w", [P, 2, G, T])
        a = K.sb(ctx, tag + "a", [P, 2, G, T])
        u_loaded = [K.sem(f"{tag}u_loaded{i}") for i in range(2)]
        v_loaded = [K.sem(f"{tag}v_loaded{i}") for i in range(2)]
        w_loaded = [K.sem(f"{tag}wt_loaded{i}") for i in range(2)]
        up_done = K.sem(tag + "up_done")
        gelu_done = K.sem(tag + "gelu_done")
        gated = K.sem(tag + "gated")
        down_done = K.sem(tag + "down_done")
        added = K.sem(tag + "added")

        def over_groups(eng, step):
            step(0, 0, True, False)
            step(1, 1, False, False)
            with eng.Fori(0, GROUPS // 2 - 2) as i:
                step(2 + 2 * i, 0, False, False)
                step(3 + 2 * i, 1, False, False)
            step(GROUPS - 2, 0, False, False)
            step(GROUPS - 1, 1, False, True)

        with nc.Block() as block:
            @block.sync
            def _(sp):
                def load(n, side, first, last):
                    peeled = not isinstance(n, int)
                    if peeled or n >= 2:
                        sp.wait_ge(up_done, G * n - G)
                    rows = bass.ds(n * G, G)
                    sp.dma_start(u[:, side].rearrange("p g c e -> p g (c e)"),
                                 io["u"][layer, rows].rearrange("g p c e -> p g (c e)")).then_inc(u_loaded[side], 16)
                    if peeled or n >= 2:
                        sp.wait_ge(gated, G * n - G)
                    sp.dma_start(w[:, side], io["gates"][rows].rearrange("g j t -> j g t")).then_inc(w_loaded[side], 16)
                    if peeled or n >= 2:
                        sp.wait_ge(down_done, DC * n - DC)
                    sp.dma_start(v[:, side], io["v"][layer, rows].rearrange("g j d -> j g d")).then_inc(v_loaded[side], 16)
                over_groups(sp, load)

            @block.tensor
            def _(pe):
                def up(n, side):
                    pe.wait_ge(u_loaded[side], 8 * n + (16 - 8 * side))
                    for r in range(G):
                        if not (isinstance(n, int) and n == 0):
                            pe.wait_ge(gelu_done, G * n - G + r + 1)
                        for k in range(DC):
                            last = nc.tensor.matmul(K.ps[r][:, :], u[:, side, r, k, :], K.hc(k), start=(k == 0),
                                                    stop=(k == DC - 1))
                        last.then_inc(up_done, 1)

                def down(n, side):
                    pe.wait_ge(v_loaded[side], 8 * n + (16 - 8 * side))
                    pe.wait_ge(gated, G * n + G)
                    for c in range(DC):
                        if not (isinstance(n, int) and n == 0 and c < 4):
                            pe.wait_ge(added, DC * n + c - 3)
                        for r in range(G):
                            last = nc.tensor.matmul(K.ps[4 + c % 4][:, :], v[:, side, r, c * P:(c + 1) * P],
                                                    a[:, side, r, :], start=(r == 0), stop=(r == G - 1))
                        last.then_inc(down_done, 1)

                def both(n, side, first, last):
                    up(n, side)
                    if not first:
                        down(n - 1, 1 - side)
                    if last:
                        down(n, side)
                over_groups(pe, both)

            @block.scalar
            def _(act):
                def gelu(n, side, first, last):
                    if not isinstance(n, int) or n >= 2:
                        act.wait_ge(down_done, DC * n - DC)
                    for r in range(G):
                        act.wait_ge(up_done, G * n + r + 1)
                        nc.scalar.activation(a[:, side, r, :], K.ps[r][:, :], ACT.Gelu_apprx_tanh).then_inc(gelu_done, 1)
                over_groups(act, gelu)

            @block.vector
            def _(dve):
                def add(n):
                    for c in range(DC):
                        dve.wait_ge(down_done, DC * n + c + 1)
                        nc.vector.scalar_tensor_tensor(out=K.x[:, c, :], in0=K.ps[4 + c % 4][:, :],
                                                       scalar=K.mod[:, layer, 40 + c:41 + c], in1=K.x[:, c, :],
                                                       op0=ALU.mult, op1=ALU.add).then_inc(added, 1)

                def gate(n, side, first, last):
                    dve.wait_ge(w_loaded[side], 8 * n + (16 - 8 * side))
                    for r in range(G):
                        dve.wait_ge(gelu_done, G * n + r + 1)
                        nc.vector.tensor_tensor(a[:, side, r, :], a[:, side, r, :], w[:, side, r, :],
                                                ALU.mult).then_inc(gated, 1)
                    if not first:
                        add(n - 1)
                    if last:
                        add(n)
                over_groups(dve, gate)


DECAY = float(np.exp(-0.5))
KINDS = ("r", "k", "v", "sg0", "sg1", "a0", "a1", "g")


def stage_rwkv(K):
    rwkv_project(K)
    rwkv_mix(K)
    project_residual(K, "rw_wo", K.io["w_o"], K.hc, 1)


def project_residual(K, tag, weights, act_of, layer):
    nc = K.nc
    WR = 4
    with ExitStack() as ctx:
        wt = K.sb(ctx, tag, [P, WR, DC, P])
        loaded = [K.sem(f"{tag}_loaded{i}") for i in range(WR)]
        projected = K.sem(tag + "_projected")
        added = K.sem(tag + "_added")
        with nc.Block() as block:
            @block.sync
            def _(sp):
                for m in range(DC):
                    if m >= WR:
                        sp.wait_ge(projected, m - WR + 1)
                    sp.dma_start(wt[:, m % WR], weights[m]).then_inc(loaded[m % WR], 16)

            @block.vector
            def _(dve):
                for m in range(DC):
                    dve.wait_ge(projected, m + 1)
                    nc.vector.scalar_tensor_tensor(out=K.x[:, m, :], in0=K.ps[m % 4][:, :],
                                                   scalar=K.mod[:, layer, 16 + m:17 + m], in1=K.x[:, m, :],
                                                   op0=ALU.mult, op1=ALU.add).then_inc(added, 1)

            @block.tensor
            def _(pe):
                for m in range(DC):
                    pe.wait_ge(loaded[m % WR], 16 * (m // WR + 1))
                    if m >= 4:
                        pe.wait_ge(added, m - 3)
                    for k in range(DC):
                        last = nc.tensor.matmul(K.ps[m % 4][:, :], wt[:, m % WR, k, :], act_of(k), start=(k == 0),
                                                stop=(k == DC - 1))
                    last.then_inc(projected, 1)


def rwkv_project(K):
    nc, io = K.nc, K.io
    WR, SR = 4, 4
    MIXES = (1, 4, 5, 0, 2, 3)
    with ExitStack() as ctx:
        xx = K.sb(ctx, "rp_xx", [P, DC, T])
        xm = K.sb(ctx, "rp_xm", [P, 2, DC, T])
        wt = K.sb(ctx, "rp_wt", [P, WR, DC, P])
        hid = K.sb(ctx, "rp_hid", [P, 3, T])
        w2 = K.sb(ctx, "rp_w2", [P, 3, D])
        out = K.sb(ctx, "rp_out", [P, SR, T])
        w_loaded = [K.sem(f"rp_w_loaded{i}") for i in range(WR)]
        w2_loaded = K.sem("rp_w2_loaded")
        shifted = K.sem("rp_shifted")
        mixed = K.sem("rp_mixed")
        projected = K.sem("rp_projected")
        hid_done = K.sem("rp_hid_done")
        evacuated = K.sem("rp_evacuated")
        stored = [K.sem(f"rp_stored{i}") for i in range(SR)]
        WIDE = [(kind, c) for kind in range(3) for c in range(DC)]
        NARROW = [(kind, c) for c in range(DC) for kind in range(3, 8)]
        OUTS = WIDE + NARROW
        with nc.Block() as block:
            @block.sync
            def _(sp):
                sp.dma_start(w2[:, :, :], io["lora2"].rearrange("a p d -> p a d")).then_inc(w2_loaded, 16)
                for n in range(3 + len(WIDE)):
                    if n >= WR:
                        sp.wait_ge(projected, n - WR + 1)
                    src = io["lora1"][n] if n < 3 else io["w_rkv"][n - 3]
                    sp.dma_start(wt[:, n % WR], src).then_inc(w_loaded[n % WR], 16)

            @block.gpsimd
            def _(gp):
                for n, (kind, c) in enumerate(OUTS):
                    gp.wait_ge(evacuated, n + 1)
                    gp.dma_start(io["rwkv"][kind, c], out[:, n % SR, :]).then_inc(stored[n % SR], 16)
                for i in range(SR):
                    gp.wait_ge(stored[i], 16 * (len(OUTS) // SR))

            @block.vector
            def _(dve):
                for c in range(DC):
                    nc.vector.tensor_tensor(xx[:, c, :], K.h[:, c, 0:T], K.h[:, c, 2:T + 2], ALU.add).then_inc(shifted, 1)
                for c in range(DC):
                    dve.wait_ge(shifted, c + 1)
                    nc.vector.scalar_tensor_tensor(out=xx[:, c, :], in0=xx[:, c, :], scalar=0.5, in1=K.hc(c),
                                                   op0=ALU.mult, op1=ALU.subtract).then_inc(shifted, 1)
                for i, row in enumerate(MIXES):
                    if i >= 2:
                        dve.wait_ge(projected, i - 1 if i < 5 else 3 + DC * (i - 4))
                    for c in range(DC):
                        dve.wait_ge(shifted, DC + c + 1)
                        nc.vector.scalar_tensor_tensor(out=xm[:, i % 2, c, :], in0=xx[:, c, :],
                                                       scalar=K.col("mix", row * DC + c), in1=K.hc(c),
                                                       op0=ALU.mult, op1=ALU.add).then_inc(mixed, 1)

            @block.tensor
            def _(pe):
                for n in range(3 + len(WIDE)):
                    i = n if n < 3 else 3 + (n - 3) // DC
                    pe.wait_ge(w_loaded[n % WR], 16 * (n // WR + 1))
                    if n >= 4:
                        pe.wait_ge(hid_done, min(n - 3, 3))
                        if n >= 7:
                            pe.wait_ge(evacuated, n - 6)
                    for k in range(DC):
                        pe.wait_ge(mixed, DC * i + k + 1)
                        last = nc.tensor.matmul(K.ps[n % 4][:, :], wt[:, n % WR, k, :], xm[:, i % 2, k, :],
                                                start=(k == 0), stop=(k == DC - 1))
                    last.then_inc(projected, 1)
                pe.wait_ge(w2_loaded, 16)
                for j, (kind, c) in enumerate(NARROW):
                    n = 3 + len(WIDE) + j
                    pe.wait_ge(evacuated, n - 6)
                    which, rows = ((0, slice(0, HD)), (0, slice(HD, P)), (1, slice(0, HD)), (1, slice(HD, P)),
                                   (2, slice(0, P)))[kind - 3]
                    nc.tensor.matmul(K.ps[n % 4][:, :], w2[rows, which, c * P:(c + 1) * P], hid[rows, which, :],
                                     start=True, stop=True).then_inc(projected, 1)

            @block.scalar
            def _(act):
                for n, f in enumerate((ACT.Tanh, ACT.Copy, ACT.Sigmoid)):
                    act.wait_ge(projected, n + 1)
                    nc.scalar.activation(hid[:, n, :], K.ps[n][:, :], f).then_inc(hid_done, 1)
                for n, (kind, c) in enumerate(OUTS):
                    act.wait_ge(projected, n + 4)
                    if n >= SR:
                        act.wait_ge(stored[n % SR], 16 * (n // SR))
                    bank = K.ps[(n + 3) % 4]
                    if 3 <= kind < 7:
                        bias = K.col("w0" if kind < 5 else "a0", (kind - 3) % 2 * DC + c)
                        nc.scalar.activation(out[:, n % SR, :], bank[:, :], ACT.Sigmoid, bias=bias).then_inc(evacuated, 1)
                    else:
                        nc.scalar.activation(out[:, n % SR, :], bank[:, :], ACT.Copy).then_inc(evacuated, 1)


def rwkv_mix(K):
    nc, io = K.nc, K.io
    NLEV = LEVELS - 1
    with ExitStack() as ctx:
        sb = lambda name, shape, dt=F32: K.sb(ctx, "rm_" + name, shape, dt)
        inp = sb("in", [P, 2, 8, T])
        masks = sb("masks", [P, 2, LEVELS, P], U32)
        tri = sb("tri", [P, 4, P], U32)
        scanmask = sb("scanmask", [P, T])
        ka1 = sb("ka1", [P, DC])
        kx = sb("kx", [P, T])
        sq = sb("sq", [P, T])
        kk = sb("kk", [P, T])
        norm = sb("norm", [P, 2, T])
        cs = sb("cs", [P, 2, T])
        mid = sb("mid", [P, 2, TC])
        emid = sb("emid", [P, 2, TC])
        fac = sb("fac", [P, 2, TC - 1])
        d = sb("d", [P, 2, T])
        A = sb("A", [P, 2, T])
        B = sb("B", [P, 2, T])
        C = sb("C", [P, 2, T])
        R = sb("R", [P, 2, T])
        Eneg = sb("Eneg", [P, 2, T])
        bonus = sb("bonus", [P, T])
        tokB = sb("tokB", [P, 2, TC, P])
        tokC = sb("tokC", [P, 2, TC, P])
        tokV = sb("tokV", [P, TC, P])
        Tm = sb("T", [P, 4, 4, P])
        TT = sb("TT", [P, 4, 4, P])
        NT = sb("NT", [P, 4, 4, P])
        Pb = sb("P", [P, 4, 4, P])
        MT = sb("MT", [P, 3, 4, 4, P])
        S = sb("S", [P, 2, 2, P])
        Stmp = sb("Stmp", [P, 2, P])
        rhs = sb("rhs", [P, 2, P])
        U = sb("U", [P, 2, P])
        y = sb("y", [P, TC, P])
        yc = sb("yc", [P, TC, P])
        ysq = sb("ysq", [P, TC, P])
        stat = sb("stat", [P, 4, 2 * TC])
        ln = sb("ln", [P, T])

        sem = lambda name: K.sem("rm_" + name)
        const_loaded = sem("const_loaded")
        in_loaded = [sem("in_loaded0"), sem("in_loaded1")]
        setup = sem("setup")
        ident_ready = sem("ident_ready")
        step = sem("step")
        kx_ready = sem("kx_ready")
        kx_squared = sem("kx_squared")
        kk_summed = sem("kk_summed")
        ss_ready = sem("ss_ready")
        kn_ready = sem("kn_ready")
        d_ready = sem("d_ready")
        e_ready = sem("e_ready")
        bonus_ready = sem("bonus_ready")
        bonus_summed = sem("bonus_summed")
        factors = sem("factors")
        tok_done = sem("tok_done")
        tok_out = sem("tok_out")
        n_done = sem("n_done")
        nt_done = sem("nt_done")
        masked_done = sem("masked_done")
        nt_out = sem("nt_out")
        prod_out = sem("prod_out")
        p_done = sem("p_done")
        p_out = sem("p_out")
        q_done = sem("q_done")
        inv_out = sem("inv_out")
        s_zero = sem("s_zero")
        rhs_done = sem("rhs_done")
        rhs_out = sem("rhs_out")
        u_done = sem("u_done")
        u_out = sem("u_out")
        s_done = sem("s_done")
        s_out = sem("s_out")
        y_done = sem("y_done")
        y_out = sem("y_out")
        var_ready = sem("var_ready")
        sd_ready = sem("sd_ready")
        yn_ready = sem("yn_ready")
        yt_done = sem("yt_done")
        ln_ready = sem("ln_ready")
        waited = sem("waited")
        done = sem("done")

        INV = 8 * (NLEV - 1) + 4

        def t_out(lv, g):
            return 8 * (lv - 1) + 2 * g + 1

        def tt_out(lv, g):
            return 8 * (lv - 1) + 2 * g + 2 if lv < NLEV else 8 * (NLEV - 1) + g + 1

        def over_chunks(eng, body):
            with eng.Fori(0, DC // 2) as i:
                body(2 * i, 0)
                body(2 * i + 1, 1)

        def bc4(m):
            return m.unsqueeze(1).to_broadcast([P, 4, P])

        def bank4(i):
            return K.ps[i][:, :].rearrange("p (u t) -> p u t", u=4)

        def blocks(a, z):
            return a[:, z].rearrange("p (b t) -> p b t", b=TC)

        with nc.Block() as block:
            @block.sync
            def _(sp):
                sp.dma_start(masks[:, :, :, :], io["masks"]).then_inc(const_loaded, 16)
                sp.dma_start(tri[:, :, :], io["tri"]).then_inc(const_loaded, 16)
                sp.dma_start(scanmask[:, :], io["scanmask"]).then_inc(const_loaded, 16)

                def load(c, side):
                    sp.dma_start(inp[:, side], io["rwkv"][:, bass.ds(c, 1)].rearrange("k c p t -> p (k c) t")
                                 ).then_inc(in_loaded[side], 16)
                load(0, 0)
                load(1, 1)
                with sp.Fori(0, DC // 2 - 1) as i:
                    for side in range(2):
                        sp.wait_ge(done, 2 * i + side + 2)
                        load(2 * i + side + 2, side)

            @block.gpsimd
            def _(gp):
                gp.memset(MT[:, :, :, :, :], 0.0).then_inc(setup, 1)

                def body(c, side):
                    gp.wait_ge(done, c + 1)
                    gp.sem_inc(waited, 1)
                    ident = K.const("ident").unsqueeze(1).to_broadcast([P, 16, P])
                    for m in (Tm, TT):
                        gp.tensor_copy(m[:, :, :, :].rearrange("p g u t -> p (g u) t"), ident).then_inc(ident_ready, 1)
                over_chunks(gp, body)

            @block.vector
            def _(dve):
                dve.wait_ge(const_loaded, 48)
                dve.nop().then_inc(done, 1)
                a = COLS["k_a"][0]
                nc.vector.tensor_scalar(ka1[:, :], K.cols[:, a:a + DC], -1.0, 1.0, ALU.mult, ALU.add).then_inc(step, 1)

                def body(c, side):
                    n = [0]
                    NSTEP = 33

                    def then(ins):
                        n[0] += 1
                        ins.then_inc(step, 1)

                    def settled():
                        dve.wait_ge(step, NSTEP * c + 1 + n[0])

                    def col(name):
                        return K.cols[:, bass.ds(c + COLS[name][0], 1)]

                    r, k, v = (inp[:, side, i] for i in range(3))
                    sg, av, g = inp[:, side, 3:5], inp[:, side, 5:7], inp[:, side, 7]
                    both = [P, 2, T]

                    def twice(m):
                        return m.unsqueeze(1).to_broadcast(both)

                    dve.wait_ge(in_loaded[side], 8 * c + (16 - 8 * side))
                    settled()
                    nc.vector.tensor_scalar(kx[:, :], k, col("k_k"), None, ALU.mult).then_inc(kx_ready, 1)
                    then(nc.vector.memset(S[:, 0], 0.0))
                    for z in range(2):
                        then(nc.vector.tensor_tensor_scan(cs[:, z], scanmask[:, :], sg[:, z], 0.0, ALU.mult, ALU.add))
                    settled()
                    then(nc.vector.tensor_scalar(mid[:, :, :].unsqueeze(3), cs[:, :, :].rearrange("p z (b t) -> p z b t", b=TC)[:, :, :, P - 1:P],
                                                 0.5, None, ALU.mult))
                    settled()
                    m0, m1 = (mid[:, z, :].unsqueeze(2).to_broadcast([P, TC, P]) for z in range(2))
                    then(nc.vector.tensor_tensor(blocks(d, 0), blocks(cs, 0), m0, ALU.subtract))
                    then(nc.vector.tensor_tensor(blocks(A, 1), m1, blocks(cs, 1), ALU.subtract))
                    settled()
                    nc.vector.tensor_tensor(A[:, 0], d[:, 0], sg[:, 0], ALU.subtract).then_inc(d_ready, 1)
                    nc.vector.tensor_tensor(d[:, 1], A[:, 1], sg[:, 1], ALU.add).then_inc(d_ready, 1)
                    then(nc.vector.tensor_scalar(C[:, :, :], av, col("k_a"), ka1[:, bass.ds(c, 1)], ALU.mult, ALU.add))
                    settled()
                    then(nc.vector.tensor_tensor(C[:, :, :], C[:, :, :], twice(k), ALU.mult))
                    settled()
                    then(nc.vector.tensor_tensor(bonus[:, :], C[:, 0], C[:, 1], ALU.add))
                    settled()
                    nc.vector.scalar_tensor_tensor(out=bonus[:, :], in0=bonus[:, :], scalar=col("r_k"), in1=r,
                                                   op0=ALU.mult, op1=ALU.mult).then_inc(bonus_ready, 1)
                    dve.wait_ge(kk_summed, c + 1)
                    nc.vector.tensor_scalar(norm[:, 0], K.ps[0][:, :], 1e-24, None, ALU.max).then_inc(ss_ready, 1)
                    dve.wait_ge(kn_ready, c + 1)
                    then(nc.vector.reciprocal(norm[:, 0], norm[:, 1]))
                    settled()
                    dve.wait_ge(kx_ready, c + 1)
                    then(nc.vector.tensor_tensor(kk[:, :], kx[:, :], norm[:, 0], ALU.mult))
                    settled()
                    then(nc.vector.scalar_tensor_tensor(out=B[:, :, :], in0=av, scalar=-1.0, in1=twice(kk[:, :]),
                                                        op0=ALU.mult, op1=ALU.mult))
                    dve.wait_ge(bonus_summed, c + 1)
                    then(nc.vector.tensor_tensor(bonus[:, :], K.ps[1][:, :], v, ALU.mult))
                    dve.wait_ge(e_ready, 4 * (c + 1))
                    settled()
                    nc.vector.tensor_tensor(B[:, :, :], B[:, :, :], Eneg[:, :, :], ALU.mult).then_inc(factors, 1)
                    nc.vector.tensor_tensor(C[:, :, :], C[:, :, :], Eneg[:, :, :], ALU.mult).then_inc(factors, 1)
                    nc.vector.tensor_tensor(A[:, :, :], A[:, :, :], twice(kk[:, :]), ALU.mult).then_inc(factors, 1)
                    nc.vector.tensor_tensor(R[:, :, :], R[:, :, :], twice(r), ALU.mult).then_inc(factors, 1)
                    then(nc.vector.tensor_tensor(fac[:, :, :], emid[:, :, 0:TC - 1], emid[:, :, 1:TC], ALU.mult))

                    for g4 in range(4):
                        z = g4 // 2
                        if g4 == 0:
                            dve.wait_ge(ident_ready, 2 * c + 2)
                            dve.wait_ge(setup, 1)
                        dve.wait_ge(n_done, 4 * c + g4 + 1)
                        dve.sem_inc(waited, 1)
                        nc.vector.copy_predicated(Tm[:, g4], bc4(masks[:, z, 0, :]), bank4(g4 % 2)).then_inc(prod_out, 1)
                        dve.wait_ge(nt_out, 4 * c + g4 + 1)
                        dve.sem_inc(waited, 1)
                        nc.vector.copy_predicated(TT[:, g4], bc4(masks[:, 1 - z, 0, :]), bank4(2 + g4 % 2)).then_inc(prod_out, 1)
                        for i in range(3):
                            dve.wait_ge(masked_done, 12 * c + 3 * g4 + i + 1)
                            dve.sem_inc(waited, 1)
                            nc.vector.copy_predicated(MT[:, i, g4], bc4(tri[:, 2 * z + (i > 0), :]),
                                                      bank4(5 + i)).then_inc(prod_out, 1)
                    for lv in range(1, NLEV + 1):
                        for g4 in range(4):
                            z = g4 // 2
                            dve.wait_ge(q_done, 4 * NLEV * c + 4 * (lv - 1) + g4 + 1)
                            if lv < NLEV:
                                dve.sem_inc(waited, 1)
                                nc.vector.copy_predicated(Tm[:, g4], bc4(masks[:, z, lv, :]),
                                                          bank4(2 + g4 % 2)).then_inc(inv_out, 1)
                            dve.sem_inc(waited, 1)
                            nc.vector.copy_predicated(TT[:, g4], bc4(masks[:, 1 - z, lv, :]),
                                                      bank4(4 + g4 % 2)).then_inc(inv_out, 1)
                    for b in range(TC):
                        for z in range(2):
                            if b == TC - 1:
                                break
                            j = b if z == 0 else TC - 2 - b
                            dve.wait_ge(s_done, 6 * c + 2 * b + z + 1)
                            if b:
                                dve.wait_ge(s_out, 6 * c + 2 * (b - 1) + z + 1)
                            then(nc.vector.tensor_tensor(Stmp[:, z], K.ps[6 + z][:, 0:P], S[:, b % 2, z], ALU.add))
                            settled()
                            nc.vector.scalar_tensor_tensor(out=S[:, 1 - b % 2, z], in0=Stmp[:, z], scalar=fac[:, z, j:j + 1],
                                                           in1=K.const("blockdiag"), op0=ALU.mult,
                                                           op1=ALU.mult).then_inc(s_out, 1)
                        for z in range(2):
                            blk = b if z == 0 else TC - 1 - b
                            dve.wait_ge(y_done, 8 * c + 2 * b + z + 1)
                            if b < 2:
                                nc.vector.tensor_copy(y[:, blk, :], K.ps[4 + z][:, 0:P]).then_inc(y_out, 1)
                            else:
                                dve.wait_ge(y_out, 8 * c + 2 * b + z)
                                nc.vector.tensor_tensor(y[:, blk, :], K.ps[4 + z][:, 0:P], y[:, blk, :],
                                                        ALU.add).then_inc(y_out, 1)
                    dve.wait_ge(y_out, 8 * (c + 1))
                    heads = [P, 2 * TC, HD]
                    yv, ycv, ysv = (m[:, :, :].rearrange("p b (h v) -> p (b h) v", h=2) for m in (y, yc, ysq))
                    then(nc.vector.tensor_reduce(stat[:, 0], yv, AX.X, ALU.add))
                    settled()
                    then(nc.vector.tensor_scalar(stat[:, 1], stat[:, 0], 1.0 / HD, None, ALU.mult))
                    settled()
                    then(nc.vector.tensor_tensor(ycv, yv, stat[:, 1].unsqueeze(2).to_broadcast(heads), ALU.subtract))
                    settled()
                    then(nc.vector.tensor_tensor(ysv, ycv, ycv, ALU.mult))
                    settled()
                    nc.vector.tensor_reduce(stat[:, 2], ysv, AX.X, ALU.add).then_inc(var_ready, 1)
                    dve.wait_ge(sd_ready, c + 1)
                    then(nc.vector.reciprocal(stat[:, 0], stat[:, 3]))
                    settled()
                    nc.vector.tensor_tensor(yv, ycv, stat[:, 0].unsqueeze(2).to_broadcast(heads),
                                            ALU.mult).then_inc(yn_ready, 1)
                    dve.wait_ge(ln_ready, c + 1)
                    then(nc.vector.tensor_tensor(ln[:, :], ln[:, :], bonus[:, :], ALU.add))
                    settled()
                    then(nc.vector.tensor_tensor(K.h[:, bass.ds(c, 1), 1:T + 1], ln[:, :].unsqueeze(1), g.unsqueeze(1), ALU.mult))
                    settled()
                    assert n[0] + 1 <= NSTEP, n[0]
                    while n[0] < NSTEP - 1:
                        n[0] += 1
                        dve.nop().then_inc(step, 1)
                    dve.nop().then_inc(done, 1)
                    dve.nop().then_inc(step, 1)
                over_chunks(dve, body)

            @block.scalar
            def _(act):
                def body(c, side):
                    act.wait_ge(kx_ready, c + 1)
                    nc.scalar.activation(sq[:, :], kx[:, :], ACT.Square).then_inc(kx_squared, 1)
                    act.wait_ge(ss_ready, c + 1)
                    nc.scalar.activation(norm[:, 1], norm[:, 0], ACT.Sqrt).then_inc(kn_ready, 1)
                    act.wait_ge(d_ready, 2 * c + 2)
                    nc.scalar.activation(R[:, :, :], d[:, :, :], ACT.Exp, scale=-DECAY).then_inc(e_ready, 1)
                    nc.scalar.activation(Eneg[:, :, :], d[:, :, :], ACT.Exp, scale=DECAY).then_inc(e_ready, 1)
                    nc.scalar.activation(A[:, :, :], A[:, :, :], ACT.Exp, scale=-DECAY).then_inc(e_ready, 1)
                    nc.scalar.activation(emid[:, :, :], mid[:, :, :], ACT.Exp, scale=-DECAY).then_inc(e_ready, 1)
                    for i, dst in enumerate((tokB[:, 0], tokB[:, 1], tokC[:, 0], tokC[:, 1], tokV[:, :, :])):
                        act.wait_ge(tok_done, 5 * c + i + 1)
                        nc.scalar.activation(dst, bank4(2 + i), ACT.Copy).then_inc(tok_out, 1)
                    for g4 in range(4):
                        act.wait_ge(nt_done, 4 * c + g4 + 1)
                        nc.scalar.activation(NT[:, g4], bank4(2 + g4 % 2), ACT.Copy).then_inc(nt_out, 1)
                    for lv in range(1, NLEV + 1):
                        for g4 in range(4):
                            act.wait_ge(p_done, 4 * NLEV * c + 4 * (lv - 1) + g4 + 1)
                            nc.scalar.activation(Pb[:, g4], bank4(g4 % 2), ACT.Copy).then_inc(p_out, 1)
                    for b in range(TC):
                        for z in range(2):
                            act.wait_ge(rhs_done, 8 * c + 2 * b + z + 1)
                            nc.scalar.activation(rhs[:, z], K.ps[z][:, 0:P], ACT.Copy).then_inc(rhs_out, 1)
                        for z in range(2):
                            act.wait_ge(u_done, 8 * c + 2 * b + z + 1)
                            nc.scalar.activation(U[:, z], K.ps[2 + z][:, 0:P], ACT.Copy).then_inc(u_out, 1)
                    act.wait_ge(var_ready, c + 1)
                    nc.scalar.activation(stat[:, 3], stat[:, 2], ACT.Sqrt, bias=K.eps[:, 1:2],
                                         scale=1.0 / HD).then_inc(sd_ready, 1)
                    act.wait_ge(yt_done, c + 1)
                    nc.scalar.activation(ln[:, :], K.ps[0][:, :], ACT.Identity,
                                         bias=K.cols[:, bass.ds(c + COLS["ln_b"][0], 1)],
                                         scale=K.cols[:, bass.ds(c + COLS["ln_g"][0], 1)]).then_inc(ln_ready, 1)
                over_chunks(act, body)

            @block.tensor
            def _(pe):
                def four(bank, lhsT, rhs_, sem_):
                    for u in range(4):
                        last = nc.tensor.matmul(K.ps[bank][:, u * P:(u + 1) * P], lhsT(u), rhs_(u), start=True, stop=True)
                    last.then_inc(sem_, 1)

                def body(c, side):
                    pe.wait_ge(kx_squared, c + 1)
                    nc.tensor.matmul(K.ps[0][:, :], K.const("ones_sum"), sq[:, :], start=True, stop=True).then_inc(kk_summed, 1)
                    pe.wait_ge(bonus_ready, c + 1)
                    nc.tensor.matmul(K.ps[1][:, :], K.const("ones_sum"), bonus[:, :], start=True,
                                     stop=True).then_inc(bonus_summed, 1)
                    pe.wait_ge(factors, 4 * (c + 1))
                    for i, src in enumerate((B[:, 0], B[:, 1], C[:, 0], C[:, 1], inp[:, side, 2])):
                        for b in range(TC):
                            last = nc.tensor.transpose(K.ps[2 + i][:, b * P:(b + 1) * P], src[:, b * P:(b + 1) * P],
                                                       K.const("ident"))
                        last.then_inc(tok_done, 1)
                    for g4 in range(4):
                        z = g4 // 2

                        def part(m):
                            def at(u):
                                return m[HD * (g4 % 2):HD * (g4 % 2 + 1), z, u * P:(u + 1) * P]
                            return at
                        if g4 >= 2:
                            pe.wait_ge(prod_out, 20 * c + 5 * (g4 - 2) + 1)
                        four(g4 % 2, part(A), part(B), n_done)
                        pe.wait_ge(tok_out, 5 * c + 2)
                        if g4 >= 2:
                            pe.wait_ge(prod_out, 20 * c + 5 * (g4 - 2) + 2)
                            pe.wait_ge(nt_out, 4 * c + g4 - 1)
                        four(2 + g4 % 2, part(B), part(A), nt_done)
                        pe.wait_ge(tok_out, 5 * c + 5)
                        for i, (left, right) in enumerate(((C, A), (B, R), (C, R))):
                            if g4:
                                pe.wait_ge(prod_out, 20 * c + 5 * (g4 - 1) + 3 + i)
                            four(5 + i, part(left), part(right), masked_done)

                    pe.wait_ge(prod_out, 20 * c + 20)
                    pe.wait_ge(nt_out, 4 * c + 4)

                    def double_p(lv, g4):
                        p = 4 * (lv - 1) + g4
                        if lv > 1:
                            pe.wait_ge(inv_out, INV * c + t_out(lv - 1, g4))
                        if p >= 2:
                            pe.wait_ge(p_out, 4 * NLEV * c + p - 1)
                        four(g4 % 2, lambda u: NT[:, g4, u, :], lambda u: Tm[:, g4, u, :], p_done)

                    def double_q(lv, g4):
                        p = 4 * (lv - 1) + g4
                        pe.wait_ge(p_out, 4 * NLEV * c + p + 1)
                        if lv > 1:
                            pe.wait_ge(inv_out, INV * c + tt_out(lv - 1, g4))
                        if p >= 2:
                            prev = p - 2
                            pe.wait_ge(inv_out, INV * c + tt_out(prev // 4 + 1, prev % 4))
                        if lv < NLEV:
                            for u in range(4):
                                nc.tensor.matmul(K.ps[2 + g4 % 2][:, u * P:(u + 1) * P], TT[:, g4, u, :], Pb[:, g4, u, :],
                                                 start=True, stop=True)
                        four(4 + g4 % 2, lambda u: Pb[:, g4, u, :], lambda u: TT[:, g4, u, :], q_done)

                    for lv in range(1, NLEV + 1):
                        double_p(lv, 0)
                        double_p(lv, 1)
                        double_q(lv, 0)
                        double_p(lv, 2)
                        double_q(lv, 1)
                        double_p(lv, 3)
                        double_q(lv, 2)
                        double_q(lv, 3)

                    pe.wait_ge(inv_out, INV * (c + 1))
                    for b in range(TC):
                        blk = (b, TC - 1 - b)
                        at = [slice(k_ * P, (k_ + 1) * P) for k_ in blk]

                        def mt(i, z, h):
                            return MT[:, i, 2 * z + h, blk[z], :]
                        for z in range(2):
                            if b:
                                pe.wait_ge(s_out, 6 * c + 2 * (b - 1) + z + 1)
                            for h in range(2):
                                cols = slice(h * HD, (h + 1) * HD)
                                nc.tensor.matmul(K.ps[z][:, cols], A[:, z, at[z]], S[:, b % 2, z, cols], start=True, stop=False)
                                last = nc.tensor.matmul(K.ps[z][:, cols], mt(0, z, h), tokV[:, blk[z], cols],
                                                        start=False, stop=True)
                            last.then_inc(rhs_done, 1)
                        for z in range(2):
                            pe.wait_ge(rhs_out, 8 * c + 2 * b + z + 1)
                            for h in range(2):
                                cols = slice(h * HD, (h + 1) * HD)
                                last = nc.tensor.matmul(K.ps[2 + z][:, cols], TT[:, 2 * z + h, blk[z], :],
                                                        rhs[:, z, cols], start=True, stop=True)
                            last.then_inc(u_done, 1)
                        for z in range(2):
                            pe.wait_ge(u_out, 8 * c + 2 * b + z + 1)
                            if b < TC - 1:
                                nc.tensor.matmul(K.ps[6 + z][:, 0:P], tokB[:, z, blk[z], :], U[:, z], start=True, stop=False)
                                nc.tensor.matmul(K.ps[6 + z][:, 0:P], tokC[:, z, blk[z], :], tokV[:, blk[z], :],
                                                 start=False, stop=True).then_inc(s_done, 1)
                            if b:
                                pe.wait_ge(y_out, 8 * c + 2 * (b - 1) + z + 1)
                            for h in range(2):
                                cols = slice(h * HD, (h + 1) * HD)
                                nc.tensor.matmul(K.ps[4 + z][:, cols], R[:, z, at[z]], S[:, b % 2, z, cols], start=True, stop=False)
                                nc.tensor.matmul(K.ps[4 + z][:, cols], mt(1, z, h), U[:, z, cols], start=False, stop=False)
                                last = nc.tensor.matmul(K.ps[4 + z][:, cols], mt(2, z, h), tokV[:, blk[z], cols],
                                                        start=False, stop=True)
                            last.then_inc(y_done, 1)
                    pe.wait_ge(yn_ready, c + 1)
                    for b in range(TC):
                        last = nc.tensor.transpose(K.ps[0][:, b * P:(b + 1) * P], y[:, b, :], K.const("ident"))
                    last.then_inc(yt_done, 1)
                over_chunks(pe, body)




def build(nc, io, only=None):
    with ExitStack() as ctx:
        rel = nc.dram_tensor("rel_rows", (MAPS, REL_W), F32, kind="Internal").ap()
        io["rel_scratch"] = rel
        io["rel_toeplitz"] = bass.AP(tensor=rel.tensor, offset=rel.offset, ap=[[1, P], [REL_W, MAPS], [1, TOEP_W]])
        io["gates"] = nc.dram_tensor("gates", (NK, NK, T), F32, kind="Internal").ap()
        io["rwkv"] = nc.dram_tensor("rwkv_proj", (8, DC, P, T), F32, kind="Internal").ap()
        K = Kernel(nc, io, ctx)
        stage_modulation(K)
        K.end_stage()
        stages = (("norm00", lambda: stage_norm(K, 0, 0)), ("attn", lambda: stage_attention(K)),
                  ("norm01", lambda: stage_norm(K, 0, 1)), ("peer0", lambda: stage_peer(K, 0)),
                  ("norm10", lambda: stage_norm(K, 1, 0)), ("rwkv", lambda: stage_rwkv(K)),
                  ("norm11", lambda: stage_norm(K, 1, 1)), ("peer1", lambda: stage_peer(K, 1)))
        for name, stage in stages:
            if only is None or name in only:
                stage()
                K.end_stage()
        stage_output(K)


def tiles_of(w):
    k, m = w.shape
    return w.reshape(k // P, P, m // P, P).transpose(2, 1, 0, 3)


def columns(v):
    return np.asarray(v).reshape(-1, P).T


def layout(inputs):
    i = {k: np.asarray(v) for k, v in inputs.items()}
    a = {}
    a["xT"] = i["x"][0].T.reshape(DC, P, T).transpose(1, 0, 2)
    a["ada_w"] = i["ada_w"]
    qk = i["attn_qk_g"][0]
    gcol = np.stack([np.concatenate([qk[n], qk[n]]) for n in [0] * 4 + [1] * 4 + [2] * 4 + [3]], 1)
    cols = np.zeros((P, NCOLS), np.float32)
    for name, v in (("c", columns(i["c"])), ("ada_b", columns(i["ada_b"])), ("norm_g", columns(i["norm_g"])),
                    ("qk_g", gcol), ("subln_g", columns(i["diff_subln_g"])), ("mix", columns(i["rwkv_mix"])),
                    ("w0", columns(i["rwkv_w0"])), ("a0", columns(i["rwkv_a0"])), ("k_k", columns(i["rwkv_k_k"])),
                    ("k_a", columns(i["rwkv_k_a"])), ("r_k", columns(i["rwkv_r_k"])),
                    ("ln_g", columns(i["rwkv_ln_g"])), ("ln_b", columns(i["rwkv_ln_b"]))):
        cols[:, COLS[name][0]:COLS[name][1]] = v
    a["cols"] = cols
    a["consts"] = host_constants()
    w = i["attn_w_in"][0]
    qb = w[:, 1536:2048].reshape(D, 2, 4, HD).transpose(0, 2, 1, 3).reshape(D, 512)
    a["w_in"] = tiles_of(np.concatenate([w[:, 0:1024], qb, w[:, 2048:2176], w[:, 1024:1536], w[:, 2176:2304]], 1))
    wo = i["attn_w_out"][0]
    a["w_out"] = tiles_of(np.concatenate([wo[:512], wo[512:].reshape(2, 4, HD, D).transpose(1, 0, 2, 3).reshape(512, D)]))
    a["lam"] = i["diff_lambda"][0].reshape(1, 4 * HD)
    a["rel_bias"] = i["rel_bias"]
    a["bucket"] = host_bucket_onehot()
    a["w_rkv"] = np.concatenate([tiles_of(i["rwkv_w_rkv"][0, n]) for n in range(3)])
    a["w_o"] = tiles_of(i["rwkv_w_o"][0])
    a["lora1"] = np.concatenate([tiles_of(np.concatenate([i["rwkv_w1"][0, 0], i["rwkv_w1"][0, 1]], 1)),
                                 tiles_of(np.concatenate([i["rwkv_a1"][0, 0], i["rwkv_a1"][0, 1]], 1)),
                                 tiles_of(i["rwkv_g1"][0])])
    a["lora2"] = np.stack([i["rwkv_w2"][0].reshape(P, D), i["rwkv_a2"][0].reshape(P, D), i["rwkv_g2"][0]])
    n = np.arange(P)
    up, up_incl = n[:, None] < n[None], n[:, None] <= n[None]
    a["tri"] = np.stack([up, up_incl, up.T, up_incl.T], 1).astype(np.uint32)
    a["scanmask"] = np.tile((np.arange(T) % P != 0).astype(np.float32), (P, 1))
    a["masks"] = host_level_masks()
    a["w_q"] = np.stack([tiles_of(i["peer_w_q"][l]) for l in range(DEPTH)])
    a["subkeys"] = i["peer_subkeys"].transpose(0, 4, 1, 2, 3).reshape(DEPTH, P, HP * NK)
    a["u"] = i["peer_u"].reshape(DEPTH, NK, NK, DC, P).transpose(0, 1, 4, 3, 2)
    a["v"] = i["peer_v"].reshape(DEPTH, NK, NK, D)
    return {k: np.ascontiguousarray(v) for k, v in a.items()}


def kernel(**inputs):
    import concourse.bacc as bacc
    from concourse.bass_utils import run_bass_kernel_spmd

    arrays = layout(inputs)
    nc = bacc.Bacc("TRN2", target_bir_lowering=False, num_devices=1)
    io = {k: nc.dram_tensor("in_" + k, v.shape, mybir.dt.from_np(v.dtype), kind="ExternalInput").ap()
          for k, v in arrays.items()}
    io["outT"] = nc.dram_tensor("out_T", (P, DC, T), F32, kind="ExternalOutput").ap()
    build(nc, io)
    r = run_bass_kernel_spmd(nc, [{"in_" + k: v for k, v in arrays.items()}], core_ids=[0])
    out = r.results[0]["out_T"]
    return np.ascontiguousarray(out.transpose(1, 0, 2).reshape(D, T).T)[None]
```

```python
from contextlib import ExitStack

import concourse.bass as bass
import numpy as np
from concourse import mybir

F32 = mybir.dt.float32
F32R = mybir.dt.float32r
F16 = mybir.dt.float16
U32 = mybir.dt.uint32
ALU = mybir.AluOpType
ACT = mybir.ActivationFunctionType
AX = mybir.AxisListType

P = 128
D = 1024
T = 512
DC = D // P
TC = T // P
DEPTH = 2
EPS = 1e-6

HD = 64
QKV_CHUNKS = 18
QK_CHUNKS = 13
ROPE_FIRST = 8
REL_BUCKETS = 32
MAPS = 8
REL_W = 1024
TOEP_W = T + (TC - 1) * P
LAMBDA_INIT = 0.2

PH = 8
HP = 2 * PH
NK = 128
TOPK = 16
NEG = -3.0e38
GROUP = 2
GROUPS = NK // GROUP

COLS = {}
_n = 0
for _name, _w in (("c", 8), ("ada_b", 96), ("norm_g", 32), ("qk_g", QK_CHUNKS), ("subln_g", 1),
                  ("mix", 48), ("w0", 16), ("a0", 16), ("k_k", 8), ("k_a", 8), ("r_k", 8),
                  ("ln_g", 8), ("ln_b", 8)):
    COLS[_name] = (_n, _n + _w)
    _n += _w
NCOLS = _n

CONSTS = {}
_n = 0
for _name, _w in (("ident", P), ("ones_d", P), ("ones_head", P), ("ones_v", P), ("ones_sum", P), ("anti", P),
                  ("rot", P), ("cos", T), ("sin", T), ("iota", P), ("lower", P), ("upper", P),
                  ("lower_incl", P), ("upper_incl", P), ("blockdiag", P)):
    CONSTS[_name] = (_n, _n + _w)
    _n += _w
NCONST = _n

LEVELS = 7


def host_constants():
    c = np.zeros((P, NCONST), np.float32)

    def put(name, a):
        c[:, CONSTS[name][0]:CONSTS[name][1]] = a

    i = np.arange(P)
    put("ident", np.eye(P))
    put("ones_d", np.full((P, P), 1.0 / D))
    put("ones_head", (i[:, None] // HD == i[None] // HD) / HD)
    put("ones_v", np.full((P, P), 1.0 / P))
    put("ones_sum", i[:, None] // HD == i[None] // HD)
    put("anti", np.eye(P)[::-1])
    rot = np.zeros((P, P))
    for m in range(P):
        if m % 32 < 16:
            rot[m + 16, m] = -1.0
        else:
            rot[m - 16, m] = 1.0
    put("rot", rot)
    inv = 10000.0 ** (-np.arange(0, 32, 2, dtype=np.float32) / 32)
    t = np.arange(T)
    pos = np.where((i % HD < 32)[:, None], (t // 64)[None], (t % 64)[None]).astype(np.float32)
    ang = pos * inv[i % 16][:, None].astype(np.float32)
    put("cos", np.cos(ang))
    put("sin", np.sin(ang))
    put("iota", np.tile(i, (P, 1)))
    put("lower", i[:, None] > i[None])
    put("upper", i[:, None] < i[None])
    put("lower_incl", i[:, None] >= i[None])
    put("upper_incl", i[:, None] <= i[None])
    put("blockdiag", i[:, None] // HD == i[None] // HD)
    return c


def host_level_masks():
    i = np.arange(P)
    out = np.zeros((P, 2, LEVELS, P), np.uint32)
    for lv in range(LEVELS):
        b = i >> lv
        m = (b[:, None] % 2 == 1) & (b[:, None] - 1 == b[None])
        out[:, 0, lv] = m
        out[:, 1, lv] = m.T
    return out


def host_bucket_onehot():
    rel = np.arange(-(T - 1), T)
    nb, me = REL_BUCKETS // 2, REL_BUCKETS // 4
    n = np.abs(rel)
    nf = np.maximum(n, 1).astype(np.float32)
    large = me + (np.log(nf / np.float32(me)) / np.float32(np.log(128 / me)) * np.float32(nb - me)).astype(np.int32)
    bucket = np.where(rel > 0, nb, 0) + np.where(n < me, n, np.minimum(large, nb - 1))
    out = np.zeros((REL_BUCKETS, REL_W), np.float32)
    out[bucket, np.arange(2 * T - 1)] = 1.0
    return out


class Kernel:

    def __init__(self, nc, io, ctx):
        self.nc, self.io, self.ctx = nc, io, ctx
        self.stage_sems = []
        self.x = self.sb(ctx, "x", [P, DC, T])
        self.h = self.sb(ctx, "h", [P, DC, T + 2])
        self.cols = self.sb(ctx, "cols", [P, NCOLS])
        self.consts = self.sb(ctx, "consts", [P, NCONST])
        self.mod = self.sb(ctx, "mod", [P, DEPTH, 48])
        self.scale = self.sb(ctx, "scale", [P, DEPTH, 2, DC])
        self.eps = self.sb(ctx, "eps", [P, 4])
        self.cs = self.sb(ctx, "cs", [P, DC])
        self.ones = self.sb(ctx, "ones_col", [P, 1])
        self.ps = [ctx.enter_context(nc.psum_tensor(f"bank{i}", [P, T], F32)) for i in range(8)]

    def sb(self, ctx, name, shape, dt=F32):
        return ctx.enter_context(self.nc.sbuf_tensor(name, shape, dt))

    def sem(self, name):
        handle = self.nc.alloc_semaphore(name)
        self.stage_sems.append(handle)
        return handle

    def end_stage(self):
        self.nc.clear_and_free_semaphores(self.stage_sems)
        self.nc.all_engine_barrier()
        self.stage_sems = []

    def col(self, name, i):
        a = COLS[name][0] + i
        return self.cols[:, a:a + 1]

    def const(self, name):
        return self.consts[:, CONSTS[name][0]:CONSTS[name][1]]

    def hc(self, c):
        return self.h[:, c, 1:T + 1]


def sum_modulation(K, acc, summed):
    for j in range(48):
        last = K.nc.tensor.matmul(K.ps[0][:, j:j + 1], acc[:, j * P:(j + 1) * P], K.ones[:, :], start=True, stop=True)
    last.then_inc(summed, 1)


def finish_modulation(K, dve, layer, summed, mod_done):
    nc = K.nc
    b = COLS["ada_b"][0] + 48 * layer
    dve.wait_ge(summed, 1)
    nc.vector.tensor_tensor(K.mod[:, layer, :], K.ps[0][:, 0:48], K.cols[:, b:b + 48], ALU.add).then_inc(mod_done, 1)
    dve.wait_ge(mod_done, 1)
    for s in range(2):
        g = COLS["norm_g"][0] + (2 * layer + s) * DC
        nc.vector.scalar_tensor_tensor(out=K.scale[:, layer, s, :], in0=K.mod[:, layer, 8 + 24 * s:16 + 24 * s],
                                       scalar=1.0, in1=K.cols[:, g:g + DC], op0=ALU.add,
                                       op1=ALU.mult).then_inc(mod_done, 1)


def stage_modulation(K):
    nc, io = K.nc, K.io
    RING, W = 3, 3072
    with ExitStack() as ctx:
        ring = K.sb(ctx, "ada_ring", [P, RING, W])
        acc = K.sb(ctx, "ada_acc", [P, 2 * W])
        sig = K.sb(ctx, "cs_sigmoid", [P, DC])
        loaded = [K.sem(f"ada_loaded{i}") for i in range(RING)]
        cols_loaded = K.sem("cols_loaded")
        in_loaded = K.sem("inputs_loaded")
        sig_done = K.sem("cs_sigmoid_done")
        cs_done = K.sem("cs_done")
        accumulated = K.sem("ada_accumulated")
        summed = K.sem("ada_summed")
        mod_done = K.sem("mod_done")
        tiles = [(k, hf) for k in range(DC) for hf in range(2)]
        with nc.Block() as block:
            @block.sync
            def _(sp):
                sp.dma_start(K.cols[:, :], io["cols"]).then_inc(cols_loaded, 16)
                for i, (k, hf) in enumerate(tiles):
                    if i >= RING:
                        sp.wait_ge(accumulated, i - RING + 1)
                    sp.dma_start(ring[:, i % RING, :],
                                 io["ada_w"][0, k * P:(k + 1) * P, hf * W:(hf + 1) * W]).then_inc(loaded[i % RING], 16)
                sp.dma_start(K.x[:, :, :], io["xT"]).then_inc(in_loaded, 16)
                sp.dma_start(K.consts[:, :], io["consts"]).then_inc(in_loaded, 16)
                sp.wait_ge(in_loaded, 32)

            @block.scalar
            def _(act):
                act.wait_ge(cols_loaded, 16)
                nc.scalar.activation(sig[:, :], K.cols[:, COLS["c"][0]:COLS["c"][1]], ACT.Sigmoid).then_inc(sig_done, 1)

            @block.vector
            def _(dve):
                nc.vector.memset(K.ones[:, :], 1.0).then_inc(cs_done, 1)
                nc.vector.memset(K.eps[:, 0:1], EPS).then_inc(cs_done, 1)
                nc.vector.memset(K.eps[:, 1:2], 64e-5).then_inc(cs_done, 1)
                nc.vector.memset(K.h[:, :, :], 0.0).then_inc(cs_done, 1)
                dve.wait_ge(sig_done, 1)
                nc.vector.tensor_tensor(K.cs[:, :], sig[:, :], K.cols[:, COLS["c"][0]:COLS["c"][1]],
                                        ALU.mult).then_inc(cs_done, 1)
                dve.wait_ge(cs_done, 5)
                for i, (k, hf) in enumerate(tiles):
                    half = acc[:, hf * W:(hf + 1) * W]
                    dve.wait_ge(loaded[i % RING], 16 * (i // RING + 1))
                    if k == 0:
                        nc.vector.tensor_scalar(half, ring[:, i % RING, :], K.cs[:, k:k + 1], None,
                                                ALU.mult).then_inc(accumulated, 1)
                    else:
                        dve.wait_ge(accumulated, i - 1)
                        nc.vector.scalar_tensor_tensor(out=half, in0=ring[:, i % RING, :], scalar=K.cs[:, k:k + 1],
                                                       in1=half, op0=ALU.mult, op1=ALU.add).then_inc(accumulated, 1)
                finish_modulation(K, dve, 0, summed, mod_done)

            @block.tensor
            def _(pe):
                pe.wait_ge(cs_done, 5)
                pe.wait_ge(accumulated, len(tiles))
                sum_modulation(K, acc, summed)


def stage_norm(K, layer, sub):
    nc = K.nc
    tag = f"n{layer}{sub}_"
    with ExitStack() as ctx:
        sq = K.sb(ctx, tag + "sq", [P, DC, T])
        std = K.sb(ctx, tag + "std", [P, T])
        rstd = K.sb(ctx, tag + "rstd", [P, T])
        squared = K.sem(tag + "squared")
        mean_done = K.sem(tag + "mean_done")
        std_done = K.sem(tag + "std_done")
        rstd_done = K.sem(tag + "rstd_done")
        scaled = K.sem(tag + "scaled")
        shifted = K.sem(tag + "shifted")
        with nc.Block() as block:
            @block.scalar
            def _(act):
                for c in range(DC):
                    nc.scalar.activation(sq[:, c, :], K.x[:, c, :], ACT.Square).then_inc(squared, 1)
                act.wait_ge(mean_done, 1)
                nc.scalar.activation(std[:, :], K.ps[0][:, :], ACT.Sqrt, bias=K.eps[:, 0:1]).then_inc(std_done, 1)
                for c in range(DC):
                    act.wait_ge(scaled, c + 1)
                    nc.scalar.activation(K.hc(c), K.hc(c), ACT.Identity,
                                         bias=K.mod[:, layer, 24 * sub + c:24 * sub + c + 1]).then_inc(shifted, 1)

            @block.tensor
            def _(pe):
                for c in range(DC):
                    pe.wait_ge(squared, c + 1)
                    last = nc.tensor.matmul(K.ps[0][:, :], K.const("ones_d"), sq[:, c, :], start=(c == 0),
                                            stop=(c == DC - 1))
                last.then_inc(mean_done, 1)

            @block.vector
            def _(dve):
                dve.wait_ge(std_done, 1)
                nc.vector.reciprocal(rstd[:, :], std[:, :]).then_inc(rstd_done, 1)
                dve.wait_ge(rstd_done, 1)
                for c in range(DC):
                    nc.vector.scalar_tensor_tensor(out=K.hc(c), in0=K.x[:, c, :],
                                                   scalar=K.scale[:, layer, sub, c:c + 1], in1=rstd[:, :],
                                                   op0=ALU.mult, op1=ALU.mult).then_inc(scaled, 1)


def stage_output(K):
    with ExitStack() as ctx:
        out_written = K.sem("out_written")
        with K.nc.Block() as block:
            @block.sync
            def _(sp):
                sp.dma_start(K.io["outT"], K.x[:, :, :]).then_inc(out_written, 16)
                sp.wait_ge(out_written, 16)


def stage_attention(K):
    nc, io = K.nc, K.io
    WR = 4
    UNITS = [(kind, a, qb) for kind in "AB" for a in range(4) for qb in range(TC)]
    with ExitStack() as ctx:
        wt = K.sb(ctx, "at_wt", [P, WR, DC, P])
        qkv = K.sb(ctx, "at_qkv", [P, QKV_CHUNKS, T])
        vtok = K.sb(ctx, "at_vtok", [P, TC, 4, P])
        vpad = K.sb(ctx, "at_vpad", [P, TC, 2, P])
        heads = K.sb(ctx, "at_heads", [P, DC, T])
        toep = K.sb(ctx, "at_toep", [P, MAPS, TOEP_W])
        sq = K.sb(ctx, "at_sq", [P, 2, T])
        std = K.sb(ctx, "at_std", [P, 2, T])
        rstd = K.sb(ctx, "at_rstd", [P, 2, T])
        rtmp = K.sb(ctx, "at_rtmp", [P, 2, T])
        bucket = K.sb(ctx, "at_bucket", [REL_BUCKETS, REL_W])
        relb = K.sb(ctx, "at_relb", [REL_BUCKETS, MAPS])
        relrow = K.sb(ctx, "at_relrow", [MAPS, REL_W])
        lam_in = K.sb(ctx, "at_lam_in", [P, 4, HD])
        lam_p = K.sb(ctx, "at_lam_p", [P, 2, HD])
        lam_s = K.sb(ctx, "at_lam_s", [P, 8])
        gq = K.sb(ctx, "at_gq", [P, QK_CHUNKS])
        subg = K.sb(ctx, "at_subg", [P, 1])
        prob = K.sb(ctx, "at_prob", [P, 2, 2, T])
        probT = K.sb(ctx, "at_probT", [P, 2, 2, TC, P])
        nmax = K.sb(ctx, "at_nmax", [P, 2, 2])
        esum = K.sb(ctx, "at_esum", [P, 2, 2])
        rinv = K.sb(ctx, "at_rinv", [P, 2, 2])
        rlam = K.sb(ctx, "at_rlam", [P, 2])

        w_loaded = [K.sem(f"at_w_loaded{i}") for i in range(WR)]
        small_loaded = K.sem("at_small_loaded")
        rel_done = K.sem("at_rel_done")
        relrow_done = K.sem("at_relrow_done")
        relrow_stored = K.sem("at_relrow_stored")
        toep_loaded = K.sem("at_toep_loaded")
        prepared = K.sem("at_prepared")
        lam_exp = K.sem("at_lam_exp")
        projected = K.sem("at_projected")
        raw_copied = K.sem("at_raw_copied")
        squared = K.sem("at_squared")
        meaned = K.sem("at_meaned")
        std_done = K.sem("at_std_done")
        rstd_done = K.sem("at_rstd_done")
        normed = K.sem("at_normed")
        rotated = K.sem("at_rotated")
        roped = K.sem("at_roped")
        rope_step = K.sem("at_rope_step")
        v_transposed = K.sem("at_v_transposed")
        v_copied = K.sem("at_v_copied")
        with nc.Block() as block:
            @block.sync
            def _(sp):
                sp.dma_start(bucket[:, :], io["bucket"]).then_inc(small_loaded, 16)
                sp.dma_start(relb[:, :], io["rel_bias"]).then_inc(small_loaded, 16)
                sp.dma_start(lam_in[:, :, :].rearrange("p a b -> p (a b)"),
                             io["lam"].to_broadcast([P, 4 * HD])).then_inc(small_loaded, 16)
                for m in range(QKV_CHUNKS):
                    if m >= WR:
                        sp.wait_ge(projected, m - WR + 1)
                    sp.dma_start(wt[:, m % WR], io["w_in"][m]).then_inc(w_loaded[m % WR], 16)
                    if m == 2:
                        sp.wait_ge(relrow_done, 2)
                        sp.dma_start(io["rel_scratch"], relrow[:, :]).then_inc(relrow_stored, 16)
                    if m == 6:
                        sp.wait_ge(relrow_stored, 16)
                        sp.dma_start(toep[:, :, :], io["rel_toeplitz"]).then_inc(toep_loaded, 16)

            @block.tensor
            def _(pe):
                pe.wait_ge(small_loaded, 48)
                for half in range(2):
                    nc.tensor.matmul(K.ps[6 + half][0:MAPS, :], relb[:, :], bucket[:, half * T:(half + 1) * T],
                                     start=True, stop=True).then_inc(rel_done, 1)

                def mean_of(m):
                    pe.wait_ge(squared, m + 1)
                    if m >= 2:
                        pe.wait_ge(std_done, m - 1)
                    nc.tensor.matmul(K.ps[3 + m % 2][:, :], K.const("ones_head"), sq[:, m % 2, :], start=True,
                                     stop=True).then_inc(meaned, 1)

                def rotate(m):
                    j = m - ROPE_FIRST
                    pe.wait_ge(normed, m + 1)
                    if j >= 1:
                        pe.wait_ge(rope_step, 3 * j)
                    nc.tensor.matmul(K.ps[5][:, :], K.const("rot"), qkv[:, m, :], start=True,
                                     stop=True).then_inc(rotated, 1)

                for m in range(QKV_CHUNKS):
                    pe.wait_ge(w_loaded[m % WR], 16 * (m // WR + 1))
                    if m >= 3:
                        pe.wait_ge(raw_copied, m - 2)
                        if m - 3 < QK_CHUNKS:
                            pe.wait_ge(squared, m - 2)
                    for k in range(DC):
                        last = nc.tensor.matmul(K.ps[m % 3][:, :], wt[:, m % WR, k, :], K.hc(k), start=(k == 0),
                                                stop=(k == DC - 1))
                    last.then_inc(projected, 1)
                    if 1 <= m <= QK_CHUNKS:
                        mean_of(m - 1)
                    if ROPE_FIRST + 3 <= m < QK_CHUNKS + 3:
                        rotate(m - 3)
                for j in range(5):
                    pe.wait_ge(raw_copied, QK_CHUNKS + j + 1)
                    if j < 2:
                        pe.wait_ge(relrow_done, 2)
                    else:
                        pe.wait_ge(v_copied, j - 1)
                    for t in range(TC):
                        last = nc.tensor.transpose(K.ps[6 + j % 2][:, t * P:(t + 1) * P],
                                                   qkv[:, QK_CHUNKS + j, t * P:(t + 1) * P], K.const("ident"))
                    last.then_inc(v_transposed, 1)

            @block.scalar
            def _(act):
                def std_of(m):
                    act.wait_ge(meaned, m + 1)
                    if m >= 2:
                        act.wait_ge(rstd_done, m - 1)
                    nc.scalar.activation(std[:, m % 2, :], K.ps[3 + m % 2][:, :], ACT.Sqrt,
                                         bias=K.eps[:, 0:1]).then_inc(std_done, 1)

                for m in range(QKV_CHUNKS):
                    act.wait_ge(projected, m + 1)
                    if m < QK_CHUNKS:
                        if m >= 2:
                            act.wait_ge(meaned, m - 1)
                        nc.scalar.activation(sq[:, m % 2, :], K.ps[m % 3][:, :], ACT.Square).then_inc(squared, 1)
                    nc.scalar.activation(qkv[:, m, :], K.ps[m % 3][:, :], ACT.Copy).then_inc(raw_copied, 1)
                    if 1 <= m <= QK_CHUNKS:
                        std_of(m - 1)
                act.wait_ge(prepared, 5)
                nc.scalar.activation(lam_s[:, 2:4], lam_s[:, 0:2], ACT.Exp).then_inc(lam_exp, 1)

            @block.vector
            def _(dve):
                for half in range(2):
                    dve.wait_ge(rel_done, half + 1)
                    nc.vector.tensor_copy(relrow[:, half * T:(half + 1) * T],
                                          K.ps[6 + half][0:MAPS, :]).then_inc(relrow_done, 1)
                q0 = COLS["qk_g"][0]
                nc.vector.tensor_copy(gq[:, :], K.cols[:, q0:q0 + QK_CHUNKS]).then_inc(prepared, 1)
                dve.wait_ge(prepared, 1)
                nc.vector.tensor_scalar(gq[:, 0:4], gq[:, 0:4], HD ** -0.5, None, ALU.mult).then_inc(prepared, 1)
                nc.vector.tensor_scalar(gq[:, 8:12], gq[:, 8:12], HD ** -0.5, None, ALU.mult).then_inc(prepared, 1)
                nc.vector.tensor_tensor(lam_p[:, :, :], lam_in[:, 0:4:2, :], lam_in[:, 1:4:2, :],
                                        ALU.mult).then_inc(prepared, 1)
                dve.wait_ge(prepared, 4)
                nc.vector.tensor_reduce(lam_s[:, 0:2], lam_p[:, :, :], AX.X, ALU.add).then_inc(prepared, 1)
                nc.vector.tensor_scalar(subg[:, :], K.col("subln_g", 0), 1.0 - LAMBDA_INIT, None,
                                        ALU.mult).then_inc(prepared, 1)
                nc.vector.memset(vpad[:, :, :, :], 0.0).then_inc(prepared, 1)

                def rope(m):
                    j = m - ROPE_FIRST
                    dve.wait_ge(rotated, j + 1)
                    nc.vector.tensor_tensor(rtmp[:, 0, :], K.ps[5][:, :], K.const("sin"), ALU.mult).then_inc(rope_step, 1)
                    nc.vector.tensor_tensor(rtmp[:, 1, :], qkv[:, m, :], K.const("cos"), ALU.mult).then_inc(rope_step, 1)
                    dve.wait_ge(rope_step, 3 * j + 2)
                    nc.vector.tensor_tensor(qkv[:, m, :], rtmp[:, 0, :], rtmp[:, 1, :], ALU.add).then_inc(rope_step, 1)

                for m in range(QK_CHUNKS):
                    dve.wait_ge(std_done, m + 1)
                    nc.vector.reciprocal(rstd[:, m % 2, :], std[:, m % 2, :]).then_inc(rstd_done, 1)
                    dve.wait_ge(rstd_done, m + 1)
                    dve.wait_ge(raw_copied, m + 1)
                    nc.vector.scalar_tensor_tensor(out=qkv[:, m, :], in0=qkv[:, m, :], scalar=gq[:, m:m + 1],
                                                   in1=rstd[:, m % 2, :], op0=ALU.mult,
                                                   op1=ALU.mult).then_inc(normed, 1)
                    if m - 2 >= ROPE_FIRST:
                        rope(m - 2)
                rope(QK_CHUNKS - 2)
                rope(QK_CHUNKS - 1)
                for j in range(5):
                    dve.wait_ge(v_transposed, j + 1)
                    if j < 4:
                        nc.vector.tensor_copy(vtok[:, :, j, :],
                                              K.ps[6 + j % 2][:, :].rearrange("p (t f) -> p t f", t=TC)).then_inc(v_copied, 1)
                    else:
                        vb = K.ps[6][:, :].rearrange("p (t g f) -> p t g f", t=TC, g=2)
                        nc.vector.tensor_copy(vpad[:, :, 0, 0:HD], vb[:, :, 0, :]).then_inc(v_copied, 1)
                        nc.vector.tensor_copy(vpad[:, :, 1, HD:P], vb[:, :, 1, :]).then_inc(v_copied, 1)
                dve.wait_ge(lam_exp, 1)
                nc.vector.tensor_tensor(lam_s[:, 4:5], lam_s[:, 3:4], lam_s[:, 2:3], ALU.subtract).then_inc(prepared, 1)
                dve.wait_ge(prepared, 8)
                nc.vector.tensor_scalar(lam_s[:, 5:6], lam_s[:, 4:5], -LAMBDA_INIT, None, ALU.add).then_inc(prepared, 1)

        scored = K.sem("at_scored")
        maxed = K.sem("at_maxed")
        exped = K.sem("at_exped")
        inverted = K.sem("at_inverted")
        weighted = K.sem("at_weighted")
        p_transposed = K.sem("at_p_transposed")
        p_copied = K.sem("at_p_copied")
        attended = K.sem("at_attended")
        head_copied = K.sem("at_head_copied")

        def tiles_before(u):
            return sum(1 if kind == "A" else 2 for kind, _, _ in UNITS[:u])

        def weights_before(u):
            return 3 * u if u < 16 else 48 + 2 * (u - 16)

        with nc.Block() as block:
            @block.tensor
            def _(pe):
                def scores(u):
                    kind, a, qb = UNITS[u]
                    qs = slice(qb * P, (qb + 1) * P)
                    if u >= 2:
                        pe.wait_ge(exped, 2 * (u - 1))
                    for e in range(2):
                        out = K.ps[2 * (u % 2) + e][:, :]
                        rows = slice(HD * e, HD * (e + 1))
                        if kind == "A":
                            off = (TC - 1 - qb) * P
                            nc.tensor.matmul(out, K.const("anti"), toep[:, 2 * a + e, off:off + T], start=True,
                                             stop=False)
                            last = nc.tensor.matmul(out, qkv[rows, a, qs], qkv[rows, 4 + a, :], start=False, stop=True)
                        else:
                            last = nc.tensor.matmul(out, qkv[rows, 8 + a, qs], qkv[rows, 12, :], start=True, stop=True)
                        last.then_inc(scored, 1)

                def attend(u):
                    kind, a, qb = UNITS[u]
                    n = 1 if kind == "A" else 2
                    pe.wait_ge(weighted, weights_before(u + 1))
                    for e in range(n):
                        tile = tiles_before(u) + e
                        if tile >= 2:
                            pe.wait_ge(p_copied, tile - 1)
                        for kc in range(TC):
                            last = nc.tensor.transpose(K.ps[4 + tile % 2][:, kc * P:(kc + 1) * P],
                                                       prob[:, u % 2, e, kc * P:(kc + 1) * P], K.const("ident"))
                        last.then_inc(p_transposed, 1)
                    if u >= 2:
                        pe.wait_ge(head_copied, u - 1)
                    out = K.ps[6 + u % 2][:, 0:P]
                    for e in range(n):
                        pe.wait_ge(p_copied, tiles_before(u) + e + 1)
                        for kc in range(TC):
                            v = vtok[:, kc, a, :] if kind == "A" else vpad[:, kc, e, :]
                            last = nc.tensor.matmul(out, v, probT[:, u % 2, e, kc, :], start=(e == 0 and kc == 0),
                                                    stop=(e == n - 1 and kc == TC - 1))
                    last.then_inc(attended, 1)

                pe.wait_ge(toep_loaded, 16)
                for u in range(len(UNITS)):
                    scores(u)
                    if u:
                        attend(u - 1)
                attend(len(UNITS) - 1)

            @block.scalar
            def _(act):
                def copy_out(u):
                    kind, a, qb = UNITS[u]
                    for e in range(1 if kind == "A" else 2):
                        tile = tiles_before(u) + e
                        act.wait_ge(p_transposed, tile + 1)
                        if u >= 2:
                            act.wait_ge(attended, u - 1)
                        nc.scalar.activation(probT[:, u % 2, e, :, :],
                                             K.ps[4 + tile % 2][:, :].rearrange("p (k q) -> p k q", k=TC),
                                             ACT.Copy).then_inc(p_copied, 1)
                for u in range(len(UNITS)):
                    for e in range(2):
                        act.wait_ge(maxed, 2 * u + e + 1)
                        if u >= 2:
                            act.wait_ge(p_transposed, tiles_before(u - 1))
                        nc.scalar.activation(prob[:, u % 2, e, :], K.ps[2 * (u % 2) + e][:, :], ACT.Exp,
                                             bias=nmax[:, u % 2, e:e + 1],
                                             accum_out=esum[:, u % 2, e:e + 1]).then_inc(exped, 1)
                    if u:
                        copy_out(u - 1)
                copy_out(len(UNITS) - 1)

            @block.vector
            def _(dve):
                def copy_head(u):
                    kind, a, qb = UNITS[u]
                    c = a if kind == "A" else 4 + a
                    dve.wait_ge(attended, u + 1)
                    nc.vector.tensor_copy(heads[:, c, qb * P:(qb + 1) * P],
                                          K.ps[6 + u % 2][:, 0:P]).then_inc(head_copied, 1)
                for u, (kind, a, qb) in enumerate(UNITS):
                    for e in range(2):
                        dve.wait_ge(scored, 2 * u + e + 1)
                        if u >= 2:
                            dve.wait_ge(exped, 2 * (u - 1))
                        nc.vector.tensor_reduce(nmax[:, u % 2, e:e + 1], K.ps[2 * (u % 2) + e][:, :], AX.X, ALU.max,
                                                negate=True).then_inc(maxed, 1)
                    if u >= 2:
                        copy_head(u - 2)
                    dve.wait_ge(exped, 2 * u + 2)
                    if u >= 2:
                        dve.wait_ge(weighted, weights_before(u - 1))
                    nc.vector.reciprocal(rinv[:, u % 2, :], esum[:, u % 2, :]).then_inc(inverted, 1)
                    dve.wait_ge(inverted, u + 1)
                    w = weights_before(u)
                    if kind == "A":
                        nc.vector.tensor_tensor(rlam[:, u % 2:u % 2 + 1], rinv[:, u % 2, 1:2], lam_s[:, 5:6],
                                                ALU.mult).then_inc(weighted, 1)
                        nc.vector.tensor_scalar(prob[:, u % 2, 0, :], prob[:, u % 2, 0, :], rinv[:, u % 2, 0:1], None,
                                                ALU.mult).then_inc(weighted, 1)
                        dve.wait_ge(weighted, w + 2)
                        nc.vector.scalar_tensor_tensor(out=prob[:, u % 2, 0, :], in0=prob[:, u % 2, 1, :],
                                                       scalar=rlam[:, u % 2:u % 2 + 1], in1=prob[:, u % 2, 0, :],
                                                       op0=ALU.mult, op1=ALU.add).then_inc(weighted, 1)
                    else:
                        for e in range(2):
                            nc.vector.tensor_scalar(prob[:, u % 2, e, :], prob[:, u % 2, e, :], rinv[:, u % 2, e:e + 1],
                                                    None, ALU.mult).then_inc(weighted, 1)
                copy_head(len(UNITS) - 2)
                copy_head(len(UNITS) - 1)

        sub_squared = K.sem("at_sub_squared")
        sub_meaned = K.sem("at_sub_meaned")
        sub_std = K.sem("at_sub_std")
        sub_rstd = K.sem("at_sub_rstd")
        sub_normed = K.sem("at_sub_normed")
        wo_loaded = [K.sem(f"at_wo_loaded{i}") for i in range(WR)]
        wo_done = K.sem("at_wo_done")
        added = K.sem("at_added")
        with nc.Block() as block:
            @block.sync
            def _(sp):
                for m in range(DC):
                    if m >= WR:
                        sp.wait_ge(wo_done, m - WR + 1)
                    sp.dma_start(wt[:, m % WR], io["w_out"][m]).then_inc(wo_loaded[m % WR], 16)

            @block.scalar
            def _(act):
                for a in range(4):
                    if a >= 2:
                        act.wait_ge(sub_meaned, a - 1)
                    nc.scalar.activation(sq[:, a % 2, :], heads[:, a, :], ACT.Square).then_inc(sub_squared, 1)
                    act.wait_ge(sub_meaned, a + 1)
                    if a >= 2:
                        act.wait_ge(sub_rstd, a - 1)
                    nc.scalar.activation(std[:, a % 2, :], K.ps[a % 2][:, :], ACT.Sqrt,
                                         bias=K.eps[:, 0:1]).then_inc(sub_std, 1)

            @block.vector
            def _(dve):
                for a in range(4):
                    dve.wait_ge(sub_std, a + 1)
                    nc.vector.reciprocal(rstd[:, a % 2, :], std[:, a % 2, :]).then_inc(sub_rstd, 1)
                    dve.wait_ge(sub_rstd, a + 1)
                    nc.vector.scalar_tensor_tensor(out=heads[:, a, :], in0=heads[:, a, :], scalar=subg[:, 0:1],
                                                   in1=rstd[:, a % 2, :], op0=ALU.mult,
                                                   op1=ALU.mult).then_inc(sub_normed, 1)
                for m in range(DC):
                    dve.wait_ge(wo_done, m + 1)
                    nc.vector.scalar_tensor_tensor(out=K.x[:, m, :], in0=K.ps[2 + m % 4][:, :],
                                                   scalar=K.mod[:, 0, 16 + m:17 + m], in1=K.x[:, m, :], op0=ALU.mult,
                                                   op1=ALU.add).then_inc(added, 1)

            @block.tensor
            def _(pe):
                for a in range(4):
                    pe.wait_ge(sub_squared, a + 1)
                    if a >= 2:
                        pe.wait_ge(sub_std, a - 1)
                    nc.tensor.matmul(K.ps[a % 2][:, :], K.const("ones_v"), sq[:, a % 2, :], start=True,
                                     stop=True).then_inc(sub_meaned, 1)
                for m in range(DC):
                    pe.wait_ge(wo_loaded[m % WR], 16 * (m // WR + 1))
                    if m >= 4:
                        pe.wait_ge(added, m - 3)
                    for i, k in enumerate((4, 5, 6, 7, 0, 1, 2, 3)):
                        if m == 0 and k < 4:
                            pe.wait_ge(sub_normed, k + 1)
                        last = nc.tensor.matmul(K.ps[2 + m % 4][:, :], wt[:, m % WR, k, :], heads[:, k, :],
                                                start=(i == 0), stop=(i == DC - 1))
                    last.then_inc(wo_done, 1)


GATE_SCALE = 4096.0
TOKENS_PER_BANK = 4
TOKENS_PER_STEP = 8


def stage_peer(K, layer):
    nc, io = K.nc, K.io
    tag = f"pe{layer}_"
    with ExitStack() as ctx:
        pairT = K.sb(ctx, tag + "pairT", [P, 4, T], F16)
        peer_choose(K, layer, tag, pairT)
        last_stored = peer_gates(K, layer, tag, pairT)
    peer_experts(K, layer, tag, last_stored)


def peer_choose(K, layer, tag, pairT):
    nc, io = K.nc, K.io
    WR = 4
    HT = PH * TOPK
    with ExitStack() as ctx:
        wt = K.sb(ctx, tag + "wt", [P, WR, DC, P])
        qT = K.sb(ctx, tag + "qT", [P, 2, T])
        keys = K.sb(ctx, tag + "keys", [P, HP, NK])
        s = K.sb(ctx, tag + "s", [P, TC, HP, NK])
        cut = K.sb(ctx, tag + "cut", [P, TC, 2, NK])
        top = K.sb(ctx, tag + "top", [P, TC, HP, TOPK])
        topi = K.sb(ctx, tag + "topi", [P, TC, HP, TOPK], U32)
        topf = K.sb(ctx, tag + "topf", [P, 2, HT, TC], F16)
        best = K.sb(ctx, tag + "best", [P, TC, PH, TOPK])
        pos = K.sb(ctx, tag + "pos", [P, TC, PH, TOPK], U32)
        posab = K.sb(ctx, tag + "posab", [P, 2, TC, PH, TOPK], U32)
        posf = K.sb(ctx, tag + "posf", [P, 2, HT, TC], F16)
        iota16 = K.sb(ctx, tag + "iota16", [P, TOPK, TC], F16)
        ij = K.sb(ctx, tag + "ij", [P, 2, TC, PH, TOPK])
        gate = K.sb(ctx, tag + "gate", [P, 2, TC, HT])
        ghalf = K.sb(ctx, tag + "ghalf", [P, TC, HT], F16)
        zsum = K.sb(ctx, tag + "zsum", [P, 2, TC, PH])
        if layer == 0:
            AR, AQ = 3, 4
            AW = 6 * D // AQ
            ada_ring = K.sb(ctx, "ada1_ring", [P, AR, AW])
            ada_acc = K.sb(ctx, "ada1_acc", [P, 6 * D])
            ada_tiles = [(k, q) for k in range(DC) for q in range(AQ)]
            ada_loaded = [K.sem(f"ada1_loaded{i}") for i in range(AR)]
            ada_scaled = K.sem("ada1_scaled")
            ada_accumulated = K.sem("ada1_accumulated")
            ada_summed = K.sem("ada1_summed")
            mod_done = K.sem("mod1_done")
        w_loaded = [K.sem(f"{tag}w_loaded{i}") for i in range(WR)]
        keys_loaded = K.sem(tag + "keys_loaded")
        queried = K.sem(tag + "queried")
        q_copied = K.sem(tag + "q_copied")
        scored = K.sem(tag + "scored")
        s_copied = K.sem(tag + "s_copied")
        step = K.sem(tag + "top_step")
        chosen = K.sem(tag + "chosen")
        exped = K.sem(tag + "exped")
        ready = K.sem(tag + "pairs_ready")
        transposed = K.sem(tag + "pairs_transposed")
        pairs_copied = K.sem(tag + "pairs_copied")
        with nc.Block() as block:
            @block.sync
            def _(sp):
                sp.dma_start(keys[:, :, :].rearrange("p a b -> p (a b)"), io["subkeys"][layer]).then_inc(keys_loaded, 16)
                for m in range(HP):
                    if m >= WR:
                        sp.wait_ge(queried, m - WR + 1)
                    sp.dma_start(wt[:, m % WR], io["w_q"][layer, m]).then_inc(w_loaded[m % WR], 16)

            if layer == 0:
                @block.gpsimd
                def _(gp):
                    def load(i):
                        k, q = ada_tiles[i]
                        gp.dma_start(ada_ring[:, i % AR, :], io["ada_w"][1, k * P:(k + 1) * P, q * AW:(q + 1) * AW]
                                     ).then_inc(ada_loaded[i % AR], 16)
                    for i in range(AR):
                        load(i)
                    for i, (k, q) in enumerate(ada_tiles):
                        part = ada_acc[:, q * AW:(q + 1) * AW]
                        gp.wait_ge(ada_scaled, i + 1)
                        if k == 0:
                            nc.gpsimd.tensor_copy(part, ada_ring[:, i % AR, :]).then_inc(ada_accumulated, 1)
                        else:
                            gp.wait_ge(ada_accumulated, i - AQ + 1)
                            nc.gpsimd.tensor_tensor(part, ada_ring[:, i % AR, :], part, ALU.add
                                                    ).then_inc(ada_accumulated, 1)
                        if i + AR < len(ada_tiles):
                            gp.wait_ge(ada_accumulated, i + 1)
                            load(i + AR)

            @block.tensor
            def _(pe):
                def score(m):
                    pe.wait_ge(q_copied, m + 1)
                    if m >= 2:
                        pe.wait_ge(s_copied, m - 1)
                    for t in range(TC):
                        last = nc.tensor.matmul(K.ps[2 + m % 2][:, t * NK:(t + 1) * NK], qT[:, m % 2, t * P:(t + 1) * P],
                                                keys[:, m, :], start=True, stop=True)
                    last.then_inc(scored, 1)

                pe.wait_ge(keys_loaded, 16)
                for m in range(HP):
                    pe.wait_ge(w_loaded[m % WR], 16 * (m // WR + 1))
                    if m >= 2:
                        pe.wait_ge(q_copied, m - 1)
                    for k in range(DC):
                        last = nc.tensor.matmul(K.ps[m % 2][:, :], wt[:, m % WR, k, :], K.hc(k), start=(k == 0),
                                                stop=(k == DC - 1))
                    last.then_inc(queried, 1)
                    if m:
                        score(m - 1)
                score(HP - 1)
                for a in range(4):
                    pe.wait_ge(ready, a + 1)
                    for t in range(TC):
                        src = gate[:, a, t, :] if a < 2 else ij[:, a - 2, t, :, :].rearrange("p h k -> p (h k)")
                        last = nc.tensor.transpose(K.ps[4 + a][:, t * P:(t + 1) * P], src, K.const("ident"))
                    last.then_inc(transposed, 1)
                    if layer == 0 and a == 1:
                        pe.wait_ge(ada_accumulated, len(ada_tiles))
                        sum_modulation(K, ada_acc, ada_summed)

            @block.scalar
            def _(act):
                def copy_scores(m):
                    act.wait_ge(scored, m + 1)
                    nc.scalar.activation(s[:, :, m, :], K.ps[2 + m % 2][:, :].rearrange("p (t n) -> p t n", t=TC),
                                         ACT.Copy).then_inc(s_copied, 1)

                def scale_ada(i):
                    k = ada_tiles[i][0]
                    act.wait_ge(ada_loaded[i % AR], 16 * (i // AR + 1))
                    nc.scalar.activation(ada_ring[:, i % AR, :], ada_ring[:, i % AR, :], ACT.Copy,
                                         scale=K.cs[:, k:k + 1]).then_inc(ada_scaled, 1)

                for m in range(HP):
                    act.wait_ge(queried, m + 1)
                    if m >= 2:
                        act.wait_ge(scored, m - 1)
                    nc.scalar.activation(qT[:, m % 2, :], K.ps[m % 2][:, :], ACT.Copy).then_inc(q_copied, 1)
                    if layer == 0:
                        scale_ada(m)
                    if m:
                        copy_scores(m - 1)
                copy_scores(HP - 1)
                if layer == 0:
                    for i in range(HP, len(ada_tiles)):
                        scale_ada(i)
                act.wait_ge(chosen, 1)
                nc.scalar.activation(gate[:, 0], gate[:, 0], ACT.Exp).then_inc(exped, 1)
                for a in range(4):
                    act.wait_ge(transposed, a + 1)
                    nc.scalar.activation(pairT[:, a, :], K.ps[4 + a][:, :], ACT.Copy).then_inc(pairs_copied, 1)

            @block.vector
            def _(dve):
                n = [0]

                def then(ins):
                    n[0] += 1
                    ins.then_inc(step, 1)

                def top16(values, cuts, tops, indices):
                    k = len(values)
                    dve.wait_ge(step, n[0])
                    for v, o in zip(values, tops):
                        then(nc.vector.max(o[:, 0:8], v))
                    for i, (v, o, x) in enumerate(zip(values, tops, indices)):
                        dve.wait_ge(step, n[0] - (k - 1))
                        then(nc.vector.max_index(x[:, 0:8], o[:, 0:8], v))
                    for v, o, c in zip(values, tops, cuts):
                        then(nc.vector.match_replace(c, o[:, 0:8], v, NEG))
                    for c, o in zip(cuts, tops):
                        dve.wait_ge(step, n[0] - (k - 1))
                        then(nc.vector.max(o[:, 8:16], c))
                    for c, o, x in zip(cuts, tops, indices):
                        dve.wait_ge(step, n[0] - (k - 1))
                        then(nc.vector.max_index(x[:, 8:16], o[:, 8:16], c))

                for m in range(HP):
                    dve.wait_ge(s_copied, m + 1)
                    top16([s[:, t, m, :] for t in range(TC)], [cut[:, t, m % 2, :] for t in range(TC)],
                          [top[:, t, m, :] for t in range(TC)], [topi[:, t, m, :] for t in range(TC)])
                dve.wait_ge(step, n[0])
                for half in range(2):
                    then(nc.vector.tensor_copy(topf[:, half].rearrange("p (h k) t -> p t h k", h=PH), topi[:, :, half:HP:2, :]))
                then(nc.vector.tensor_copy(iota16[:, :, :], K.const("iota")[:, 0:TOPK].unsqueeze(2).to_broadcast([P, TOPK, TC])))

                cand = s[:, :, :, :].rearrange("p t (h c) n -> p t h (c n)", h=PH)
                shape = [P, PH, TOPK, TOPK]
                for t in range(TC):
                    first = top[:, t, 0:HP:2, :].unsqueeze(3).to_broadcast(shape)
                    second = top[:, t, 1:HP:2, :].unsqueeze(2).to_broadcast(shape)
                    then(nc.vector.tensor_tensor(cand[:, t].rearrange("p h (a b) -> p h a b", a=TOPK), first, second,
                                                 ALU.add))
                cuts = cut[:, :, :, :].rearrange("p t a n -> p t (a n)")
                for t in range(TC):
                    for h in range(0, PH, 4):
                        top16([cand[:, t, h + e, :] for e in range(4)], [cuts[:, e, :] for e in range(4)],
                              [best[:, t, h + e, :] for e in range(4)], [pos[:, t, h + e, :] for e in range(4)])
                dve.wait_ge(step, n[0])
                bestv = best[:, :, :, :].rearrange("p t h k -> p (t h) k")
                gatev = gate[:, 0].rearrange("p t (h k) -> p (t h) k", h=PH)
                flat = [P, TC * PH, TOPK]
                nc.vector.tensor_tensor(gatev, bestv, bestv[:, :, 0:1].to_broadcast(flat), ALU.subtract).then_inc(chosen, 1)
                then(nc.vector.tensor_scalar(posab[:, 0], pos[:, :, :, :], 4, None, ALU.logical_shift_right))
                then(nc.vector.tensor_scalar(posab[:, 1], pos[:, :, :, :], TOPK - 1, None, ALU.bitwise_and))
                dve.wait_ge(step, n[0])
                for half in range(2):
                    then(nc.vector.tensor_copy(posf[:, half].rearrange("p (h k) t -> p t h k", h=PH), posab[:, half]))
                dve.wait_ge(exped, 1)
                zs = zsum[:, :, :, :].rearrange("p a t h -> p a (t h)")
                then(nc.vector.tensor_reduce(zs[:, 0, :], gatev, AX.X, ALU.add))
                dve.wait_ge(step, n[0])
                then(nc.vector.reciprocal(zs[:, 1, :], zs[:, 0, :]))
                dve.wait_ge(step, n[0])
                then(nc.vector.tensor_scalar(zs[:, 1, :], zs[:, 1, :], GATE_SCALE, None, ALU.mult))
                dve.wait_ge(step, n[0])
                then(nc.vector.tensor_tensor(gatev, gatev, zs[:, 1, :].unsqueeze(2).to_broadcast(flat), ALU.mult))
                dve.wait_ge(step, n[0])
                then(nc.vector.tensor_copy(ghalf[:, :, :], gate[:, 0]))
                dve.wait_ge(step, n[0])
                then(nc.vector.tensor_tensor(gate[:, 1], gate[:, 0], ghalf[:, :, :], ALU.subtract))
                dve.wait_ge(step, n[0])
                nc.vector.tensor_copy(gate[:, 0], ghalf[:, :, :]).then_inc(ready, 1)
                nc.vector.memset(zsum[:, 0, :, :], 0.0).then_inc(ready, 1)
                halves = cand.rearrange("p t h n -> p (t h n)").bitcast(F16)
                n_hot = HT * TOPK * TC
                eq, picked = (halves[:, i * n_hot:(i + 1) * n_hot].rearrange("p (m j t) -> p m j t", m=HT, j=TOPK)
                              for i in range(2))
                for half in range(2):
                    dve.wait_ge(step, n[0])
                    then(nc.vector.tensor_tensor(eq, posf[:, half].unsqueeze(2).to_broadcast([P, HT, TOPK, TC]),
                                                 iota16[:, :, :].unsqueeze(1).to_broadcast([P, HT, TOPK, TC]),
                                                 ALU.is_equal))
                    dve.wait_ge(step, n[0])
                    for h in range(PH):
                        rows = slice(h * TOPK, (h + 1) * TOPK)
                        then(nc.vector.tensor_tensor(picked[:, rows], eq[:, rows], topf[:, half, rows, :].unsqueeze(1)
                                                     .to_broadcast([P, TOPK, TOPK, TC]), ALU.mult))
                    w = TOPK // 2
                    while w > 1:
                        dve.wait_ge(step, n[0])
                        then(nc.vector.tensor_tensor(picked[:, :, 0:w], picked[:, :, 0:w], picked[:, :, w:2 * w], ALU.add))
                        w //= 2
                    dve.wait_ge(step, n[0])
                    nc.vector.tensor_tensor(ij[:, half].rearrange("p t h k -> p (h k) t"), picked[:, :, 0],
                                            picked[:, :, 1], ALU.add).then_inc(ready, 1)
                if layer == 0:
                    finish_modulation(K, dve, 1, ada_summed, mod_done)


def peer_gates(K, layer, tag, pairT):
    nc, io = K.nc, K.io
    G = TOKENS_PER_BANK
    S = TOKENS_PER_STEP
    QS = S // G
    STEPS = P // S
    with ExitStack() as ctx:
        iota = K.sb(ctx, tag + "iota", [P, P, S], F16)
        hot = K.sb(ctx, tag + "hot", [P, 2, 4, P, S], F16)
        stage = K.sb(ctx, tag + "stage", [P, 2, NK, P])
        iota_ready = K.sem(tag + "iota_ready")
        rows_ready = K.sem(tag + "rows_ready")
        hot_ready = K.sem(tag + "hot_ready")
        bank_done = K.sem(tag + "bank_done")
        bank_free = K.sem(tag + "bank_free")
        chunk_done = K.sem(tag + "chunk_done")
        chunk_stored = [K.sem(f"{tag}chunk_stored{i}") for i in range(2)]
        with nc.Block() as block:
            @block.vector
            def _(dve):
                nc.vector.tensor_copy(iota[:, :, :], K.const("iota").unsqueeze(2).to_broadcast([P, P, S])
                                      ).then_inc(iota_ready, 1)
                dve.wait_ge(iota_ready, 1)
                with dve.Fori(0, TC * STEPS // 2) as i:
                    for side in range(2):
                        def pair(which):
                            return pairT[:, which, bass.ds(i * (2 * S) + side * S, S)].unsqueeze(1).to_broadcast([P, P, S])
                        dve.wait_ge(bank_done, 2 * QS * i + QS * (side + 1))
                        nc.vector.tensor_tensor(hot[:, side, 1], iota[:, :, :], pair(2), ALU.is_equal).then_inc(rows_ready, 1)
                        nc.vector.tensor_tensor(hot[:, side, 0], iota[:, :, :], pair(3), ALU.is_equal).then_inc(hot_ready, 1)
                        dve.wait_ge(rows_ready, 2 * i + side + 1)
                        nc.vector.tensor_tensor(hot[:, side, 2], hot[:, side, 1], pair(0), ALU.mult).then_inc(hot_ready, 1)
                        nc.vector.tensor_tensor(hot[:, side, 3], hot[:, side, 1], pair(1), ALU.mult).then_inc(hot_ready, 1)

            @block.tensor
            def _(pe):
                pe.nop().then_inc(bank_done, 2 * QS)
                with pe.Fori(0, TC * STEPS // 2) as i:
                    for side in range(2):
                        pe.wait_ge(hot_ready, 6 * i + 3 * side + 3)
                        for q in range(QS):
                            pe.wait_ge(bank_free, 2 * QS * i + QS * side + q + 1)
                            for r in range(G):
                                t = q * G + r
                                out = K.ps[QS * side + q][:, r * NK:(r + 1) * NK]
                                nc.tensor.matmul(out, hot[:, side, 0, :, t], hot[:, side, 2, :, t], start=True, stop=False)
                                last = nc.tensor.matmul(out, hot[:, side, 0, :, t], hot[:, side, 3, :, t], start=False,
                                                        stop=True)
                            last.then_inc(bank_done, 1)

            @block.scalar
            def _(act):
                act.nop().then_inc(bank_free, 2 * QS)
                for c in range(TC):
                    if c >= 2:
                        act.wait_ge(chunk_stored[c % 2], 16 * (c // 2))
                    with act.Fori(0, STEPS // 2) as i:
                        for side in range(2):
                            for q in range(QS):
                                b = QS * side + q
                                act.wait_ge(bank_done, 2 * QS * i + (QS * STEPS * c + b + 1 + 2 * QS))
                                nc.scalar.activation(stage[:, c % 2, :, bass.ds(i * (2 * S) + b * G, G)],
                                                     K.ps[b][:, :].rearrange("p (t n) -> p n t", t=G), ACT.Copy,
                                                     scale=1.0 / GATE_SCALE).then_inc(bank_free, 1)
                    act.wait_ge(bank_free, QS * STEPS * (c + 1) + 2 * QS)
                    act.nop().then_inc(chunk_done, 1)

            @block.sync
            def _(sp):
                for c in range(TC):
                    sp.wait_ge(chunk_done, c + 1)
                    sp.dma_start(io["gates"][:, :, c * P:(c + 1) * P].rearrange("i j t -> j i t"),
                                 stage[:, c % 2, :, :]).then_inc(chunk_stored[c % 2], 16)
                sp.wait_ge(chunk_stored[0], 16 * (TC // 2))
    return chunk_stored[1]


def split_matmul(nc, out, left, right, start, stop):
    nc.tensor.matmul(out, left[0], right[0], start=start, stop=False)
    nc.tensor.matmul(out, left[0], right[1], start=False, stop=False)
    return nc.tensor.matmul(out, left[1], right[0], start=False, stop=stop)


def peer_experts(K, layer, tag, last_stored):
    nc, io = K.nc, K.io
    G = GROUP
    with ExitStack() as ctx:
        hh = K.sb(ctx, tag + "hh", [P, DC, T], F32R)
        hl = K.sb(ctx, tag + "hl", [P, DC, T], F32R)
        uh = K.sb(ctx, tag + "uh", [P, 2, G, D], F32R)
        ul = K.sb(ctx, tag + "ul", [P, 2, G, D], F32R)
        u = K.sb(ctx, tag + "u", [P, 2, G, D])
        vh = K.sb(ctx, tag + "vh", [P, 2, G, D], F32R)
        vl = K.sb(ctx, tag + "vl", [P, 2, G, D], F32R)
        w = K.sb(ctx, tag + "w", [P, 2, G, T])
        ah = K.sb(ctx, tag + "ah", [P, 2, G, T], F32R)
        al = K.sb(ctx, tag + "al", [P, 2, G, T], F32R)
        v = K.sb(ctx, tag + "v", [P, 2, G, D])

        def a(side, r):
            return K.hc(G * side + r)
        u_loaded = [K.sem(f"{tag}u_loaded{i}") for i in range(2)]
        v_loaded = [K.sem(f"{tag}v_loaded{i}") for i in range(2)]
        w_loaded = [K.sem(f"{tag}wt_loaded{i}") for i in range(2)]
        h_high = K.sem(tag + "h_high")
        h_low = K.sem(tag + "h_low")
        u_high = K.sem(tag + "u_high")
        u_low = K.sem(tag + "u_low")
        v_high = K.sem(tag + "v_high")
        v_low = K.sem(tag + "v_low")
        up_done = K.sem(tag + "up_done")
        gelu_done = K.sem(tag + "gelu_done")
        gated = K.sem(tag + "gated")
        a_high = K.sem(tag + "a_high")
        a_low = K.sem(tag + "a_low")
        down_done = K.sem(tag + "down_done")
        added = K.sem(tag + "added")

        def over_groups(eng, step):
            step(0, 0, True, False)
            step(1, 1, False, False)
            with eng.Fori(0, GROUPS // 2 - 2) as i:
                step(2 + 2 * i, 0, False, False)
                step(3 + 2 * i, 1, False, False)
            step(GROUPS - 2, 0, False, False)
            step(GROUPS - 1, 1, False, True)

        def reuses(n):
            return not isinstance(n, int) or n >= 2

        def loads(side, n):
            return 8 * n + (16 - 8 * side)

        with nc.Block() as block:
            @block.sync
            def _(sp):
                def load_u(n, side):
                    if reuses(n):
                        sp.wait_ge(u_low, n - 1)
                    sp.dma_start(u[:, side], io["u"][layer, bass.ds(n * G, G)].rearrange("g p c e -> p g (c e)")
                                 ).then_inc(u_loaded[side], 16)

                def load(n, side, first, last):
                    if not last:
                        load_u(n + 1, 1 - side)
                    if first:
                        sp.wait_ge(last_stored, 16 * (TC // 2))
                    rows = bass.ds(n * G, G)
                    if reuses(n):
                        sp.wait_ge(gated, G * n - G)
                    sp.dma_start(w[:, side], io["gates"][rows].rearrange("g j t -> j g t")).then_inc(w_loaded[side], 16)
                    if reuses(n):
                        sp.wait_ge(v_low, n - 1)
                    sp.dma_start(v[:, side], io["v"][layer, rows].rearrange("g j d -> j g d")).then_inc(v_loaded[side], 16)
                load_u(0, 0)
                over_groups(sp, load)

            @block.tensor
            def _(pe):
                def up(n, side):
                    pe.wait_ge(u_low, n + 1)
                    for r in range(G):
                        if reuses(n):
                            pe.wait_ge(gelu_done, G * n + r - 3)
                        for k in range(DC):
                            if isinstance(n, int) and n == 0 and r == 0:
                                pe.wait_ge(h_low, k + 1)
                            cols = slice(k * P, (k + 1) * P)
                            last = split_matmul(nc, K.ps[G * side + r][:, :], (uh[:, side, r, cols], ul[:, side, r, cols]),
                                                (hh[:, k, :], hl[:, k, :]), k == 0, k == DC - 1)
                        last.then_inc(up_done, 1)

                def down(n, side):
                    pe.wait_ge(v_low, n + 1)
                    pe.wait_ge(a_low, G * n + G)
                    for c in range(DC):
                        if not (isinstance(n, int) and n == 0 and c < 4):
                            pe.wait_ge(added, DC * n + c - 3)
                        cols = slice(c * P, (c + 1) * P)
                        for r in range(G):
                            last = split_matmul(nc, K.ps[4 + c % 4][:, :], (vh[:, side, r, cols], vl[:, side, r, cols]),
                                                (ah[:, side, r, :], al[:, side, r, :]), r == 0, r == G - 1)
                        last.then_inc(down_done, 1)

                def both(n, side, first, last):
                    up(n, side)
                    if not first:
                        down(n - 1, 1 - side)
                    if last:
                        down(n, side)
                over_groups(pe, both)

            @block.scalar
            def _(act):
                def high_u(n, side):
                    act.wait_ge(u_loaded[side], loads(side, n))
                    if reuses(n):
                        act.wait_ge(up_done, G * n - G)
                    nc.scalar.activation(uh[:, side], u[:, side], ACT.Copy).then_inc(u_high, 1)

                def gelu(n, side, r):
                    if r == 0 and reuses(n):
                        act.wait_ge(down_done, DC * n - DC)
                    act.wait_ge(up_done, G * n + r + 1)
                    nc.scalar.activation(a(side, r), K.ps[G * side + r][:, :],
                                         ACT.Gelu_apprx_tanh).then_inc(gelu_done, 1)

                def both(n, side, first, last):
                    if not last:
                        high_u(n + 1, 1 - side)
                    gelu(n, side, 0)
                    act.wait_ge(v_loaded[side], loads(side, n))
                    nc.scalar.activation(vh[:, side], v[:, side], ACT.Copy).then_inc(v_high, 1)
                    gelu(n, side, 1)
                    for r in range(G):
                        act.wait_ge(gated, G * n + r + 1)
                        nc.scalar.activation(ah[:, side, r, :], a(side, r), ACT.Copy).then_inc(a_high, 1)

                for c in range(DC):
                    nc.scalar.activation(hh[:, c, :], K.hc(c), ACT.Copy).then_inc(h_high, 1)
                    if c == 0:
                        high_u(0, 0)
                over_groups(act, both)

            @block.vector
            def _(dve):
                def low_u(n, side):
                    dve.wait_ge(u_high, n + 1)
                    nc.vector.tensor_tensor(ul[:, side], u[:, side], uh[:, side].bitcast(F32),
                                            ALU.subtract).then_inc(u_low, 1)

                def add(n):
                    for c in range(DC):
                        dve.wait_ge(down_done, DC * n + c + 1)
                        nc.vector.scalar_tensor_tensor(out=K.x[:, c, :], in0=K.ps[4 + c % 4][:, :],
                                                       scalar=K.mod[:, layer, 40 + c:41 + c], in1=K.x[:, c, :],
                                                       op0=ALU.mult, op1=ALU.add).then_inc(added, 1)

                def gate(n, side, r):
                    dve.wait_ge(gelu_done, G * n + r + 1)
                    nc.vector.tensor_tensor(a(side, r), a(side, r), w[:, side, r, :],
                                            ALU.mult).then_inc(gated, 1)

                def both(n, side, first, last):
                    if not last:
                        low_u(n + 1, 1 - side)
                    dve.wait_ge(w_loaded[side], loads(side, n))
                    gate(n, side, 0)
                    dve.wait_ge(v_high, n + 1)
                    nc.vector.tensor_tensor(vl[:, side], v[:, side], vh[:, side].bitcast(F32),
                                            ALU.subtract).then_inc(v_low, 1)
                    gate(n, side, 1)
                    if not first:
                        add(n - 1)
                    for r in range(G):
                        dve.wait_ge(a_high, G * n + r + 1)
                        nc.vector.tensor_tensor(al[:, side, r, :], a(side, r), ah[:, side, r, :].bitcast(F32),
                                                ALU.subtract).then_inc(a_low, 1)
                    if last:
                        add(n)

                for c in range(DC):
                    dve.wait_ge(h_high, c + 1)
                    nc.vector.tensor_tensor(hl[:, c, :], K.hc(c), hh[:, c, :].bitcast(F32), ALU.subtract).then_inc(h_low, 1)
                    if c == 0:
                        low_u(0, 0)
                over_groups(dve, both)


DECAY = float(np.exp(-0.5))
PLACE = (0, 1, 6, 2, 3, 4, 5, 7)
FRONT = 6


def stage_rwkv(K):
    rwkv_project(K)
    rwkv_mix(K)
    project_residual(K, "rw_wo", K.io["w_o"], K.hc, 1)


def project_residual(K, tag, weights, act_of, layer):
    nc = K.nc
    WR = 4
    with ExitStack() as ctx:
        wt = K.sb(ctx, tag, [P, WR, DC, P])
        loaded = [K.sem(f"{tag}_loaded{i}") for i in range(WR)]
        projected = K.sem(tag + "_projected")
        added = K.sem(tag + "_added")
        x_loaded = K.sem(tag + "_x_loaded")
        with nc.Block() as block:
            @block.sync
            def _(sp):
                for m in range(DC):
                    if m >= WR:
                        sp.wait_ge(projected, m - WR + 1)
                    sp.dma_start(wt[:, m % WR], weights[m]).then_inc(loaded[m % WR], 16)
                    if m == 1:
                        sp.dma_start(K.x[:, :, :], K.io["x_parked"]).then_inc(x_loaded, 16)

            @block.vector
            def _(dve):
                dve.wait_ge(x_loaded, 16)
                for m in range(DC):
                    dve.wait_ge(projected, m + 1)
                    nc.vector.scalar_tensor_tensor(out=K.x[:, m, :], in0=K.ps[m % 4][:, :],
                                                   scalar=K.mod[:, layer, 16 + m:17 + m], in1=K.x[:, m, :],
                                                   op0=ALU.mult, op1=ALU.add).then_inc(added, 1)

            @block.tensor
            def _(pe):
                for m in range(DC):
                    pe.wait_ge(loaded[m % WR], 16 * (m // WR + 1))
                    if m >= 4:
                        pe.wait_ge(added, m - 3)
                    for k in range(DC):
                        last = nc.tensor.matmul(K.ps[m % 4][:, :], wt[:, m % WR, k, :], act_of(k), start=(k == 0),
                                                stop=(k == DC - 1))
                    last.then_inc(projected, 1)


def rwkv_project(K):
    nc, io = K.nc, K.io
    WR, SR = 4, 4
    MIXES = (1, 4, 5, 0, 2, 3)
    with ExitStack() as ctx:
        xx = K.sb(ctx, "rp_xx", [P, DC, T])
        xm = K.sb(ctx, "rp_xm", [P, 2, DC, T])
        wt = K.sb(ctx, "rp_wt", [P, WR, DC, P])
        hid = K.sb(ctx, "rp_hid", [P, 3, T])
        w2 = K.sb(ctx, "rp_w2", [P, 3, D])
        out = K.sb(ctx, "rp_out", [P, SR, T])
        w_loaded = [K.sem(f"rp_w_loaded{i}") for i in range(WR)]
        w2_loaded = K.sem("rp_w2_loaded")
        x_stored = K.sem("rp_x_stored")
        shifted = K.sem("rp_shifted")
        mixed = K.sem("rp_mixed")
        projected = K.sem("rp_projected")
        hid_done = K.sem("rp_hid_done")
        evacuated = K.sem("rp_evacuated")
        stored = [K.sem(f"rp_stored{i}") for i in range(SR)]
        WIDE = [(kind, c) for kind in range(3) for c in range(DC)]
        NARROW = [(kind, c) for c in range(DC) for kind in range(3, 8)]
        OUTS = WIDE + NARROW
        with nc.Block() as block:
            @block.sync
            def _(sp):
                sp.dma_start(w2[:, :, :], io["lora2"].rearrange("a p d -> p a d")).then_inc(w2_loaded, 16)
                for n in range(3 + len(WIDE)):
                    if n >= WR:
                        sp.wait_ge(projected, n - WR + 1)
                    src = io["lora1"][n] if n < 3 else io["w_rkv"][n - 3]
                    sp.dma_start(wt[:, n % WR], src).then_inc(w_loaded[n % WR], 16)
                    if n == 2 * WR:
                        sp.dma_start(io["x_parked"], K.x[:, :, :]).then_inc(x_stored, 16)
                sp.wait_ge(x_stored, 16)

            @block.gpsimd
            def _(gp):
                for n, (kind, c) in enumerate(OUTS):
                    gp.wait_ge(evacuated, n + 1)
                    gp.dma_start(io["rwkv"][PLACE[kind], c], out[:, n % SR, :]).then_inc(stored[n % SR], 16)
                for i in range(SR):
                    gp.wait_ge(stored[i], 16 * (len(OUTS) // SR))

            @block.vector
            def _(dve):
                for c in range(DC):
                    nc.vector.tensor_tensor(xx[:, c, :], K.h[:, c, 0:T], K.h[:, c, 2:T + 2], ALU.add).then_inc(shifted, 1)
                for c in range(DC):
                    dve.wait_ge(shifted, c + 1)
                    nc.vector.scalar_tensor_tensor(out=xx[:, c, :], in0=xx[:, c, :], scalar=0.5, in1=K.hc(c),
                                                   op0=ALU.mult, op1=ALU.subtract).then_inc(shifted, 1)
                for i, row in enumerate(MIXES):
                    if i >= 2:
                        dve.wait_ge(projected, i - 1 if i < 5 else 3 + DC * (i - 4))
                    for c in range(DC):
                        dve.wait_ge(shifted, DC + c + 1)
                        nc.vector.scalar_tensor_tensor(out=xm[:, i % 2, c, :], in0=xx[:, c, :],
                                                       scalar=K.col("mix", row * DC + c), in1=K.hc(c),
                                                       op0=ALU.mult, op1=ALU.add).then_inc(mixed, 1)

            @block.tensor
            def _(pe):
                for n in range(3 + len(WIDE)):
                    i = n if n < 3 else 3 + (n - 3) // DC
                    pe.wait_ge(w_loaded[n % WR], 16 * (n // WR + 1))
                    if n >= 4:
                        pe.wait_ge(hid_done, min(n - 3, 3))
                        if n >= 7:
                            pe.wait_ge(evacuated, n - 6)
                    for k in range(DC):
                        pe.wait_ge(mixed, DC * i + k + 1)
                        last = nc.tensor.matmul(K.ps[n % 4][:, :], wt[:, n % WR, k, :], xm[:, i % 2, k, :],
                                                start=(k == 0), stop=(k == DC - 1))
                    last.then_inc(projected, 1)
                pe.wait_ge(w2_loaded, 16)
                for j, (kind, c) in enumerate(NARROW):
                    n = 3 + len(WIDE) + j
                    pe.wait_ge(evacuated, n - 6)
                    which, rows = ((0, slice(0, HD)), (0, slice(HD, P)), (1, slice(0, HD)), (1, slice(HD, P)),
                                   (2, slice(0, P)))[kind - 3]
                    nc.tensor.matmul(K.ps[n % 4][:, :], w2[rows, which, c * P:(c + 1) * P], hid[rows, which, :],
                                     start=True, stop=True).then_inc(projected, 1)

            @block.scalar
            def _(act):
                for n, f in enumerate((ACT.Tanh, ACT.Copy, ACT.Sigmoid)):
                    act.wait_ge(projected, n + 1)
                    nc.scalar.activation(hid[:, n, :], K.ps[n][:, :], f).then_inc(hid_done, 1)
                for n, (kind, c) in enumerate(OUTS):
                    act.wait_ge(projected, n + 4)
                    if n >= SR:
                        act.wait_ge(stored[n % SR], 16 * (n // SR))
                    bank = K.ps[(n + 3) % 4]
                    if 3 <= kind < 7:
                        bias = K.col("w0" if kind < 5 else "a0", (kind - 3) % 2 * DC + c)
                        nc.scalar.activation(out[:, n % SR, :], bank[:, :], ACT.Sigmoid, bias=bias).then_inc(evacuated, 1)
                    else:
                        nc.scalar.activation(out[:, n % SR, :], bank[:, :], ACT.Copy).then_inc(evacuated, 1)


def rwkv_mix(K):
    nc, io = K.nc, K.io
    NLEV = LEVELS - 1
    with ExitStack() as ctx:
        sb = lambda name, shape, dt=F32: K.sb(ctx, "rm_" + name, shape, dt)
        infront = sb("infront", [P, FRONT, T])
        intail = sb("intail", [P, 2, 2, T])
        masks = sb("masks", [P, 2, LEVELS, P], U32)
        tri = sb("tri", [P, 4, P], U32)
        scanmask = sb("scanmask", [P, T])
        ka1 = sb("ka1", [P, DC])
        kk = sb("kk", [P, T])
        sq = sb("sq", [P, T])
        norm = sb("norm", [P, 2, T])
        cs = sb("cs", [P, 2, T])
        mid = sb("mid", [P, 2, TC])
        emid = sb("emid", [P, 2, TC])
        fac = sb("fac", [P, 2, 2, TC - 1])
        dA = sb("dA", [P, 2, T])
        dR = sb("dR", [P, 2, T])
        A = sb("A", [P, 2, 2, TC, 2, P])
        R = sb("R", [P, 2, 2, TC, 2, P])
        B = sb("B", [P, 2, 2, T])
        C = sb("C", [P, 2, 2, T])
        bonus = sb("bonus", [P, 2, T])
        tokB = sb("tokB", [P, 2, TC, P])
        tokC = sb("tokC", [P, 2, TC, P])
        tokV = sb("tokV", [P, TC, P])
        Tm = sb("T", [P, 4, 4, P])
        Pb = sb("P", [P, 2, 4, P])
        MT = sb("MT", [P, 3, 4, 4, P])
        S = sb("S", [P, 2, 2, P])
        Stmp = sb("Stmp", [P, 2, P])
        rhs = sb("rhs", [P, 2, P])
        U = sb("U", [P, 2, P])
        y = sb("y", [P, TC, P])
        yc = sb("yc", [P, TC, P])
        ysq = sb("ysq", [P, TC, P])
        stat = sb("stat", [P, 4, 2 * TC])
        ln = sb("ln", [P, T])

        sem = lambda name: K.sem("rm_" + name)
        const_loaded = sem("const_loaded")
        front_loaded = sem("front_loaded")
        tail_loaded = [sem("tail_loaded0"), sem("tail_loaded1")]
        setup = sem("setup")
        ident_ready = sem("ident_ready")
        step = sem("step")
        kx_ready = sem("kx_ready")
        kx_squared = sem("kx_squared")
        kk_summed = sem("kk_summed")
        ss_ready = sem("ss_ready")
        kn_ready = sem("kn_ready")
        d_ready = sem("d_ready")
        e_ready = sem("e_ready")
        bonus_ready = sem("bonus_ready")
        bonus_summed = sem("bonus_summed")
        bonus_out = sem("bonus_out")
        factors = sem("factors")
        tok_done = sem("tok_done")
        tok_out = sem("tok_out")
        n_done = sem("n_done")
        nt_done = sem("nt_done")
        masked_done = sem("masked_done")
        nt_out = sem("nt_out")
        prod_out = sem("prod_out")
        p_done = sem("p_done")
        p_out = sem("p_out")
        q_done = sem("q_done")
        tt_done = sem("tt_done")
        tt_out = sem("tt_out")
        inv_out = sem("inv_out")
        s_zero = sem("s_zero")
        rhs_done = sem("rhs_done")
        rhs_out = sem("rhs_out")
        u_done = sem("u_done")
        u_out = sem("u_out")
        s_done = sem("s_done")
        s_out = sem("s_out")
        y_done = sem("y_done")
        y_out = sem("y_out")
        var_ready = sem("var_ready")
        sd_ready = sem("sd_ready")
        yn_ready = sem("yn_ready")
        yt_done = sem("yt_done")
        ln_ready = sem("ln_ready")
        waited = sem("waited")
        done = sem("done")

        COLS_OF = (slice(0, HD), slice(HD, P))
        INV = 4 * NLEV
        FRONT_AT = ((1, 1), (1, 3), (2, 1), (2, 3), (3, 3), (4, 3), (5, 1), (5, 3))
        ACT_FRONT_AT = ((1, 3), (2, 3), (3, 1), (3, 3))
        NFRONT, NSTEP = 20, 44

        def group(lv, g):
            return 4 * (lv - 1) + g + 1

        def over_chunks(eng, body):
            body(0, 0, True, False)
            with eng.Fori(0, DC // 2 - 1) as i:
                body(2 * i + 1, 1, False, False)
                body(2 * i + 2, 0, False, False)
            body(DC - 1, 1, False, True)

        def bc4(m):
            return m.unsqueeze(1).to_broadcast([P, 4, P])

        def bank4(i):
            return K.ps[i][:, :].rearrange("p (u t) -> p u t", u=4)

        def blocks(a, z):
            return a[:, z].rearrange("p (b t) -> p b t", b=TC)

        PLACES = K.x[:, :, :].rearrange("p c t -> p (c t)")
        NTx = PLACES[:, 0:4 * 4 * P].rearrange("p (g u t) -> p g u t", g=4, u=4)
        TTx = PLACES[:, 4 * 4 * P:8 * 4 * P].rearrange("p (g u t) -> p g u t", g=4, u=4)
        NT, TT = NTx, TTx
        with nc.Block() as block:
            @block.sync
            def _(sp):
                sp.dma_start(masks[:, :, :, :], io["masks"]).then_inc(const_loaded, 16)
                sp.dma_start(tri[:, :, :], io["tri"]).then_inc(const_loaded, 16)
                sp.dma_start(scanmask[:, :], io["scanmask"]).then_inc(const_loaded, 16)

                def load(c, side):
                    if not (isinstance(c, int) and c == 0):
                        sp.wait_ge(factors, 6 * c)
                    sp.dma_start(infront[:, :, :], io["rwkv"][0:FRONT, bass.ds(c, 1)].rearrange("k c p t -> p (k c) t")
                                 ).then_inc(front_loaded, 16)
                    if not (isinstance(c, int) and c < 2):
                        sp.wait_ge(done, c - 1)
                    sp.dma_start(intail[:, side], io["rwkv"][FRONT:8, bass.ds(c, 1)].rearrange("k c p t -> p (k c) t")
                                 ).then_inc(tail_loaded[side], 16)
                load(0, 0)
                load(1, 1)
                with sp.Fori(0, DC // 2 - 1) as i:
                    for side in range(2):
                        load(2 * i + side + 2, side)

            @block.gpsimd
            def _(gp):
                for m in (MT[:, :, :, :, :], A[:, :, :, :, :, :], R[:, :, :, :, :, :]):
                    gp.memset(m, 0.0).then_inc(setup, 1)

                def body(c, side, first, last):
                    if not first:
                        gp.wait_ge(tt_done, INV * c)
                        gp.wait_ge(p_done, 4 * NLEV * c)
                        gp.sem_inc(waited, 1)
                    for g4 in range(4):
                        gp.tensor_copy(Tm[:, g4], bc4(K.const("ident"))).then_inc(ident_ready, 1)
                over_chunks(gp, body)

            @block.vector
            def _(dve):
                dve.wait_ge(const_loaded, 48)
                a = COLS["k_a"][0]
                nc.vector.tensor_scalar(ka1[:, :], K.cols[:, a:a + DC], -1.0, 1.0, ALU.mult, ALU.add).then_inc(step, 1)
                n = [0]
                base = [1]

                def then(ins):
                    n[0] += 1
                    ins.then_inc(step, 1)

                def settled():
                    dve.wait_ge(step, base[0] + n[0])

                def round_up(to):
                    assert n[0] <= to, n[0]
                    for _ in range(to - n[0]):
                        then(dve.nop())

                def col(name, c):
                    return K.cols[:, bass.ds(c + COLS[name][0], 1)]

                both = [P, 2, T]

                def twice(m):
                    return m.unsqueeze(1).to_broadcast(both)

                def front(part, c, side):
                    r, k, sg, av = infront[:, 0], infront[:, 1], infront[:, 2:4], infront[:, 4:6]
                    v = intail[:, side, 0]
                    if part == 0:
                        dve.wait_ge(front_loaded, 16 * c + 16)
                        settled()
                        nc.vector.tensor_scalar(kk[:, :], k, col("k_k", c), None, ALU.mult).then_inc(kx_ready, 1)
                        for z in range(2):
                            then(nc.vector.tensor_tensor_scan(cs[:, z], scanmask[:, :], sg[:, z], 0.0, ALU.mult, ALU.add))
                        settled()
                        then(nc.vector.tensor_scalar(mid[:, :, :].unsqueeze(3), cs[:, :, :].rearrange(
                            "p z (b t) -> p z b t", b=TC)[:, :, :, P - 1:P], 0.5, None, ALU.mult))
                    elif part == 1:
                        settled()
                        m0, m1 = (mid[:, z, :].unsqueeze(2).to_broadcast([P, TC, P]) for z in range(2))
                        then(nc.vector.tensor_tensor(blocks(dR, 0), blocks(cs, 0), m0, ALU.subtract))
                        then(nc.vector.tensor_tensor(blocks(dA, 1), m1, blocks(cs, 1), ALU.subtract))
                        settled()
                        nc.vector.tensor_tensor(dA[:, 0], dR[:, 0], sg[:, 0], ALU.subtract).then_inc(d_ready, 1)
                        nc.vector.tensor_tensor(dR[:, 1], dA[:, 1], sg[:, 1], ALU.add).then_inc(d_ready, 1)
                    elif part == 2:
                        then(nc.vector.tensor_scalar(C[:, side], av, col("k_a", c), ka1[:, bass.ds(c, 1)], ALU.mult, ALU.add))
                        settled()
                        then(nc.vector.tensor_tensor(C[:, side], C[:, side], twice(k), ALU.mult))
                    elif part == 3:
                        settled()
                        then(nc.vector.tensor_tensor(bonus[:, side], C[:, side, 0], C[:, side, 1], ALU.add))
                        settled()
                        nc.vector.scalar_tensor_tensor(out=bonus[:, side], in0=bonus[:, side], scalar=col("r_k", c), in1=r,
                                                       op0=ALU.mult, op1=ALU.mult).then_inc(bonus_ready, 1)
                    elif part == 4:
                        dve.wait_ge(kk_summed, c + 1)
                        nc.vector.tensor_scalar(norm[:, 0], K.ps[6][:, :], 1e-24, None, ALU.max).then_inc(ss_ready, 1)
                        dve.wait_ge(bonus_summed, c + 1)
                        dve.wait_ge(tail_loaded[side], 8 * c + (16 - 8 * side))
                        nc.vector.tensor_tensor(bonus[:, side], K.ps[7][:, :], v, ALU.mult).then_inc(bonus_out, 1)
                    elif part == 5:
                        dve.wait_ge(kn_ready, c + 1)
                        then(nc.vector.reciprocal(norm[:, 0], norm[:, 1]))
                        settled()
                        dve.wait_ge(kx_ready, c + 1)
                        then(nc.vector.tensor_tensor(kk[:, :], kk[:, :], norm[:, 0], ALU.mult))
                        settled()
                        then(nc.vector.scalar_tensor_tensor(out=B[:, side], in0=av, scalar=-1.0, in1=twice(kk[:, :]),
                                                            op0=ALU.mult, op1=ALU.mult))
                    elif part == 6:
                        dve.wait_ge(e_ready, 4 * c + 4)
                        settled()
                        nc.vector.tensor_tensor(B[:, side], B[:, side], cs[:, :, :], ALU.mult).then_inc(factors, 1)
                        nc.vector.tensor_tensor(C[:, side], C[:, side], cs[:, :, :], ALU.mult).then_inc(factors, 1)
                    else:
                        dve.wait_ge(setup, 3)
                        for dst, d, by in ((A, dA, kk[:, :]), (R, dR, r)):
                            for h in range(2):
                                rows = slice(h * HD, (h + 1) * HD)
                                nc.vector.tensor_tensor(
                                    dst[rows, side, :, :, h, :].rearrange("p z b t -> p (z b) t"),
                                    d[rows, :, :].rearrange("p z (b t) -> p (z b) t", b=TC),
                                    by[rows].rearrange("p (b t) -> p b t", b=TC).unsqueeze(1).to_broadcast([HD, 2, TC, P]),
                                    ALU.mult).then_inc(factors, 1)
                        then(nc.vector.tensor_tensor(fac[:, side], emid[:, :, 0:TC - 1], emid[:, :, 1:TC], ALU.mult))

                heads = [P, 2 * TC, HD]
                yv, ycv, ysv = (m[:, :, :].rearrange("p b (h v) -> p (b h) v", h=2) for m in (y, yc, ysq))

                def group_norm(c):
                    dve.wait_ge(y_out, 8 * c + 8)
                    then(nc.vector.tensor_reduce(stat[:, 0], yv, AX.X, ALU.add))
                    settled()
                    then(nc.vector.tensor_scalar(stat[:, 1], stat[:, 0], 1.0 / HD, None, ALU.mult))
                    settled()
                    then(nc.vector.tensor_tensor(ycv, yv, stat[:, 1].unsqueeze(2).to_broadcast(heads), ALU.subtract))
                    settled()
                    then(nc.vector.tensor_tensor(ysv, ycv, ycv, ALU.mult))
                    settled()
                    nc.vector.tensor_reduce(stat[:, 2], ysv, AX.X, ALU.add).then_inc(var_ready, 1)
                    dve.wait_ge(sd_ready, c + 1)
                    then(nc.vector.reciprocal(stat[:, 0], stat[:, 3]))
                    settled()
                    nc.vector.tensor_tensor(yv, ycv, stat[:, 0].unsqueeze(2).to_broadcast(heads),
                                            ALU.mult).then_inc(yn_ready, 1)

                def gated_sum(c, side):
                    dve.wait_ge(ln_ready, c + 1)
                    then(nc.vector.tensor_tensor(ln[:, :], ln[:, :], bonus[:, side], ALU.add))
                    settled()
                    nc.vector.tensor_tensor(K.h[:, bass.ds(c, 1), 1:T + 1], ln[:, :].unsqueeze(1),
                                            intail[:, side, 1].unsqueeze(1), ALU.mult).then_inc(done, 1)

                def body(c, side, first, last):
                    base[0], n[0] = NSTEP * c + 1 + NFRONT, 0
                    if not first:
                        group_norm(c - 1)
                    nc.vector.memset(S[:, 0], 0.0).then_inc(s_zero, 1)
                    for g4 in range(4):
                        z = g4 // 2
                        dve.wait_ge(ident_ready, 4 * c + g4 + 1)
                        dve.wait_ge(n_done, 4 * c + g4 + 1)
                        dve.sem_inc(waited, 1)
                        nc.vector.copy_predicated(Tm[:, g4], bc4(masks[:, z, 0, :]), bank4(g4 % 2)).then_inc(prod_out, 1)
                        for i in range(3):
                            dve.wait_ge(masked_done, 12 * c + 3 * g4 + i + 1)
                            dve.sem_inc(waited, 1)
                            nc.vector.copy_predicated(MT[:, i, g4], bc4(tri[:, 2 * z + (i > 0), :]),
                                                      bank4(5 + i)).then_inc(prod_out, 1)
                        if g4 == 1 and not first:
                            gated_sum(c - 1, 1 - side)
                    for lv in range(1, NLEV + 1):
                        for g4 in range(4):
                            z = g4 // 2
                            dve.wait_ge(q_done, 4 * NLEV * c + 4 * (lv - 1) + g4 + 1)
                            dve.sem_inc(waited, 1)
                            dst, which = (Tm, z) if lv < NLEV else (TT, 1 - z)
                            nc.vector.copy_predicated(dst[:, g4], bc4(masks[:, which, lv, :]),
                                                      bank4(2 + g4 % 2)).then_inc(inv_out, 1)
                            if not last and (lv, g4) in FRONT_AT:
                                front(FRONT_AT.index((lv, g4)), c + 1, 1 - side)
                    for b in range(TC):
                        for z in range(2):
                            if b == TC - 1:
                                break
                            j = b if z == 0 else TC - 2 - b
                            dve.wait_ge(s_done, 6 * c + 2 * b + z + 1)
                            if b:
                                dve.wait_ge(s_out, 6 * c + 2 * (b - 1) + z + 1)
                            then(nc.vector.tensor_tensor(Stmp[:, z], K.ps[6 + z][:, 0:P], S[:, b % 2, z], ALU.add))
                            settled()
                            nc.vector.scalar_tensor_tensor(out=S[:, 1 - b % 2, z], in0=Stmp[:, z],
                                                           scalar=fac[:, side, z, j:j + 1],
                                                           in1=K.const("blockdiag"), op0=ALU.mult,
                                                           op1=ALU.mult).then_inc(s_out, 1)
                        for z in range(2):
                            blk = b if z == 0 else TC - 1 - b
                            dve.wait_ge(y_done, 8 * c + 2 * b + z + 1)
                            if b < 2:
                                nc.vector.tensor_copy(y[:, blk, :], K.ps[4 + z][:, 0:P]).then_inc(y_out, 1)
                            else:
                                dve.wait_ge(y_out, 8 * c + 2 * b + z)
                                nc.vector.tensor_tensor(y[:, blk, :], K.ps[4 + z][:, 0:P], y[:, blk, :],
                                                        ALU.add).then_inc(y_out, 1)
                    round_up(NSTEP)

                for part in range(len(FRONT_AT)):
                    front(part, 0, 0)
                round_up(NFRONT)
                over_chunks(dve, body)
                base[0], n[0] = NSTEP * DC + 1 + NFRONT, 0
                group_norm(DC - 1)
                gated_sum(DC - 1, 1)

            @block.scalar
            def _(act):
                def front(part, c, side):
                    if part == 0:
                        act.wait_ge(kx_ready, c + 1)
                        nc.scalar.activation(sq[:, :], kk[:, :], ACT.Square).then_inc(kx_squared, 1)
                    elif part == 1:
                        act.wait_ge(d_ready, 2 * c + 2)
                        nc.scalar.activation(cs[:, :, :], dR[:, :, :], ACT.Exp, scale=DECAY).then_inc(e_ready, 1)
                        act.wait_ge(e_ready, 4 * c + 1)
                        nc.scalar.activation(dR[:, :, :], dR[:, :, :], ACT.Exp, scale=-DECAY).then_inc(e_ready, 1)
                    elif part == 2:
                        nc.scalar.activation(dA[:, :, :], dA[:, :, :], ACT.Exp, scale=-DECAY).then_inc(e_ready, 1)
                        nc.scalar.activation(emid[:, :, :], mid[:, :, :], ACT.Exp, scale=-DECAY).then_inc(e_ready, 1)
                    else:
                        act.wait_ge(ss_ready, c + 1)
                        nc.scalar.activation(norm[:, 1], norm[:, 0], ACT.Sqrt).then_inc(kn_ready, 1)

                def deviation(c):
                    act.wait_ge(var_ready, c + 1)
                    nc.scalar.activation(stat[:, 3], stat[:, 2], ACT.Sqrt, bias=K.eps[:, 1:2],
                                         scale=1.0 / HD).then_inc(sd_ready, 1)

                def affine(c):
                    act.wait_ge(yt_done, c + 1)
                    nc.scalar.activation(ln[:, :], K.ps[4][:, :], ACT.Identity,
                                         bias=K.cols[:, bass.ds(c + COLS["ln_b"][0], 1)],
                                         scale=K.cols[:, bass.ds(c + COLS["ln_g"][0], 1)]).then_inc(ln_ready, 1)

                def body(c, side, first, last):
                    for i, dst in enumerate((tokB[:, 0], tokB[:, 1], tokC[:, 0], tokC[:, 1], tokV[:, :, :])):
                        act.wait_ge(tok_done, 5 * c + i + 1)
                        nc.scalar.activation(dst, bank4((2, 3, 4, 5, 6)[i]), ACT.Copy).then_inc(tok_out, 1)
                    if not first:
                        deviation(c - 1)
                    for g4 in range(4):
                        act.wait_ge(nt_done, 4 * c + g4 + 1)
                        nc.scalar.activation(NT[:, g4], bank4(2 + g4 % 2), ACT.Copy).then_inc(nt_out, 1)
                        if g4 == 1 and not first:
                            affine(c - 1)
                    for lv in range(1, NLEV + 1):
                        for g4 in range(4):
                            act.wait_ge(p_done, 4 * NLEV * c + 4 * (lv - 1) + g4 + 1)
                            nc.scalar.activation(Pb[:, g4 % 2], bank4(g4 % 2), ACT.Copy).then_inc(p_out, 1)
                            act.wait_ge(tt_done, INV * c + group(lv, g4))
                            nc.scalar.activation(TT[:, g4], bank4(4 + g4 % 2), ACT.Copy).then_inc(tt_out, 1)
                            if not last and (lv, g4) in ACT_FRONT_AT:
                                front(ACT_FRONT_AT.index((lv, g4)), c + 1, 1 - side)
                    for b in range(TC):
                        for z in range(2):
                            act.wait_ge(rhs_done, 8 * c + 2 * b + z + 1)
                            nc.scalar.activation(rhs[:, z], K.ps[z][:, 0:P], ACT.Copy).then_inc(rhs_out, 1)
                        for z in range(2):
                            act.wait_ge(u_done, 8 * c + 2 * b + z + 1)
                            nc.scalar.activation(U[:, z], K.ps[2 + z][:, 0:P], ACT.Copy).then_inc(u_out, 1)

                for part in range(len(ACT_FRONT_AT)):
                    front(part, 0, 0)
                over_chunks(act, body)
                deviation(DC - 1)
                affine(DC - 1)

            @block.tensor
            def _(pe):
                def sum_kk(c):
                    pe.wait_ge(kx_squared, c + 1)
                    nc.tensor.matmul(K.ps[6][:, :], K.const("ones_sum"), sq[:, :], start=True, stop=True).then_inc(kk_summed, 1)

                def sum_bonus(c, side):
                    pe.wait_ge(bonus_ready, c + 1)
                    nc.tensor.matmul(K.ps[7][:, :], K.const("ones_sum"), bonus[:, side], start=True,
                                     stop=True).then_inc(bonus_summed, 1)

                def transpose_y(c):
                    pe.wait_ge(yn_ready, c + 1)
                    for b in range(TC):
                        last = nc.tensor.transpose(K.ps[4][:, b * P:(b + 1) * P], y[:, b, :], K.const("ident"))
                    last.then_inc(yt_done, 1)

                def four(bank, lhsT, rhs_, sem_):
                    for u in range(4):
                        last = nc.tensor.matmul(K.ps[bank][:, u * P:(u + 1) * P], lhsT(u), rhs_(u), start=True, stop=True)
                    last.then_inc(sem_, 1)

                def two(bank, left, right, side, g4, sem_):
                    z = g4 // 2
                    for e in range(2):
                        b = 2 * (g4 % 2) + e
                        last = nc.tensor.matmul(K.ps[bank][:, 2 * e * P:2 * (e + 1) * P], left[:, side, z, b * P:(b + 1) * P],
                                                right[:, side, z, b].rearrange("p h t -> p (h t)"), start=True, stop=True)
                    last.then_inc(sem_, 1)

                def body(c, side, first, last_chunk):
                    pe.wait_ge(factors, 6 * c + 6)
                    if not first:
                        pe.wait_ge(y_out, 8 * c)
                    pe.wait_ge(bonus_out, c + 1)
                    for i, src in enumerate((B[:, side, 0], B[:, side, 1], C[:, side, 0], C[:, side, 1], intail[:, side, 0])):
                        for b in range(TC):
                            last = nc.tensor.transpose(K.ps[2 + i][:, b * P:(b + 1) * P], src[:, b * P:(b + 1) * P],
                                                       K.const("ident"))
                        last.then_inc(tok_done, 1)
                    for g4 in range(4):
                        z = g4 // 2
                        if g4 >= 2:
                            pe.wait_ge(prod_out, 16 * c + 4 * (g4 - 2) + 1)

                        def unit(m, padded):
                            def at(u):
                                b = 2 * (g4 % 2) + u // 2
                                return m[:, side, z, b, u % 2, :] if padded else m[:, side, z, b * P:(b + 1) * P]
                            return at
                        four(g4 % 2, unit(A, True), unit(B, False), n_done)
                        pe.wait_ge(tok_out, 5 * c + 2)
                        if g4 >= 2:
                            pe.wait_ge(nt_out, 4 * c + g4 - 1)
                        two(2 + g4 % 2, B, A, side, g4, nt_done)
                        pe.wait_ge(tok_out, 5 * c + 5)
                        for i, (left, right) in enumerate(((C, A), (B, R), (C, R))):
                            if g4:
                                pe.wait_ge(prod_out, 16 * c + 4 * (g4 - 1) + 2 + i)
                            two(5 + i, left, right, side, g4, masked_done)
                        if g4 == 1 and not first:
                            transpose_y(c - 1)

                    pe.wait_ge(prod_out, 16 * c + 16)
                    pe.wait_ge(nt_out, 4 * c + 4)
                    if not first:
                        pe.wait_ge(ln_ready, c)

                    def double_p(lv, g4):
                        p = group(lv, g4)
                        if lv > 1:
                            pe.wait_ge(inv_out, INV * c + group(lv - 1, g4))
                        if p > 2:
                            pe.wait_ge(p_out, 4 * NLEV * c + p - 2)
                        four(g4 % 2, lambda u: NT[:, g4, u, :], lambda u: Tm[:, g4, u, :], p_done)
                        if p > 2:
                            pe.wait_ge(tt_out, INV * c + p - 2)
                        for u in range(4):
                            last = nc.tensor.transpose(K.ps[4 + g4 % 2][:, u * P:(u + 1) * P], Tm[:, g4, u, :],
                                                       K.const("ident"))
                        last.then_inc(tt_done, 1)

                    def double_q(lv, g4):
                        q = group(lv, g4)
                        pe.wait_ge(p_out, 4 * NLEV * c + q)
                        pe.wait_ge(tt_out, INV * c + q)
                        if q > 2:
                            pe.wait_ge(inv_out, INV * c + q - 2)
                        t_of = lambda u: TT[:, g4, u, :]
                        p_of = lambda u: Pb[:, g4 % 2, u, :]
                        left, right = (t_of, p_of) if lv < NLEV else (p_of, t_of)
                        four(2 + g4 % 2, left, right, q_done)

                    for lv in range(1, NLEV + 1):
                        double_p(lv, 0)
                        double_p(lv, 1)
                        double_q(lv, 0)
                        if not last_chunk and lv == 3:
                            sum_kk(c + 1)
                            sum_bonus(c + 1, 1 - side)
                        double_p(lv, 2)
                        double_q(lv, 1)
                        double_p(lv, 3)
                        double_q(lv, 2)
                        double_q(lv, 3)

                    pe.wait_ge(inv_out, INV * c + INV)
                    pe.wait_ge(s_zero, c + 1)
                    if not last_chunk:
                        pe.wait_ge(bonus_out, c + 2)
                    for b in range(TC):
                        blk = (b, TC - 1 - b)

                        def mt(i, z, h):
                            return MT[:, i, 2 * z + blk[z] // 2, 2 * (blk[z] % 2) + h, :]
                        def without_u(z):
                            if b < TC - 1:
                                nc.tensor.matmul(K.ps[6 + z][:, 0:P], tokC[:, z, blk[z], :], tokV[:, blk[z], :],
                                                 start=True, stop=False)
                            if b:
                                pe.wait_ge(y_out, 8 * c + 2 * (b - 1) + z + 1)
                            nc.tensor.matmul(K.ps[4 + z][:, 0:P], R[:, side, z, blk[z], 0, :], S[:, b % 2, z],
                                             start=True, stop=False)
                            for h in range(2):
                                nc.tensor.matmul(K.ps[4 + z][:, COLS_OF[h]], mt(2, z, h), tokV[:, blk[z], COLS_OF[h]],
                                                 start=False, stop=False)

                        for z in range(2):
                            if b:
                                pe.wait_ge(s_out, 6 * c + 2 * (b - 1) + z + 1)
                            nc.tensor.matmul(K.ps[z][:, 0:P], A[:, side, z, blk[z], 0, :], S[:, b % 2, z],
                                             start=True, stop=False)
                            for h in range(2):
                                nc.tensor.matmul(K.ps[z][:, COLS_OF[h]], mt(0, z, h), tokV[:, blk[z], COLS_OF[h]],
                                                 start=False, stop=False)
                            nc.tensor.matmul(K.ps[z][:, 0:P], A[:, side, z, blk[z], 1, :], S[:, b % 2, z],
                                             start=False, stop=True).then_inc(rhs_done, 1)
                        without_u(0)
                        for z in range(2):
                            pe.wait_ge(rhs_out, 8 * c + 2 * b + z + 1)
                            for h in range(2):
                                cols = COLS_OF[h]
                                last = nc.tensor.matmul(K.ps[2 + z][:, cols], TT[:, 2 * z + blk[z] // 2, 2 * (blk[z] % 2) + h, :],
                                                        rhs[:, z, cols], start=True, stop=True)
                            last.then_inc(u_done, 1)
                        without_u(1)
                        for z in range(2):
                            pe.wait_ge(u_out, 8 * c + 2 * b + z + 1)
                            if b < TC - 1:
                                nc.tensor.matmul(K.ps[6 + z][:, 0:P], tokB[:, z, blk[z], :], U[:, z], start=False,
                                                 stop=True).then_inc(s_done, 1)
                            for h in range(2):
                                nc.tensor.matmul(K.ps[4 + z][:, COLS_OF[h]], mt(1, z, h), U[:, z, COLS_OF[h]],
                                                 start=False, stop=False)
                            nc.tensor.matmul(K.ps[4 + z][:, 0:P], R[:, side, z, blk[z], 1, :], S[:, b % 2, z],
                                             start=False, stop=True).then_inc(y_done, 1)

                sum_kk(0)
                sum_bonus(0, 0)
                over_chunks(pe, body)
                transpose_y(DC - 1)



def build(nc, io, only=None):
    with ExitStack() as ctx:
        rel = nc.dram_tensor("rel_rows", (MAPS, REL_W), F32, kind="Internal").ap()
        io["rel_scratch"] = rel
        io["rel_toeplitz"] = bass.AP(tensor=rel.tensor, offset=rel.offset, ap=[[1, P], [REL_W, MAPS], [1, TOEP_W]])
        io["gates"] = nc.dram_tensor("gates", (NK, NK, T), F32, kind="Internal").ap()
        io["x_parked"] = nc.dram_tensor("x_parked", (P, DC, T), F32, kind="Internal").ap()
        io["rwkv"] = nc.dram_tensor("rwkv_proj", (8, DC, P, T), F32, kind="Internal").ap()
        K = Kernel(nc, io, ctx)
        stage_modulation(K)
        K.end_stage()
        stages = (("norm00", lambda: stage_norm(K, 0, 0)), ("attn", lambda: stage_attention(K)),
                  ("norm01", lambda: stage_norm(K, 0, 1)), ("peer0", lambda: stage_peer(K, 0)),
                  ("norm10", lambda: stage_norm(K, 1, 0)), ("rwkv", lambda: stage_rwkv(K)),
                  ("norm11", lambda: stage_norm(K, 1, 1)), ("peer1", lambda: stage_peer(K, 1)))
        for name, stage in stages:
            if only is None or name in only:
                stage()
                K.end_stage()
        stage_output(K)


def tiles_of(w):
    k, m = w.shape
    return w.reshape(k // P, P, m // P, P).transpose(2, 1, 0, 3)


def columns(v):
    return np.asarray(v).reshape(-1, P).T


def layout(inputs):
    i = {k: np.asarray(v) for k, v in inputs.items()}
    a = {}
    a["xT"] = i["x"][0].T.reshape(DC, P, T).transpose(1, 0, 2)
    a["ada_w"] = i["ada_w"]
    qk = i["attn_qk_g"][0]
    gcol = np.stack([np.concatenate([qk[n], qk[n]]) for n in [0] * 4 + [1] * 4 + [2] * 4 + [3]], 1)
    cols = np.zeros((P, NCOLS), np.float32)
    for name, v in (("c", columns(i["c"])), ("ada_b", columns(i["ada_b"])), ("norm_g", columns(i["norm_g"])),
                    ("qk_g", gcol), ("subln_g", columns(i["diff_subln_g"])), ("mix", columns(i["rwkv_mix"])),
                    ("w0", columns(i["rwkv_w0"])), ("a0", columns(i["rwkv_a0"])), ("k_k", columns(i["rwkv_k_k"])),
                    ("k_a", columns(i["rwkv_k_a"])), ("r_k", columns(i["rwkv_r_k"])),
                    ("ln_g", columns(i["rwkv_ln_g"])), ("ln_b", columns(i["rwkv_ln_b"]))):
        cols[:, COLS[name][0]:COLS[name][1]] = v
    a["cols"] = cols
    a["consts"] = host_constants()
    w = i["attn_w_in"][0]
    qb = w[:, 1536:2048].reshape(D, 2, 4, HD).transpose(0, 2, 1, 3).reshape(D, 512)
    a["w_in"] = tiles_of(np.concatenate([w[:, 0:1024], qb, w[:, 2048:2176], w[:, 1024:1536], w[:, 2176:2304]], 1))
    wo = i["attn_w_out"][0]
    a["w_out"] = tiles_of(np.concatenate([wo[:512], wo[512:].reshape(2, 4, HD, D).transpose(1, 0, 2, 3).reshape(512, D)]))
    a["lam"] = i["diff_lambda"][0].reshape(1, 4 * HD)
    a["rel_bias"] = i["rel_bias"]
    a["bucket"] = host_bucket_onehot()
    a["w_rkv"] = np.concatenate([tiles_of(i["rwkv_w_rkv"][0, n]) for n in range(3)])
    a["w_o"] = tiles_of(i["rwkv_w_o"][0])
    a["lora1"] = np.concatenate([tiles_of(np.concatenate([i["rwkv_w1"][0, 0], i["rwkv_w1"][0, 1]], 1)),
                                 tiles_of(np.concatenate([i["rwkv_a1"][0, 0], i["rwkv_a1"][0, 1]], 1)),
                                 tiles_of(i["rwkv_g1"][0])])
    a["lora2"] = np.stack([i["rwkv_w2"][0].reshape(P, D), i["rwkv_a2"][0].reshape(P, D), i["rwkv_g2"][0]])
    n = np.arange(P)
    up, up_incl = n[:, None] < n[None], n[:, None] <= n[None]
    a["tri"] = np.stack([up, up_incl, up.T, up_incl.T], 1).astype(np.uint32)
    a["scanmask"] = np.tile((np.arange(T) % P != 0).astype(np.float32), (P, 1))
    a["masks"] = host_level_masks()
    a["w_q"] = np.stack([tiles_of(i["peer_w_q"][l]) for l in range(DEPTH)])
    a["subkeys"] = i["peer_subkeys"].transpose(0, 4, 1, 2, 3).reshape(DEPTH, P, HP * NK)
    a["u"] = i["peer_u"].reshape(DEPTH, NK, NK, DC, P).transpose(0, 1, 4, 3, 2)
    a["v"] = i["peer_v"].reshape(DEPTH, NK, NK, D)
    return {k: np.ascontiguousarray(v) for k, v in a.items()}


def kernel(**inputs):
    import concourse.bacc as bacc
    from concourse.bass_utils import run_bass_kernel_spmd

    arrays = layout(inputs)
    nc = bacc.Bacc("TRN2", target_bir_lowering=False, num_devices=1)
    io = {k: nc.dram_tensor("in_" + k, v.shape, mybir.dt.from_np(v.dtype), kind="ExternalInput").ap()
          for k, v in arrays.items()}
    io["outT"] = nc.dram_tensor("out_T", (P, DC, T), F32, kind="ExternalOutput").ap()
    build(nc, io)
    r = run_bass_kernel_spmd(nc, [{"in_" + k: v for k, v in arrays.items()}], core_ids=[0])
    out = r.results[0]["out_T"]
    return np.ascontiguousarray(out.transpose(1, 0, 2).reshape(D, T).T)[None]
```
